# Optimizing a Trainium2 kernel written in Bass

```python
import math
import jax, jax.numpy as jnp
from jax import lax
import numpy as np

D_MODEL = 1024
BATCH = 1
SEQ = 256
DEPTH = 2

SSM_GROUPS = 32
SSM_GROUP_CH = 16
SSM_WIDTH = SSM_GROUPS * SSM_GROUP_CH
SSM_STATE = 64
DT_MIN = 0.001
DT_MAX = 0.1
N_HEADS = 8
HEAD_DIM = 64
ATTN_WIDTH = N_HEADS * HEAD_DIM
MOBA_BLOCK = 256
MOBA_TOPK = 3
Q_BLOCK = 128
ROPE_THETA = 10000.0
D_IN = SSM_WIDTH + 3 * ATTN_WIDTH + 2 * D_MODEL
N_GROUPS = 4
EXPERTS_PER_GROUP = 8
N_EXPERTS = N_GROUPS * EXPERTS_PER_GROUP
EXPERT_TOPK = 2
D_EXPERT = 512
EXPERT_ROWS = 256
NORM_EPS = 1e-6

kernel_name = "hybrid_s5_moba_hmoe_trunk"

def rms_norm(x, gain):
    xf = x.astype(jnp.float32)
    y = xf * lax.rsqrt(jnp.mean(xf * xf, axis=-1, keepdims=True) + NORM_EPS)
    return (y * gain.astype(jnp.float32)).astype(x.dtype)

def rope_tables(seq, dh):
    inv = ROPE_THETA ** (-jnp.arange(0, dh, 2, dtype=jnp.float32) / dh)
    ang = jnp.arange(seq, dtype=jnp.float32)[:, None] * inv[None, :]
    return jnp.cos(ang), jnp.sin(ang)

def apply_rope(x, cos, sin):
    half = x.shape[-1] // 2
    xf = x.astype(jnp.float32)
    x1, x2 = xf[..., :half], xf[..., half:]
    return jnp.concatenate([x1 * cos - x2 * sin, x2 * cos + x1 * sin], axis=-1).astype(x.dtype)

def _complex_linear_combine(left, right):
    ar1, ai1, br1, bi1 = left
    ar2, ai2, br2, bi2 = right
    ar = ar2 * ar1 - ai2 * ai1
    ai = ar2 * ai1 + ai2 * ar1
    br = ar2 * br1 - ai2 * bi1 + br2
    bi = ar2 * bi1 + ai2 * br1 + bi2
    return ar, ai, br, bi

def s5_branch(u, a_re, a_im, log_dt, b_re, b_im, c_re, c_im, d_skip, w_glu):
    bsz, seq, _ = u.shape
    ug = u.astype(jnp.float32).reshape(bsz, seq, SSM_GROUPS, SSM_GROUP_CH)
    dt = jnp.exp(log_dt.astype(jnp.float32))[:, None]
    lam_re = a_re.astype(jnp.float32)
    lam_im = a_im.astype(jnp.float32)
    decay = jnp.exp(lam_re * dt)
    abar_re = decay * jnp.cos(lam_im * dt)
    abar_im = decay * jnp.sin(lam_im * dt)
    den = lam_re * lam_re + lam_im * lam_im
    num_re = abar_re - 1.0
    f_re = (num_re * lam_re + abar_im * lam_im) / den
    f_im = (abar_im * lam_re - num_re * lam_im) / den
    bf_re = b_re.astype(jnp.float32)
    bf_im = b_im.astype(jnp.float32)
    bbar_re = f_re[..., None] * bf_re - f_im[..., None] * bf_im
    bbar_im = f_re[..., None] * bf_im + f_im[..., None] * bf_re
    bu_re = jnp.einsum('bsgh,gph->bsgp', ug, bbar_re)
    bu_im = jnp.einsum('bsgh,gph->bsgp', ug, bbar_im)
    a_r = jnp.broadcast_to(abar_re, bu_re.shape)
    a_i = jnp.broadcast_to(abar_im, bu_re.shape)
    _, _, s_re, s_im = lax.associative_scan(_complex_linear_combine, (a_r, a_i, bu_re, bu_im), axis=1)
    y = (jnp.einsum('bsgp,ghp->bsgh', s_re, c_re.astype(jnp.float32))
         - jnp.einsum('bsgp,ghp->bsgh', s_im, c_im.astype(jnp.float32))
         + d_skip.astype(jnp.float32).reshape(SSM_GROUPS, SSM_GROUP_CH) * ug)
    z = jax.nn.gelu(y.reshape(bsz, seq, SSM_WIDTH)).astype(u.dtype)
    val, gate = jnp.split(z @ w_glu, 2, axis=-1)
    return val * jax.nn.sigmoid(gate)

def moba_attention(q, k, v):
    bsz, nh, seq, dh = q.shape
    nb = -(-seq // MOBA_BLOCK)
    pad = nb * MOBA_BLOCK - seq
    nqb = seq // Q_BLOCK
    n_sel = min(MOBA_TOPK, nb - 1)
    scale = dh ** -0.5
    neg = jnp.finfo(jnp.float32).min
    kp = jnp.pad(k, ((0, 0), (0, 0), (0, pad), (0, 0)))
    vp = jnp.pad(v, ((0, 0), (0, 0), (0, pad), (0, 0)))
    kblk = kp.reshape(bsz, nh, nb, MOBA_BLOCK, dh)
    vblk = vp.reshape(bsz, nh, nb, MOBA_BLOCK, dh)

    def to_qblocks(t):
        return t.reshape(bsz, nh, nqb, Q_BLOCK, t.shape[-1]).transpose(0, 2, 1, 3, 4).reshape(
            bsz * nqb, nh, Q_BLOCK, t.shape[-1])

    qr = to_qblocks(q)
    q_blk = jnp.arange(seq) // MOBA_BLOCK
    if n_sel > 0:
        kmean = jnp.mean(kblk.astype(jnp.float32), axis=3)
        gate = jnp.einsum('bhsd,bhnd->bhsn', q.astype(jnp.float32), kmean)
        fully_past = jnp.arange(nb)[None, :] < q_blk[:, None]
        gate = jnp.where(fully_past, gate, neg)
        _, sel = lax.top_k(gate, n_sel)
        valid = sel < q_blk[:, None]
        sel_r = to_qblocks(sel)
        valid_r = to_qblocks(valid)
    else:
        sel_r = jnp.zeros((bsz * nqb, nh, Q_BLOCK, 0), jnp.int32)
        valid_r = jnp.zeros((bsz * nqb, nh, Q_BLOCK, 0), jnp.bool_)
    b_idx = jnp.repeat(jnp.arange(bsz), nqb)
    j_idx = jnp.tile(jnp.arange(nqb), bsz)
    hidx = jnp.arange(nh)[:, None, None]

    def step(args):
        qb, sel_b, valid_b, b, j = args
        q_start = j * Q_BLOCK
        cur = q_start // MOBA_BLOCK
        kb = kblk[b]
        vb = vblk[b]
        k_cur = kb[:, cur]
        v_cur = vb[:, cur]
        qpos = q_start + jnp.arange(Q_BLOCK)
        kpos = cur * MOBA_BLOCK + jnp.arange(MOBA_BLOCK)
        s_cur = jnp.einsum('hqd,hkd->hqk', qb, k_cur, preferred_element_type=jnp.float32) * scale
        s_cur = jnp.where(kpos[None, None, :] <= qpos[None, :, None], s_cur, neg)
        if n_sel == 0:
            p = jax.nn.softmax(s_cur, axis=-1).astype(vb.dtype)
            out = jnp.einsum('hqk,hkd->hqd', p, v_cur)
        else:
            k_sel = kb[hidx, sel_b]
            v_sel = vb[hidx, sel_b]
            s_past = jnp.einsum('hqd,hqnkd->hqnk', qb, k_sel, preferred_element_type=jnp.float32) * scale
            s_past = jnp.where(valid_b[..., None], s_past, neg)
            s = jnp.concatenate([s_past.reshape(nh, Q_BLOCK, n_sel * MOBA_BLOCK), s_cur], axis=-1)
            p = jax.nn.softmax(s, axis=-1).astype(vb.dtype)
            p_past = p[..., :n_sel * MOBA_BLOCK].reshape(nh, Q_BLOCK, n_sel, MOBA_BLOCK)
            p_cur = p[..., n_sel * MOBA_BLOCK:]
            out = (jnp.einsum('hqnk,hqnkd->hqd', p_past, v_sel)
                   + jnp.einsum('hqk,hkd->hqd', p_cur, v_cur))
        return out.astype(q.dtype)

    outs = lax.map(step, (qr, sel_r, valid_r, b_idx, j_idx))
    outs = outs.reshape(bsz, nqb, nh, Q_BLOCK, dh).transpose(0, 1, 3, 2, 4)
    return outs.reshape(bsz, seq, nh * dh)

def hier_moe(h, w_group, b_group, w_expert, b_expert, w_gate_up, w_down):
    bsz, seq, d = h.shape
    n = bsz * seq
    xt = h.reshape(n, d)
    glog = (xt @ w_group).astype(jnp.float32) + b_group.astype(jnp.float32)
    gprob = jax.nn.softmax(glog, axis=-1)
    g_top = jnp.argmax(glog, axis=-1)
    p_g = jnp.take_along_axis(gprob, g_top[:, None], axis=-1)[:, 0]
    elog = ((xt @ w_expert).astype(jnp.float32) + b_expert.astype(jnp.float32)).reshape(
        n, N_GROUPS, EXPERTS_PER_GROUP)
    elog = jnp.take_along_axis(elog, g_top[:, None, None], axis=1)[:, 0]
    eprob = jax.nn.softmax(elog, axis=-1)
    top_p, top_e = lax.top_k(eprob, EXPERT_TOPK)
    top_p = top_p / jnp.sum(top_p, axis=-1, keepdims=True)
    weights = p_g[:, None] * top_p
    expert_id = g_top[:, None] * EXPERTS_PER_GROUP + top_e
    n_assign = n * EXPERT_TOPK
    flat_e = expert_id.reshape(-1).astype(jnp.int32)
    flat_tok = jnp.repeat(jnp.arange(n, dtype=jnp.int32), EXPERT_TOPK)
    flat_w = weights.reshape(-1)
    order = jnp.argsort(flat_e)
    se, stok, sw = flat_e[order], flat_tok[order], flat_w[order]
    counts = jnp.bincount(flat_e, length=N_EXPERTS)
    padded = (counts + EXPERT_ROWS - 1) // EXPERT_ROWS * EXPERT_ROWS
    start = jnp.cumsum(counts) - counts
    pend = jnp.cumsum(padded)
    pstart = pend - padded
    dest = pstart[se] + (jnp.arange(n_assign) - start[se])
    cap = n_assign + N_EXPERTS * EXPERT_ROWS
    nblk = cap // EXPERT_ROWS
    slot_tok = jnp.zeros((cap,), jnp.int32).at[dest].set(stok)
    slot_w = jnp.zeros((cap,), jnp.float32).at[dest].set(sw)
    blk_e = jnp.minimum(jnp.searchsorted(pend, jnp.arange(nblk) * EXPERT_ROWS, side='right'),
                        N_EXPERTS - 1)

    def expert_block(args):
        tok, e = args
        xb = xt[tok]
        gt, up = jnp.split(xb @ w_gate_up[e], 2, axis=-1)
        return (jax.nn.silu(gt) * up) @ w_down[e]

    yb = lax.map(expert_block, (slot_tok.reshape(nblk, EXPERT_ROWS), blk_e))
    y = yb.reshape(cap, d) * slot_w[:, None].astype(h.dtype)
    out = jax.ops.segment_sum(y, slot_tok, num_segments=n)
    return out.reshape(bsz, seq, d)

def setup_inputs(seed: int = 0) -> dict:
    key = jax.random.key(seed)
    ks = jax.random.split(key, 24)
    L = DEPTH
    f32 = jnp.float32

    def nrm(k, shape, scale):
        return jax.random.normal(k, shape, f32) * scale

    x = jax.random.normal(ks[0], (BATCH, SEQ, D_MODEL), f32)
    norm1_g = 1.0 + nrm(ks[1], (L, D_MODEL), 0.01)
    w_in = nrm(ks[2], (L, D_MODEL, D_IN), D_MODEL ** -0.5)
    ssm_a_re = -0.5 + nrm(ks[3], (L, SSM_GROUPS, SSM_STATE), 0.01)
    ssm_a_im = math.pi * jnp.arange(SSM_STATE, dtype=f32)[None, None, :] + nrm(
        ks[4], (L, SSM_GROUPS, SSM_STATE), 0.01)
    ssm_log_dt = jax.random.uniform(ks[5], (L, SSM_GROUPS), f32, math.log(DT_MIN), math.log(DT_MAX))
    ssm_b_re = nrm(ks[6], (L, SSM_GROUPS, SSM_STATE, SSM_GROUP_CH), (2 * SSM_GROUP_CH) ** -0.5)
    ssm_b_im = nrm(ks[7], (L, SSM_GROUPS, SSM_STATE, SSM_GROUP_CH), (2 * SSM_GROUP_CH) ** -0.5)
    ssm_c_re = nrm(ks[8], (L, SSM_GROUPS, SSM_GROUP_CH, SSM_STATE), (2 * SSM_STATE) ** -0.5)
    ssm_c_im = nrm(ks[9], (L, SSM_GROUPS, SSM_GROUP_CH, SSM_STATE), (2 * SSM_STATE) ** -0.5)
    ssm_d = nrm(ks[10], (L, SSM_WIDTH), 1.0)
    w_glu = nrm(ks[11], (L, SSM_WIDTH, 2 * D_MODEL), SSM_WIDTH ** -0.5)
    q_norm_g = 1.0 + nrm(ks[12], (L, HEAD_DIM), 0.01)
    k_norm_g = 1.0 + nrm(ks[13], (L, HEAD_DIM), 0.01)
    w_attn = nrm(ks[14], (L, ATTN_WIDTH, D_MODEL), ATTN_WIDTH ** -0.5)
    w_out = nrm(ks[15], (L, D_MODEL, D_MODEL), D_MODEL ** -0.5)
    norm2_g = 1.0 + nrm(ks[16], (L, D_MODEL), 0.01)
    router_w_group = nrm(ks[17], (L, D_MODEL, N_GROUPS), D_MODEL ** -0.5)
    router_b_group = nrm(ks[18], (L, N_GROUPS), 0.01)
    router_w_expert = nrm(ks[19], (L, D_MODEL, N_EXPERTS), D_MODEL ** -0.5)
    router_b_expert = nrm(ks[20], (L, N_EXPERTS), 0.01)
    w_gate_up = nrm(ks[21], (L, N_EXPERTS, D_MODEL, 2 * D_EXPERT), D_MODEL ** -0.5)
    w_down = nrm(ks[22], (L, N_EXPERTS, D_EXPERT, D_MODEL), D_EXPERT ** -0.5)
    return {"x": x, "norm1_g": norm1_g, "w_in": w_in, "ssm_a_re": ssm_a_re, "ssm_a_im": ssm_a_im,
            "ssm_log_dt": ssm_log_dt, "ssm_b_re": ssm_b_re, "ssm_b_im": ssm_b_im, "ssm_c_re": ssm_c_re,
            "ssm_c_im": ssm_c_im, "ssm_d": ssm_d, "w_glu": w_glu, "q_norm_g": q_norm_g,
            "k_norm_g": k_norm_g, "w_attn": w_attn, "w_out": w_out, "norm2_g": norm2_g,
            "router_w_group": router_w_group, "router_b_group": router_b_group,
            "router_w_expert": router_w_expert, "router_b_expert": router_b_expert,
            "w_gate_up": w_gate_up, "w_down": w_down}

def reference(x, norm1_g, w_in, ssm_a_re, ssm_a_im, ssm_log_dt, ssm_b_re, ssm_b_im, ssm_c_re, ssm_c_im,
              ssm_d, w_glu, q_norm_g, k_norm_g, w_attn, w_out, norm2_g, router_w_group, router_b_group,
              router_w_expert, router_b_expert, w_gate_up, w_down):
    bsz, seq, _ = x.shape
    cos, sin = rope_tables(seq, HEAD_DIM)
    splits = [SSM_WIDTH, SSM_WIDTH + ATTN_WIDTH, SSM_WIDTH + 2 * ATTN_WIDTH,
              SSM_WIDTH + 3 * ATTN_WIDTH, SSM_WIDTH + 3 * ATTN_WIDTH + D_MODEL]
    for l in range(DEPTH):
        h = rms_norm(x, norm1_g[l])
        proj = h @ w_in[l]
        u, q, k, v, g_ssm, g_attn = jnp.split(proj, splits, axis=-1)
        y_ssm = s5_branch(u, ssm_a_re[l], ssm_a_im[l], ssm_log_dt[l], ssm_b_re[l], ssm_b_im[l],
                          ssm_c_re[l], ssm_c_im[l], ssm_d[l], w_glu[l])
        q = q.reshape(bsz, seq, N_HEADS, HEAD_DIM).transpose(0, 2, 1, 3)
        k = k.reshape(bsz, seq, N_HEADS, HEAD_DIM).transpose(0, 2, 1, 3)
        v = v.reshape(bsz, seq, N_HEADS, HEAD_DIM).transpose(0, 2, 1, 3)
        q = apply_rope(rms_norm(q, q_norm_g[l]), cos, sin)
        k = apply_rope(rms_norm(k, k_norm_g[l]), cos, sin)
        y_attn = moba_attention(q, k, v) @ w_attn[l]
        mixed = jax.nn.sigmoid(g_ssm) * y_ssm + jax.nn.sigmoid(g_attn) * y_attn
        x = x + mixed @ w_out[l]
        h2 = rms_norm(x, norm2_g[l])
        x = x + hier_moe(h2, router_w_group[l], router_b_group[l], router_w_expert[l],
                         router_b_expert[l], w_gate_up[l], w_down[l])
    return x


_drawn_inputs = setup_inputs


def setup_inputs(seed=0):
    import zlib

    import numpy as np

    out = dict(_drawn_inputs(seed))
    spreads = {}
    factors = {'norm1_g': 3.26,
     'ssm_a_re': 58.272,
     'q_norm_g': 4.991,
     'k_norm_g': 3.555,
     'norm2_g': 2.671,
     'router_b_group': 8.0,
     'router_b_expert': 3.478}
    for name, (base, spread) in spreads.items():
        noise = np.random.default_rng([zlib.crc32(name.encode()), seed]).standard_normal(out[name].shape)
        drawn = base * np.exp(spread * noise) if base else spread * noise
        out[name] = __import__('jax').numpy.asarray(drawn.astype(out[name].dtype))
    for name, factor in factors.items():
        out[name] = (out[name] * factor).astype(out[name].dtype)
    return out
```

```python
from contextlib import ExitStack

import numpy as np

import concourse.bass as bass
from concourse import mybir

F32 = mybir.dt.float32
I32 = mybir.dt.int32
U32 = mybir.dt.uint32
ALU = mybir.AluOpType
ACT = mybir.ActivationFunctionType
AX = mybir.AxisListType

P = 128
DEPTH = 2
D = 1024
SEQ = 256
NT = SEQ // P
KC = D // P
HEADS, HD = 8, 64
GROUPS, GCH, NSTATE = 32, 16, 64
TILES = GROUPS * NSTATE // P
QUADS = TILES // 4
HALF = SEQ // 2
TW = HALF + 1
EXPERTS, EGROUPS, EPG = 32, 4, 8
FF = 512
SLOTS = 64
PAIRS = EXPERTS // 2
OV_BLOCKS = 8
OV_PAIRS = OV_BLOCKS // 2
BLOCKS = EXPERTS + OV_BLOCKS + 2
EXTRA = SEQ // SLOTS - 1
RING = 12
FRONT_GROUPS = 26
LAYER_GROUPS = FRONT_GROUPS + RING * PAIRS
EPS = 1e-6
BIG = 3.0e38
ROUND = 1.5 * 2.0 ** 23
ROUND15 = 1.5 * 2.0 ** 8
TWO_PI = 6.2831850
GELU_C = 0.7978845608028654
ATT_SCALE = HD ** -0.5

CONST = {}
_at = 0
for _name, _n in (("ident", P), ("before", P), ("ones", P), ("causal", P), ("zero", P), ("rope_a", NT * HD),
                  ("rope_b", NT * HD), ("slot", SLOTS), ("expert", EXPERTS), ("egroup", EXPERTS),
                  ("step", TW), ("ov_expert", EXTRA * EXPERTS), ("ov_shift", EXTRA * EXPERTS),
                  ("ov_limit", EXTRA * EXPERTS), ("ov_block", OV_BLOCKS), ("side", 2), ("gside", 2),
                  ("odd_tile", 2), ("eps", 1)):
    CONST[_name] = (_at, _at + _n)
    _at += _n
N_CONST = _at

VEC = {"norm1": (0, 8), "norm2": (8, 16), "skip": (16, 20), "a_re": (20, 36), "a_im": (36, 52)}
N_VEC = 52


def constants():
    c = np.zeros((P, N_CONST), np.float32)

    def put(name, value):
        a, b = CONST[name]
        c[:, a:b] = value

    row = np.arange(P)[:, None]
    col = np.arange(P)[None, :]
    put("ident", row == col)
    put("before", row < col)
    put("ones", 1.0)
    put("causal", np.where(col <= row, 0.0, -1e30))
    inv = (np.float32(10000.0) ** (-np.arange(0, HD, 2, dtype=np.float32) / np.float32(HD))).astype(np.float32)
    ang = np.arange(SEQ, dtype=np.float32)[:, None] * inv[None, :]
    cos, sin = np.cos(ang).astype(np.float32), np.sin(ang).astype(np.float32)
    a = np.concatenate([cos, cos], 1).reshape(NT, P, HD).transpose(1, 0, 2).reshape(P, -1)
    b = np.concatenate([-sin, sin], 1).reshape(NT, P, HD).transpose(1, 0, 2).reshape(P, -1)
    put("rope_a", a)
    put("rope_b", b)
    put("slot", np.arange(SLOTS))
    put("expert", np.arange(EXPERTS))
    put("egroup", np.arange(EXPERTS) // EPG)
    put("step", np.arange(TW))
    r = np.arange(EXTRA * EXPERTS) // EXPERTS
    put("ov_expert", np.arange(EXTRA * EXPERTS) % EXPERTS)
    put("ov_shift", 1.0 - SLOTS * (r + 1))
    put("ov_limit", SLOTS * (r + 1))
    put("ov_block", np.arange(OV_BLOCKS) + 1)
    put("side", (row // NSTATE) == np.arange(2)[None, :])
    put("gside", (row // GCH) % 2 == np.arange(2)[None, :])
    put("odd_tile", (row // (2 * GCH)) % 2 == np.arange(2)[None, :])
    put("eps", EPS)
    return c


class Counted:

    def __init__(self, start, per):
        self.start, self.per, self.n = start, per, 0

    def add(self):
        self.n += 1

    def value(self):
        return self.start + self.n

    def next(self):
        self.add()
        return self.value()

    def close(self):
        assert self.n == self.per, (self.n, self.per)


def trunk(nc, x, norm1_g, w_in, ssm_a_re, ssm_a_im, ssm_log_dt, ssm_b_re, ssm_b_im, ssm_c_re, ssm_c_im,
          ssm_d, w_glu, q_norm_g, k_norm_g, w_attn, w_out, norm2_g, router_w_group, router_b_group,
          router_w_expert, router_b_expert, w_gate_up, w_down, consts, out):
    ctx = ExitStack()

    def sb(name, cols, dt=F32):
        return ctx.enter_context(nc.sbuf_tensor(name, [P, cols], dt))[:]

    per, ahead = {}, {}

    def signal(name, times=1, start=0):
        sem = ctx.enter_context(nc.semaphore(name))
        per[sem.name], ahead[sem.name] = times, start
        return sem

    def at(sem, rnd, k):
        return rnd * per[sem.name] + k + ahead[sem.name]

    def counted(sem, rnd):
        return Counted(at(sem, rnd, 0), per[sem.name])

    ps = ctx.enter_context(nc.psum_tensor("ps", [P, 8, 512], F32))[:]

    ring = sb("ring", RING * 2 * D).rearrange("p (g c n) -> p g c n", g=RING, c=2)
    xs = sb("xs", NT * D).rearrange("p (t d) -> p t d", t=NT)
    hT = sb("hT", KC * SEQ).rearrange("p (k s) -> p k s", k=KC)
    cosT = sb("cosT", TILES * TW).rearrange("p (i t) -> p i t", i=TILES)
    sinT = sb("sinT", TILES * TW).rearrange("p (i t) -> p i t", i=TILES)
    b_lhs = sb("b_lhs", 2 * 2 * QUADS * P).rearrange("p (r o q s) -> p r o q s", r=2, o=2, q=QUADS)
    c_lhs = sb("c_lhs", 3 * QUADS * P).rearrange("p (v q s) -> p v q s", v=3, q=QUADS)
    cst = sb("cst", N_CONST)
    vec = sb("vec", N_VEC)
    rows = sb("rows", P)
    log_dt = sb("log_dt", GROUPS)
    diag = sb("diag", NT * P).rearrange("p (t s) -> p t s", t=NT)
    rope = sb("rope", 2 * 2 * NT * HD).rearrange("p (w f t d) -> p w f t d", w=2, f=2, t=NT)
    router_w = sb("router_w", KC * 36).rearrange("p (k n) -> p k n", k=KC)
    router_b = sb("router_b", 36)
    qk_gain = sb("qk_gain", 2 * HD).rearrange("p (w d) -> p w d", w=2)
    ov_flag = sb("ov_flag", 1, I32)
    ov_ids = sb("ov_ids", OV_BLOCKS, I32)
    tops = sb("tops", 4 * 8).rearrange("p (a t n) -> p a t n", a=2, t=NT)
    tops_at = sb("tops_at", 4 * 8, U32).rearrange("p (a t n) -> p a t n", a=2, t=NT)

    (decay, dt_, theta, turns_hi, turns_lo, den, f_re, f_im, a_bar_re, a_bar_im, sc0, sc1) = (
        sb(n, TILES) for n in ("decay", "dt", "theta", "turns_hi", "turns_lo", "den", "f_re", "f_im",
                               "a_bar_re", "a_bar_im", "sc0", "sc1"))
    carry = sb("carry", 4 * TILES).rearrange("p (r i) -> p r i", r=4)
    gain2 = sb("gain2", KC)
    ssq, std, rstd = (sb(n, NT) for n in ("ssq", "std", "rstd"))
    head_ss = sb("head_ss", 4 * HEADS).rearrange("p (n h) -> p n h", n=4)
    head_rs = sb("head_rs", 4 * HEADS).rearrange("p (n h) -> p n h", n=4)
    row_max, row_sum, row_inv = (sb(n, HEADS) for n in ("row_max", "row_sum", "row_inv"))
    glog = sb("glog", NT * 8).rearrange("p (t n) -> p t n", t=NT)
    elog = sb("elog", NT * EXPERTS).rearrange("p (t n) -> p t n", t=NT)
    emask = sb("emask", NT * EXPERTS).rearrange("p (t n) -> p t n", t=NT)
    assign = sb("assign", NT * EXPERTS).rearrange("p (t n) -> p t n", t=NT)
    onehot = sb("onehot", 2 * NT * EXPERTS).rearrange("p (a t n) -> p a t n", a=2, t=NT)
    ids = sb("ids", 3 * NT).rearrange("p (a t) -> p a t", a=3)
    rt = sb("rt", 8 * NT).rearrange("p (a t) -> p a t", a=8)
    count = sb("count", EXPERTS)
    slot_of = sb("slot_of", NT * BLOCKS).rearrange("p (t b) -> p t b", t=NT)
    weight_of = sb("weight_of", NT * BLOCKS).rearrange("p (t b) -> p t b", t=NT)

    def const(name):
        a, b = CONST[name]
        return cst[:, a:b]

    def turned(name):
        a, b = VEC[name]
        return vec[:, a:b]

    PHASE = 12672
    phase = sb("phase", PHASE)
    uT = phase[:, 0:1024].rearrange("p (q s) -> p q s", q=QUADS)
    raw = phase[:, 1024:3072].rearrange("p (n c) -> p n c", n=4)
    mix = phase[:, 1024:3072].rearrange("p (t d) -> p t d", t=NT)
    rope_tmp = phase[:, 3072:4096].rearrange("p (w n) -> p w n", w=2)
    rope_tmp_k = phase[:, 6144:7168].rearrange("p (w n) -> p w n", w=2)
    attn = rope_tmp
    squares = phase[:, 4096:5120].rearrange("p (t n) -> p t n", t=NT)
    vtok = phase[:, 4096:5120].rearrange("p (t n) -> p t n", t=NT)
    qT = phase[:, 5120:6144].rearrange("p (c s) -> p c s", c=4)
    oT = qT
    kT = phase[:, 6144:7168].rearrange("p (c s) -> p c s", c=4)
    probs = phase[:, 1024:2048]
    pre = phase[:, 7168:9216].rearrange("p (v i t) -> p v i t", v=4, i=4)
    wst = phase[:, 9216:10240].rearrange("p (v i t) -> p v i t", v=2, i=4)
    post = phase[:, 10240:12288].rearrange("p (v i t) -> p v i t", v=4, i=4)
    y1, y2, y3 = (phase[:, 12288 + 128 * n:12416 + 128 * n] for n in range(3))
    att_gate = phase[:, 7168:9216].rearrange("p (u n) -> p u n", u=4)
    gates = phase[:, 9216:11264].rearrange("p (w u n) -> p w u n", w=2, u=2)
    junk = phase[:, 0:2048].rearrange("p (t d) -> p t d", t=NT)
    turn_a = phase[:, 4096:6160].rearrange("p (h i t) -> p h i t", h=2, i=8)
    turn_b = phase[:, 6160:8224].rearrange("p (h i t) -> p h i t", h=2, i=8)
    b_tmp = phase[:, 8224:9248].rearrange("p (v i h) -> p v i h", v=4, i=TILES)
    b_exp = phase[:, 9248:10272].rearrange("p (r i g h) -> p r i g h", r=2, i=TILES, g=2)
    c_exp = phase[:, 10272:11296].rearrange("p (r q g s) -> p r q g s", r=2, q=QUADS, g=2)
    b_raw = phase[:, 11296:11808].rearrange("p (r i h) -> p r i h", r=2, i=TILES)
    c_raw = phase[:, 11808:12320].rearrange("p (r q s) -> p r q s", r=2, q=QUADS)
    xT = phase[:, 0:1024].rearrange("p (k s) -> p k s", k=KC)
    pick = phase[:, 1024:1280].rearrange("p (t s) -> p t s", t=NT)
    back = phase[:, 1280:1536].rearrange("p (t s) -> p t s", t=NT)
    match = phase[:, 1536:1792].rearrange("p (t e s) -> p t e s", t=NT, e=2)
    backT = phase[:, 1792:2048].rearrange("p (t s) -> p t s", t=NT)
    act_buf = phase[:, 2048:2560]
    ffT = phase[:, 2560:3072].rearrange("p (c s) -> p c s", c=4)
    ybuf = phase[:, 3072:4096].rearrange("p (h n) -> p h n", h=2)
    ov_sel = phase[:, 4096:4864].rearrange("p (b j) -> p b j", b=OV_BLOCKS)
    ov_tmp = phase[:, 4864:5632].rearrange("p (b j) -> p b j", b=OV_BLOCKS)
    NJ = EXTRA * EXPERTS
    ov_on, ov_cum, ov_v = (phase[:, 5632 + NJ * n:5632 + NJ * (n + 1)] for n in range(3))

    const_in, x_in = signal("const_in", 16), signal("x_in", 16)
    layer_in = signal("layer_in", 6 * 16)
    setup_in = signal("setup_in", 10 * 16)
    landed = [signal(f"landed{g}", 16 * ((3 if g < 2 else 2) + PAIRS)) for g in range(RING)]
    ov_landed = signal("ov_landed", 16 * RING * OV_PAIRS)
    w_used = signal("w_used", LAYER_GROUPS, RING)
    ov_used = signal("ov_used", RING * OV_PAIRS, 1)
    stored = signal("stored", 64)
    ssq_act, ssq_dve, std_ready, rstd_ready = (signal(n) for n in ("ssq_act", "ssq_dve", "std_ready", "rstd_ready"))
    diag_ready, hT_mm, hT_act, hT_dve = signal("diag_ready", 2), signal("hT_mm", 4), signal("hT_act", 2), signal("hT_dve", 2)
    u_mm, uT_act, uT_dve, k_mm = (signal(n) for n in ("u_mm", "uT_act", "uT_dve", "k_mm"))
    q_raw, k_raw, v_raw = (signal(n, 2) for n in ("q_raw", "k_raw", "v_raw"))
    rope_ready, qk_sq, qk_ss, qk_std = signal("rope_ready"), signal("qk_sq", 4), signal("qk_ss", 2), signal("qk_std", 2)
    qk_inv = signal("qk_inv", 2)
    q_roped, k_roped = signal("q_roped", 2), signal("k_roped", 2)
    qk_turned, qT_ready, kT_ready = signal("qk_turned", 2), signal("qT_ready", 2), signal("kT_ready", 2)
    scored, maxed, exped = signal("scored", 3), signal("maxed", 3), signal("exped", 16)
    p_turned, pT_ready, pv_done, o_ready = signal("p_turned", 3), signal("pT_ready", 6), signal("pv_done", 3), signal("o_ready", 3)
    o_turned, oT_ready = signal("o_turned"), signal("oT_ready", 2)
    bu_done, scanned, rotated, carried = signal("bu_done", 8), signal("scanned", 8), signal("rotated", 32), signal("carried", 4)
    y_done, y_ready, gelu_in, gelu_tanh, z_ready = (signal(n, 8) for n in ("y_done", "y_ready", "gelu_in", "gelu_tanh", "z_ready"))
    ga_done, ya_done, ga_tanh, mix_a = signal("ga_done", 3), signal("ya_done", 3), signal("ga_tanh", 4), signal("mix_a", 4)
    gs_done, glu_done, gate_tanh, mixed = signal("gs_done", 3), signal("glu_done", 3), signal("gate_tanh", 8), signal("mixed", 4)
    mixT_mm, mixT_act, mixT_dve = signal("mixT_mm", 4), signal("mixT_act", 2), signal("mixT_dve", 2)
    wo_done, x_mid, x_new = signal("wo_done", 1), signal("x_mid", 4), signal("x_new", 4)
    vec_mm, vec_ready, dt_exp, log_decay, decay_ready = (signal(n) for n in ("vec_mm", "vec_ready", "dt_exp", "log_decay", "decay_ready"))
    turns_ready, sin_ready, half_ready = signal("turns_ready", 2), signal("sin_ready", 2), signal("half_ready", 2)
    f_ready, expanded = signal("f_ready"), signal("expanded", 4)
    bt_mm, ct_mm, b_ready, c_ready = signal("bt_mm"), signal("ct_mm"), signal("b_ready", 4), signal("c_ready", 3)
    logits_mm, group_max, group_exp, top_diff, top_exp = (signal(n, k) for n, k in (
        ("logits_mm", 1), ("group_max", 1), ("group_exp", 2), ("top_diff", 1), ("top_exp", 1)))
    assigned, pos_mm, routed, ov_listed = signal("assigned"), signal("pos_mm"), signal("routed"), signal("ov_listed")
    dve_start, dve_layer, dve_setup, dve_list = signal("dve_start", 2), signal("dve_layer", 114), signal("dve_setup", 38), signal("dve_list", 21)
    settled = signal("settled")
    pool_layer, pool_setup = signal("pool_layer", 57), signal("pool_setup", 6)

    def pair_signals(prefix, pairs, used):
        s = {"pairs": pairs, "used": used}
        for n in ("match", "pick", "gathered", "xT"):
            s[n] = signal(prefix + n, pairs + 1)
        for n in ("back", "tanh", "silu", "h", "ffT_mm", "backT_mm", "ffT", "backT", "y0_mm", "y0", "y1", "scattered"):
            s[n] = signal(prefix + n, pairs)
        return s

    main, over = pair_signals("m_", PAIRS, w_used), pair_signals("ov_", OV_PAIRS, ov_used)

    def wide(ap, axis, shape):
        return ap.unsqueeze(axis).to_broadcast([P] + list(shape))

    win_d = w_in.rearrange("l (k p) n -> l p k n", p=P)
    wattn_d = w_attn.rearrange("l (k p) n -> l p k n", p=P)
    wglu_d = w_glu.rearrange("l (k p) (c n) -> l p k c n", p=P, c=2)
    wout_d = w_out.rearrange("l (k p) n -> l p k n", p=P)
    wgu_d = w_gate_up.rearrange("l e (k p) n -> (l e) p k n", p=P)
    wdn_d = w_down.rearrange("l e (k p) n -> (l e) p k n", p=P)

    U0, V0, GS, GA = 0, D, 2 * D, 3 * D
    front = []
    for j in range(4):
        front.append((j, lambda l, j=j: win_d[bass.ds(l, 1), :, 2 * j:2 * j + 2, U0:U0 + D]))
    for j in range(4):
        front.append((4 + j, lambda l, j=j: win_d[bass.ds(l, 1), :, 2 * j:2 * j + 2, V0:V0 + D]))
    for j in range(4):
        front.append((8 + j, lambda l, j=j: win_d[bass.ds(l, 1), :, 2 * j:2 * j + 2, GA:GA + D]))
    for j in range(2):
        front.append((j, lambda l, j=j: wattn_d[bass.ds(l, 1), :, 2 * j:2 * j + 2, :]))
    for j in range(4):
        front.append((2 + j, lambda l, j=j: win_d[bass.ds(l, 1), :, 2 * j:2 * j + 2, GS:GS + D]))
    for j in range(4):
        front.append((6 + j, lambda l, j=j: wglu_d[bass.ds(l, 1), :, j, :, :]))
    for j in range(4):
        front.append(((10 + j) % RING, lambda l, j=j: wout_d[bass.ds(l, 1), :, 2 * j:2 * j + 2, :]))
    assert len(front) == FRONT_GROUPS

    def pair_group(g):
        return (g % 2, False, g // 2) if g < 8 else (g % 2, True, (g - 8) // 2)

    def flat(ap, pattern="o p c n -> (o p) c n"):
        return ap.rearrange(pattern)

    def load_expert_group(sp, g, index, landing):
        _, down, j = pair_group(g)
        src = (wdn_d if down else wgu_d)[bass.ds(index, 1), :, 2 * j:2 * j + 2, :]
        sp.dma_start(ring[:, g], flat(src)).then_inc(landing, 16)

    block = ctx.enter_context(nc.Block())

    @block.sync
    def _(sp):
        sp.dma_start(xs, x.rearrange("o (t p) d -> p (o t) d", p=P)).then_inc(x_in, 16)
        sp.dma_start(cst, consts).then_inc(const_in, 16)
        with sp.Fori(0, DEPTH) as l:
            for n, (g, src) in enumerate(front):
                sp.wait_ge(w_used, at(w_used, l, n + 1 - RING))
                sp.dma_start(ring[:, g], flat(src(l))).then_inc(landed[g], 16)
            for g in list(range(2, RING)) + [0, 1]:
                sp.wait_ge(w_used, at(w_used, l, RING + g + 1 if g > 1 else 2 * RING + g + 1))
                sp.sem_inc(settled, 1)
                load_expert_group(sp, g, l * EXPERTS + g % 2, landed[g])
            with sp.Fori(1, PAIRS) as p:
                for g in range(RING):
                    sp.wait_ge(w_used, at(w_used, l, FRONT_GROUPS + (p - 1) * RING + g + 1))
                    sp.sem_inc(settled, 1)
                    load_expert_group(sp, g, l * EXPERTS + p * 2 + g % 2, landed[g])
            sp.wait_ge(routed, at(routed, l, 1))
            sp.sem_inc(settled, 1)
            most = sp.value_load(ov_flag[0:1, 0:1], min_val=0, max_val=SEQ)
            with sp.If(most > SLOTS):
                sp.wait_ge(ov_listed, at(ov_listed, l, 1))
                sp.sem_inc(settled, 1)
                sp.wait_ge(w_used, at(w_used, l, LAYER_GROUPS))
                sp.sem_inc(settled, 1)
                with sp.Fori(0, OV_PAIRS) as i:
                    sp.wait_ge(ov_used, at(ov_used, l, i * RING))
                    for e in range(2):
                        expert = sp.value_load(ov_ids[0:1, bass.ds(i * 2 + e, 1)], min_val=0, max_val=EXPERTS - 1)
                        for g in range(e, RING, 2):
                            load_expert_group(sp, g, l * EXPERTS + expert, ov_landed)
                sp.wait_ge(ov_used, at(ov_used, l, RING * OV_PAIRS))
                sp.sem_inc(settled, 1)
            with sp.Else():
                sp.sem_inc(ov_landed, per[ov_landed.name])
            sp.nop()
        for t in range(NT):
            sp.wait_ge(x_new, at(x_new, DEPTH - 1, 2 * (t + 1)))
            sp.dma_start(out.rearrange("o (t p) d -> p (o t) d", p=P)[:, t], xs[:, t]).then_inc(stored, 16)
        sp.wait_ge(stored, 16 * NT)

    @block.tensor
    def _(pe):
        def norm(n):
            pe.wait_ge(diag_ready, at(diag_ready, n, 2))
            for k in range(KC):
                for t in range(NT):
                    mm = pe.matmul(ps[:, k // 2, (k % 2) * SEQ + t * P:(k % 2) * SEQ + (t + 1) * P],
                                   xs[:, t, k * P:(k + 1) * P], diag[:, t], start=True, stop=True)
                if k % 2:
                    mm.then_inc(hT_mm, 1)

        def hT_wait(n, k):
            sig, c = ((hT_act, hT_dve)[(k // 2) % 2], k // 4 + 1)
            pe.wait_ge(sig, at(sig, n, c))

        def setup_vectors(n, bank):
            pe.wait_ge(setup_in, at(setup_in, n, per[setup_in.name]))
            pe.sem_inc(settled, 1)
            pe.transpose(ps[:, bank, 0:N_VEC], rows[0:N_VEC, :], const("ident")[0:N_VEC, 0:N_VEC]).then_inc(vec_mm, 1)

        def setup_matrices(l):
            pe.wait_ge(expanded, at(expanded, l, 4))
            for r in range(2):
                for q in range(QUADS):
                    mm = pe.transpose(ps[:, r, q * P:(q + 1) * P],
                                      b_exp[:, r, 4 * q:4 * q + 4].rearrange("p i g h -> p (i g h)"), const("ident"))
            mm.then_inc(bt_mm, 1)
            for r in range(2):
                for q in range(QUADS):
                    mm = pe.transpose(ps[:, 2 + r, q * P:(q + 1) * P],
                                      c_exp[:, r, q].rearrange("p g s -> p (g s)"), const("ident"))
            mm.then_inc(ct_mm, 1)

        pe.wait_ge(const_in, 16)
        pe.wait_ge(x_in, 16)
        pe.sem_inc(w_used, ahead[w_used.name])
        pe.sem_inc(ov_used, ahead[ov_used.name])
        norm(0)
        setup_vectors(0, 7)
        pe.wait_ge(vec_ready, at(vec_ready, 0, 1))

        with pe.Fori(0, DEPTH) as l:
            def weights(g, turn):
                pe.wait_ge(landed[g], at(landed[g], l, 16 * (turn + 1)))

            def release(mm):
                mm.then_inc(w_used, 1)

            def project_u():
                for k in range(KC):
                    if k % 2 == 0:
                        hT_wait(l * 2, k)
                        weights(k // 2, 0)
                    for c in range(4):
                        mm = pe.matmul(ps[:, 4 + c // 2, (c % 2) * SEQ:(c % 2 + 1) * SEQ],
                                       ring[:, k // 2, k % 2, c * P:(c + 1) * P], hT[:, k],
                                       start=(k == 0 and c % 2 == 0), stop=(k == KC - 1), skip_group_check=True)
                mm.then_inc(u_mm, 1)

            def project_qkv(which, ks):
                bank, group, col = {"q": (0, 0, 512), "k": (2, 4, 0), "v": (0, 4, 512)}[which]
                for k in ks:
                    if k == 0 and which == "q":
                        pe.wait_ge(b_ready, at(b_ready, l, 4))
                        pe.wait_ge(c_ready, at(c_ready, l, 3))
                    if k == 0 and which == "v":
                        pe.wait_ge(q_raw, at(q_raw, l, 2))
                        pe.wait_ge(qk_sq, at(qk_sq, l, 2))
                    if which == "k" and k % 2 == 0:
                        weights(4 + k // 2, 0)
                    for t in range(NT):
                        mm = pe.matmul(ps[:, bank + t], hT[:, k, t * P:(t + 1) * P],
                                       ring[:, group + k // 2, k % 2, col:col + 512], start=(k == 0), stop=(k == KC - 1))
                    if k % 2 and which != "k":
                        release(mm)
                    if which == "k" and k == KC - 1:
                        mm.then_inc(k_mm, 1)

            def scan_input(k):
                half, q = divmod(k, 4)
                if k == 0:
                    pe.wait_ge(uT_act, at(uT_act, l, 1))
                    pe.wait_ge(uT_dve, at(uT_dve, l, 1))
                if k == 0:
                    pe.wait_ge(b_ready, at(b_ready, l, 4))
                if k >= 2:
                    pe.wait_ge(y_ready, at(y_ready, l, k - 1))
                for j in range(4):
                    r = slice(64 * (j // 2), 64 * (j // 2) + 64)
                    for part in range(2):
                        mm = pe.matmul(ps[:, 4 + 2 * (k % 2) + j // 2, (2 * part + j % 2) * P:(2 * part + j % 2 + 1) * P],
                                       b_lhs[r, part, j % 2, q], uT[r, q, half * HALF:(half + 1) * HALF],
                                       start=True, stop=True)
                mm.then_inc(bu_done, 1)

            def scan_output(k):
                q = k % 4
                pe.wait_ge(rotated, at(rotated, l, 4 * (k + 1)))
                for v in range(4):
                    for j in range(4):
                        mm = pe.matmul(ps[32 * j:32 * j + 32, 4 + 2 * (k % 2), 0:P],
                                       c_lhs[:, (0, 1, 2, 2)[v], q, 32 * j:32 * j + 32], post[:, v, j],
                                       start=(v == 0), stop=(v == 3), skip_group_check=True)
                mm.then_inc(y_done, 1)

            def turn_heads(w):
                if w == 0:
                    pe.wait_ge(k_raw, at(k_raw, l, 2))
                    pe.wait_ge(qk_sq, at(qk_sq, l, 4))
                    pe.wait_ge(q_roped, at(q_roped, l, 2))
                else:
                    pe.wait_ge(v_raw, at(v_raw, l, 2))
                    pe.wait_ge(k_roped, at(k_roped, l, 2))
                for t in range(NT):
                    for c in range(4):
                        mm = pe.transpose(ps[:, 2 - 2 * w + c // 2, (c % 2) * SEQ + t * P:(c % 2) * SEQ + (t + 1) * P],
                                          raw[:, 2 * w + t, c * P:(c + 1) * P], const("ident"))
                mm.then_inc(qk_turned, 1)

            BATCH = [(0, range(0, 8)), (1, range(0, 4)), (1, range(4, 8))]

            def bank(b):
                return (0, 2, 0)[b]

            def scores(b):
                tile, heads = BATCH[b]
                n = P * (tile + 1)
                if b == 0:
                    pe.wait_ge(qT_ready, at(qT_ready, l, 2))
                    pe.wait_ge(kT_ready, at(kT_ready, l, 2))
                if b == 2:
                    pe.wait_ge(o_ready, at(o_ready, l, 1))
                for i, h in enumerate(heads):
                    r = slice(64 * (h % 2), 64 * (h % 2) + 64)
                    mm = pe.matmul(ps[:, bank(b) + h % 2, (i // 2) * n:(i // 2 + 1) * n],
                                   qT[r, h // 2, tile * P:(tile + 1) * P], kT[r, h // 2, 0:n], start=True, stop=True)
                mm.then_inc(scored, 1)

            def turn_probs(b):
                pe.wait_ge(exped, at(exped, l, (8, 12, 16)[b]))
                for j in range(8):
                    mm = pe.transpose(ps[:, bank(b) + j // 4, (j % 4) * P:(j % 4 + 1) * P], probs[:, j * P:(j + 1) * P],
                                      const("ident"))
                mm.then_inc(p_turned, 1)

            def values(b):
                tile, heads = BATCH[b]
                pe.wait_ge(pT_ready, at(pT_ready, l, 2 * (b + 1)))
                for i, h in enumerate(heads):
                    s = (h % 2) * (len(heads) // 2) + i // 2
                    for c in range(tile + 1):
                        j = s * (tile + 1) + c
                        mm = pe.matmul(ps[:, bank(b), i * HD:(i + 1) * HD], probs[:, j * P:(j + 1) * P],
                                       vtok[:, c, h * HD:(h + 1) * HD], start=(c == 0), stop=(c == tile))
                mm.then_inc(pv_done, 1)

            def turn_attention():
                pe.wait_ge(o_ready, at(o_ready, l, 3))
                for t in range(NT):
                    for c in range(4):
                        mm = pe.transpose(ps[:, 2 + c // 2, (c % 2) * SEQ + t * P:(c % 2) * SEQ + (t + 1) * P],
                                          attn[:, t, c * P:(c + 1) * P], const("ident"))
                mm.then_inc(o_turned, 1)

            def attention_gate(u):
                t, half = divmod(u, 2)
                if u == 0:
                    for j in range(4):
                        weights(8 + j, 0)
                if u < 2:
                    pe.wait_ge(y_ready, at(y_ready, l, 7 + u))
                else:
                    pe.wait_ge(ga_tanh, at(ga_tanh, l, u - 1))
                for k in range(KC):
                    mm = pe.matmul(ps[:, 4 + 2 * (u % 2)], hT[:, k, t * P:(t + 1) * P],
                                   ring[:, 8 + k // 2, k % 2, 512 * half:512 * half + 512], start=(k == 0), stop=(k == KC - 1))
                    if u == 3 and k % 2:
                        release(mm)
                if u < 3:
                    mm.then_inc(ga_done, 1)

            def attention_project(u):
                t, half = divmod(u, 2)
                if u == 0:
                    pe.wait_ge(oT_ready, at(oT_ready, l, 2))
                    weights(0, 1)
                    weights(1, 1)
                if u >= 2:
                    pe.wait_ge(mix_a, at(mix_a, l, u - 1))
                for c in range(4):
                    mm = pe.matmul(ps[:, 5 + 2 * (u % 2)], oT[:, c, t * P:(t + 1) * P],
                                   ring[:, c // 2, c % 2, 512 * half:512 * half + 512], start=(c == 0), stop=(c == 3))
                    if u == 3 and c % 2:
                        release(mm)
                if u < 3:
                    mm.then_inc(ya_done, 1)

            def ssm_gate(u):
                t, half = divmod(u, 2)
                if u == 0:
                    for j in range(4):
                        weights(2 + j, 1)
                if u == 1:
                    pe.wait_ge(mix_a, at(mix_a, l, 4))
                if u >= 2:
                    pe.wait_ge(mixed, at(mixed, l, u - 1))
                for k in range(KC):
                    mm = pe.matmul(ps[:, 4 * (u % 2)], hT[:, k, t * P:(t + 1) * P],
                                   ring[:, 2 + k // 2, k % 2, 512 * half:512 * half + 512], start=(k == 0), stop=(k == KC - 1))
                    if u == 3 and k % 2:
                        release(mm)
                if u < 3:
                    mm.then_inc(gs_done, 1)

            def ssm_project(u):
                t, half = divmod(u, 2)
                pe.wait_ge(z_ready, at(z_ready, l, 4 * (t + 1)))
                for k in range(4):
                    if u == 0:
                        weights(6 + k, 1)
                    for w in range(2):
                        mm = pe.matmul(ps[:, 4 * (u % 2) + 1 + w], uT[:, k, t * P:(t + 1) * P],
                                       ring[:, 6 + k, w, 512 * half:512 * half + 512], start=(k == 0), stop=(k == 3))
                    if u == 3:
                        release(mm)
                if u < 3:
                    mm.then_inc(glu_done, 1)

            def turn_mix(t):
                pe.wait_ge(mixed, at(mixed, l, 2 * (t + 1)))
                if t:
                    pe.wait_ge(mixT_act, at(mixT_act, l, t))
                    pe.wait_ge(mixT_dve, at(mixT_dve, l, t))
                for c in range(KC):
                    mm = pe.transpose(ps[:, (3, 7)[c // 4], (c % 4) * P:(c % 4 + 1) * P], mix[:, t, c * P:(c + 1) * P],
                                      const("ident"))
                    if c % 4 == 3:
                        mm.then_inc(mixT_mm, 1)

            def project_out(t):
                pe.wait_ge(mixT_act, at(mixT_act, l, t + 1))
                pe.wait_ge(mixT_dve, at(mixT_dve, l, t + 1))
                pe.wait_ge(mixed, at(mixed, l, 3 + t))
                for k in range(KC):
                    g = (10 + k // 2) % RING
                    if t == 0 and k % 2 == 0:
                        weights(g, 1 if k < 4 else 2)
                    for half in range(2):
                        mm = pe.matmul(ps[:, 4 * t + half], hT[:, k, t * P:(t + 1) * P],
                                       ring[:, g, k % 2, 512 * half:512 * half + 512], start=(k == 0), stop=(k == KC - 1))
                    if t == 1 and k % 2:
                        release(mm)
                if t == 0:
                    mm.then_inc(wo_done, 1)

            project_u()
            setup_matrices(l)
            scan_input(0)
            scan_input(1)
            project_qkv("q", range(0, 6))
            scan_output(0)
            project_qkv("q", range(6, 7))
            scan_input(2)
            project_qkv("q", range(7, 8))
            project_qkv("k", range(0, 2))
            scan_output(1)
            project_qkv("k", range(2, 3))
            scan_input(3)
            project_qkv("k", range(3, 5))
            scan_output(2)
            project_qkv("k", range(5, 6))
            scan_input(4)
            project_qkv("k", range(6, 8))
            project_qkv("v", range(0, 1))
            scan_output(3)
            project_qkv("v", range(1, 2))
            scan_input(5)
            project_qkv("v", range(2, 5))
            scan_output(4)
            project_qkv("v", range(5, 6))
            scan_input(6)
            project_qkv("v", range(6, 8))
            scan_output(5)
            turn_heads(0)
            scan_input(7)
            turn_heads(1)
            scan_output(6)
            scores(0)
            attention_gate(0)
            turn_probs(0)
            scores(1)
            scan_output(7)
            values(0)
            attention_gate(1)
            turn_probs(1)
            scores(2)
            values(1)
            attention_gate(2)
            turn_probs(2)
            values(2)
            attention_gate(3)
            turn_attention()
            ssm_gate(0)
            for u in range(4):
                attention_project(u)
            ssm_project(0)
            for u in range(1, 3):
                ssm_gate(u)
                ssm_project(u)
            turn_mix(0)
            ssm_gate(3)
            ssm_project(3)
            pe.wait_ge(mixed, at(mixed, l, 3))
            setup_vectors(l + 1, 2)
            project_out(0)
            turn_mix(1)
            project_out(1)

            pe.wait_ge(x_mid, at(x_mid, l, 4))
            pe.wait_ge(vec_ready, at(vec_ready, l + 1, 1))
            norm(l * 2 + 1)
            pe.wait_ge(layer_in, at(layer_in, l, per[layer_in.name]))
            pe.wait_ge(hT_act, at(hT_act, l * 2 + 1, 2))
            pe.wait_ge(hT_dve, at(hT_dve, l * 2 + 1, 2))
            for t in range(NT):
                for k in range(KC):
                    mm = pe.matmul(ps[:, 0, t * 36:(t + 1) * 36], hT[:, k, t * P:(t + 1) * P], router_w[:, k],
                                   start=(k == 0), stop=(k == KC - 1))
            mm.then_inc(logits_mm, 1)
            for n in range(4):
                pe.matmul(ps[:, 4 + n], const("zero"), cst[:, 0:512], start=True, stop=False, skip_group_check=True)
            pe.wait_ge(assigned, at(assigned, l, 1))
            pe.matmul(ps[:, 1, 0:32], const("before"), assign[:, 0], start=True, stop=True)
            pe.matmul(ps[:, 1, 32:64], const("ones"), assign[:, 0], start=True, stop=False)
            pe.matmul(ps[:, 1, 32:64], const("before"), assign[:, 1], start=False, stop=True)
            pe.matmul(ps[:, 1, 64:96], const("ones"), assign[:, 0], start=True, stop=False)
            pe.matmul(ps[:, 1, 64:96], const("ones"), assign[:, 1], start=False, stop=True).then_inc(pos_mm, 1)

            def gather(S, i):
                pe.wait_ge(S["pick"], at(S["pick"], l, i + 1))
                for k in range(KC):
                    for t in range(NT):
                        mm = pe.matmul(ps[:, 2 + k // 4, (k % 4) * P:(k % 4 + 1) * P], xs[:, t, k * P:(k + 1) * P],
                                       pick[:, t], start=(t == 0), stop=(t == NT - 1))
                mm.then_inc(S["gathered"], 1)

            def pair(S, i, wait_weights):
                pe.wait_ge(S["xT"], at(S["xT"], l, i + 1))
                for k in range(KC):
                    for e in range(2):
                        g = 2 * (k // 2) + e
                        if k % 2 == 0:
                            wait_weights(g)
                        rows_e = slice(SLOTS * e, SLOTS * (e + 1))
                        for half in range(2):
                            mm = pe.matmul(ps[rows_e, half], xT[:, k, rows_e], ring[:, g, k % 2, 512 * half:512 * half + 512],
                                           start=(k == 0), stop=(k == KC - 1), skip_group_check=True)
                        if k % 2:
                            mm.then_inc(S["used"], 1)
                gather(S, i + 1)
                pe.wait_ge(S["h"], at(S["h"], l, i + 1))
                for c in range(4):
                    mm = pe.transpose(ps[:, 0, c * P:(c + 1) * P], act_buf[:, c * P:(c + 1) * P], const("ident"))
                mm.then_inc(S["ffT_mm"], 1)
                pe.wait_ge(S["back"], at(S["back"], l, i + 1))
                for t in range(NT):
                    mm = pe.transpose(ps[:, 1, t * P:(t + 1) * P], back[:, t], const("ident"))
                mm.then_inc(S["backT_mm"], 1)
                pe.wait_ge(S["ffT"], at(S["ffT"], l, i + 1))
                pe.wait_ge(S["xT"], at(S["xT"], l, i + 2))
                for half in range(2):
                    for c in range(4):
                        for e in range(2):
                            g = 8 + 2 * (c // 2) + e
                            if half == 0 and c % 2 == 0:
                                wait_weights(g)
                            rows_e = slice(SLOTS * e, SLOTS * (e + 1))
                            mm = pe.matmul(ps[rows_e, 2 + half], ffT[:, c, rows_e],
                                           ring[:, g, c % 2, 512 * half:512 * half + 512],
                                           start=(c == 0), stop=(c == 3), skip_group_check=True)
                            if half == 1 and c % 2:
                                mm.then_inc(S["used"], 1)
                    if half == 0:
                        mm.then_inc(S["y0_mm"], 1)
                pe.wait_ge(S["backT"], at(S["backT"], l, i + 1))
                for half in range(2):
                    pe.wait_ge(S[("y0", "y1")[half]], at(S[("y0", "y1")[half]], l, i + 1))
                    for t in range(NT):
                        mm = pe.matmul(ps[:, 4 + 2 * t + half], backT[:, t], ybuf[:, half],
                                       start=False, stop=False, skip_group_check=True)
                mm.then_inc(S["scattered"], 1)

            gather(main, 0)
            with pe.Fori(0, PAIRS) as p:
                pair(main, p, lambda g: pe.wait_ge(landed[g], at(landed[g], l, 16 * ((3 if g < 2 else 2) + 1) + p * 16)))
            most = pe.value_load(ov_flag[0:1, 0:1], min_val=0, max_val=SEQ)
            with pe.If(most > SLOTS):
                gather(over, 0)
                with pe.Fori(0, OV_PAIRS) as i:
                    pe.wait_ge(ov_landed, at(ov_landed, l, (i + 1) * 16 * RING))
                    pair(over, i, lambda g: None)
            with pe.Else():
                for n in ("gathered", "ffT_mm", "backT_mm", "y0_mm", "scattered"):
                    pe.sem_inc(over[n], per[over[n].name])
                pe.sem_inc(ov_used, per[ov_used.name])
            pe.nop()
            norm(l * 2 + 2)

    @block.scalar
    def _(act):
        def load_setup(l):
            def put(dst, src):
                act.dma_start(dst, src).then_inc(setup_in, 16)

            one = bass.ds(l, 1)
            put(rows[0:8, :], norm1_g[one].rearrange("o (r c) -> (o r) c", c=P))
            put(rows[8:16, :], norm2_g[one].rearrange("o (r c) -> (o r) c", c=P))
            put(rows[16:20, :], ssm_d[one].rearrange("o (r c) -> (o r) c", c=P))
            put(rows[20:36, :], ssm_a_re[one].rearrange("o (i g) s -> (o i) (g s)", g=2))
            put(rows[36:52, :], ssm_a_im[one].rearrange("o (i g) s -> (o i) (g s)", g=2))
            put(log_dt, ssm_log_dt[one].to_broadcast([P, GROUPS]))
            for r, b in enumerate((ssm_b_re, ssm_b_im)):
                put(b_raw[:, r], b[one].rearrange("o (i g) s h -> (o g s) i h", g=2))
            for r, c in enumerate((ssm_c_re, ssm_c_im)):
                put(c_raw[:, r], c[one].rearrange("o (q g) h s -> (o g h) q s", q=QUADS))

        def load_layer(l):
            def put(dst, src):
                act.dma_start(dst, src).then_inc(layer_in, 16)

            one = bass.ds(l, 1)
            put(qk_gain[:, 0], q_norm_g[one].to_broadcast([P, HD]))
            put(qk_gain[:, 1], k_norm_g[one].to_broadcast([P, HD]))
            put(router_w[:, :, 0:4], router_w_group[one].rearrange("o (k p) n -> (o p) k n", p=P))
            put(router_w[:, :, 4:36], router_w_expert[one].rearrange("o (k p) n -> (o p) k n", p=P))
            put(router_b[:, 0:4], router_b_group[one].to_broadcast([P, EGROUPS]))
            put(router_b[:, 4:36], router_b_expert[one].to_broadcast([P, EXPERTS]))

        def norm_squares(n):
            act.activation(junk[:, 0], xs[:, 0], ACT.Square, accum_out=ssq[:, 0:1]).then_inc(ssq_act, 1)
            act.wait_ge(ssq_act, at(ssq_act, n, 1))
            act.wait_ge(ssq_dve, at(ssq_dve, n, 1))
            act.activation(std, ssq, ACT.Sqrt, bias=const("eps"), scale=1.0 / D).then_inc(std_ready, 1)

        def norm_turned(n, gain):
            for m, b in enumerate((0, 2)):
                act.wait_ge(hT_mm, at(hT_mm, n, b + 1))
                for k in (2 * b, 2 * b + 1):
                    ins = act.activation(hT[:, k], ps[:, b, (k % 2) * SEQ:(k % 2 + 1) * SEQ], ACT.Copy, scale=gain[:, k:k + 1])
                ins.then_inc(hT_act, 1)

        def setup_exps(n):
            act.wait_ge(setup_in, at(setup_in, n, per[setup_in.name]))
            act.activation(log_dt, log_dt, ACT.Exp).then_inc(dt_exp, 1)
            act.wait_ge(log_decay, at(log_decay, n, 1))
            act.activation(decay, sc0, ACT.Exp).then_inc(decay_ready, 1)

        def setup_sines(n, h):
            act.wait_ge(turns_ready, at(turns_ready, n, h + 1))
            act.activation(sinT[:, 8 * h:8 * h + 8], turn_a[:, h], ACT.Sin, scale=TWO_PI).then_inc(sin_ready, 1)
            act.activation(turn_b[:, h], turn_a[:, h], ACT.Sin, scale=TWO_PI / 2).then_inc(half_ready, 1)

        load_setup(0)
        act.wait_ge(x_in, 16)
        act.wait_ge(const_in, 16)
        norm_squares(0)
        setup_exps(0)
        norm_turned(0, turned("norm1"))
        for h in range(2):
            setup_sines(0, h)

        with act.Fori(0, DEPTH) as l:
            load_layer(l)
            act.wait_ge(u_mm, at(u_mm, l, 1))
            act.copy(uT[:, 0:2].rearrange("p q s -> p (q s)"), ps[:, 4]).then_inc(uT_act, 1)
            act.wait_ge(bt_mm, at(bt_mm, l, 1))
            for r in range(2):
                for o in range(2):
                    act.activation(b_lhs[:, r, o].rearrange("p q s -> p (q s)"), ps[:, r], ACT.Copy,
                                   scale=const("odd_tile")[:, o:o + 1]).then_inc(b_ready, 1)

            def heads_out(w):
                if w == 0:
                    act.wait_ge(w_used, at(w_used, l, 4))
                else:
                    act.wait_ge(k_mm, at(k_mm, l, 1))
                for t in range(NT):
                    act.copy(raw[:, 2 * w + t], ps[:, 2 * w + t]).then_inc((q_raw, k_raw)[w], 1)
                if w == 1:
                    act.wait_ge(qk_ss, at(qk_ss, l, 1))
                for t in range(NT):
                    act.activation(squares[:, t], ps[:, 2 * w + t], ACT.Square).then_inc(qk_sq, 1)

            def heads_std(w):
                act.wait_ge(qk_ss, at(qk_ss, l, w + 1))
                act.activation(head_rs[:, 2 * w:2 * w + 2], head_ss[:, 2 * w:2 * w + 2], ACT.Sqrt, bias=const("eps"),
                               scale=1.0 / HD).then_inc(qk_std, 1)

            def gelu(k):
                act.wait_ge(gelu_in, at(gelu_in, l, k + 1))
                act.activation(y2, y3, ACT.Tanh, scale=GELU_C).then_inc(gelu_tanh, 1)

            def exps(b):
                n = (8, 4, 4)[b]
                w = 1024 // n
                act.wait_ge(maxed, at(maxed, l, b + 1))
                for s in range(n):
                    i = 2 * (s % (n // 2)) + s // (n // 2)
                    act.activation(probs[:, s * w:(s + 1) * w], probs[:, s * w:(s + 1) * w], ACT.Exp,
                                   bias=row_max[:, s:s + 1], scale=ATT_SCALE,
                                   accum_out=row_sum[:, i:i + 1]).then_inc(exped, 1)

            def probs_turned(b):
                act.wait_ge(p_turned, at(p_turned, l, b + 1))
                for n in range(2):
                    act.copy(probs[:, n * 512:(n + 1) * 512], ps[:, (0, 2, 0)[b] + n]).then_inc(pT_ready, 1)

            def att_gate_out(u):
                if u < 3:
                    act.wait_ge(ga_done, at(ga_done, l, u + 1))
                else:
                    act.wait_ge(w_used, at(w_used, l, 12))
                if u == 0:
                    act.wait_ge(scanned, at(scanned, l, 8))
                act.activation(att_gate[:, u], ps[:, 4 + 2 * (u % 2)], ACT.Tanh, scale=0.5).then_inc(ga_tanh, 1)

            heads_out(0)
            heads_std(0)
            gelu(0)
            gelu(1)
            heads_out(1)
            gelu(2)
            heads_std(1)
            gelu(3)
            act.wait_ge(w_used, at(w_used, l, 8))
            for t in range(NT):
                act.copy(vtok[:, t], ps[:, t]).then_inc(v_raw, 1)
            gelu(4)
            act.wait_ge(qk_turned, at(qk_turned, l, 1))
            for n in range(2):
                act.copy(qT[:, 2 * n:2 * n + 2].rearrange("p c s -> p (c s)"), ps[:, 2 + n]).then_inc(qT_ready, 1)
            gelu(5)
            act.wait_ge(qk_turned, at(qk_turned, l, 2))
            for n in range(2):
                act.copy(kT[:, 2 * n:2 * n + 2].rearrange("p c s -> p (c s)"), ps[:, n]).then_inc(kT_ready, 1)
            exps(0)
            probs_turned(0)
            gelu(6)
            att_gate_out(0)
            exps(1)
            probs_turned(1)
            gelu(7)
            att_gate_out(1)
            exps(2)
            probs_turned(2)
            att_gate_out(2)
            att_gate_out(3)
            act.wait_ge(o_turned, at(o_turned, l, 1))
            for n in range(2):
                act.copy(oT[:, 2 * n:2 * n + 2].rearrange("p c s -> p (c s)"), ps[:, 2 + n]).then_inc(oT_ready, 1)
            for u in range(4):
                b = 4 * (u % 2)
                if u < 3:
                    act.wait_ge(gs_done, at(gs_done, l, u + 1))
                else:
                    act.wait_ge(w_used, at(w_used, l, 18))
                if u >= 2:
                    act.wait_ge(mixed, at(mixed, l, u - 1))
                act.activation(gates[:, 0, u % 2], ps[:, b], ACT.Tanh, scale=0.5).then_inc(gate_tanh, 1)
                if u < 3:
                    act.wait_ge(glu_done, at(glu_done, l, u + 1))
                else:
                    act.wait_ge(w_used, at(w_used, l, 22))
                act.activation(gates[:, 1, u % 2], ps[:, b + 2], ACT.Tanh, scale=0.25).then_inc(gate_tanh, 1)
                if u == 2:
                    load_setup(1 - l)
                    act.wait_ge(mixT_mm, at(mixT_mm, l, 1))
                    act.copy(hT[:, 0:4, 0:P], ps[:, 3].rearrange("p (c s) -> p c s", c=4)).then_inc(mixT_act, 1)
            setup_exps(l + 1)
            act.wait_ge(mixT_mm, at(mixT_mm, l, 3))
            act.copy(hT[:, 0:4, P:2 * P], ps[:, 3].rearrange("p (c s) -> p c s", c=4)).then_inc(mixT_act, 1)
            setup_sines(l + 1, 0)
            setup_sines(l + 1, 1)
            act.wait_ge(x_mid, at(x_mid, l, 2))
            norm_squares(l * 2 + 1)
            norm_turned(l * 2 + 1, gain2)
            act.wait_ge(group_max, at(group_max, l, 1))
            for t in range(NT):
                act.activation(glog[:, t, 0:EGROUPS], glog[:, t, 0:EGROUPS], ACT.Exp, bias=rt[:, 0, t:t + 1],
                               accum_out=rt[:, 2, t:t + 1]).then_inc(group_exp, 1)
            act.wait_ge(top_diff, at(top_diff, l, 1))
            act.activation(rt[:, 4], rt[:, 1], ACT.Exp).then_inc(top_exp, 1)

            def pair(S, i, gate_up_done):
                gate_up_done()
                act.activation(act_buf, ps[:, 0], ACT.Tanh, scale=0.5).then_inc(S["tanh"], 1)
                act.wait_ge(S["ffT_mm"], at(S["ffT_mm"], l, i + 1))
                act.copy(ffT.rearrange("p c s -> p (c s)"), ps[:, 0]).then_inc(S["ffT"], 1)
                act.wait_ge(S["y0_mm"], at(S["y0_mm"], l, i + 1))
                act.copy(ybuf[:, 0], ps[:, 2]).then_inc(S["y0"], 1)

            with act.Fori(0, PAIRS) as p:
                pair(main, p, lambda: act.wait_ge(w_used, at(w_used, l, FRONT_GROUPS + p * RING + 8)))
            act.wait_ge(routed, at(routed, l, 1))
            act.sem_inc(settled, 1)
            most = act.value_load(ov_flag[0:1, 0:1], min_val=0, max_val=SEQ)
            with act.If(most > SLOTS):
                with act.Fori(0, OV_PAIRS) as i:
                    pair(over, i, lambda: act.wait_ge(ov_used, at(ov_used, l, i * RING + 8)))
            with act.Else():
                for n in ("tanh", "ffT", "y0"):
                    act.sem_inc(over[n], per[over[n].name])
            act.nop()
            act.wait_ge(x_new, at(x_new, l, 4))
            norm_squares(l * 2 + 2)
            norm_turned(l * 2 + 2, turned("norm1"))

    @block.vector
    def _(ve):
        def norm_squares(n):
            ve.tensor_tensor_reduce(out=junk[:, 1], in0=xs[:, 1], in1=xs[:, 1], scale=1.0, scalar=0.0, op0=ALU.mult,
                                    op1=ALU.add, accum_out=ssq[:, 1:2]).then_inc(ssq_dve, 1)

        def norm_scale(n):
            ve.wait_ge(std_ready, at(std_ready, n, 1))
            ve.reciprocal(rstd, std).then_inc(rstd_ready, 1)
            ve.wait_ge(rstd_ready, at(rstd_ready, n, 1))
            for t in range(NT):
                ve.tensor_scalar(diag[:, t], const("ident"), rstd[:, t:t + 1], None, ALU.mult).then_inc(diag_ready, 1)

        def norm_turned(n, gain):
            for b in (1, 3):
                ve.wait_ge(hT_mm, at(hT_mm, n, b + 1))
                ve.tensor_tensor(hT[:, 2 * b:2 * b + 2], ps[:, b].rearrange("p (k s) -> p k s", k=2),
                                 wide(gain[:, 2 * b:2 * b + 2], 2, [2, SEQ]), ALU.mult).then_inc(hT_dve, 1)

        def angles(n, S, h):
            a, b = turn_a[:, h], turn_b[:, h]
            tiles = slice(8 * h, 8 * h + 8)
            step = wide(const("step"), 1, [8, TW])
            ve.tensor_tensor(a, step, wide(turns_hi[:, tiles], 2, [8, TW]), ALU.mult).then_inc(dve_setup, 1)
            ve.wait_ge(dve_setup, S.next())
            ve.tensor_scalar(b, a, ROUND, ROUND, ALU.add, ALU.subtract).then_inc(dve_setup, 1)
            ve.wait_ge(dve_setup, S.next())
            ve.tensor_tensor(a, a, b, ALU.subtract).then_inc(dve_setup, 1)
            ve.wait_ge(dve_setup, S.next())
            ve.tensor_tensor(b, step, wide(turns_lo[:, tiles], 2, [8, TW]), ALU.mult).then_inc(dve_setup, 1)
            ve.wait_ge(dve_setup, S.next())
            ve.tensor_tensor(a, a, b, ALU.add).then_inc(dve_setup, 1)
            ve.wait_ge(dve_setup, S.next())
            ve.tensor_scalar(b, a, ROUND, ROUND, ALU.add, ALU.subtract).then_inc(dve_setup, 1)
            ve.wait_ge(dve_setup, S.next())
            ve.tensor_tensor(a, a, b, ALU.subtract).then_inc(turns_ready, 1)

        def setup_first(n, S, bank):
            ve.wait_ge(vec_mm, at(vec_mm, n, 1))
            ve.tensor_copy(vec, ps[:, bank, 0:N_VEC]).then_inc(vec_ready, 1)
            ve.wait_ge(vec_ready, at(vec_ready, n, 1))
            ve.wait_ge(dt_exp, at(dt_exp, n, 1))
            a_re, a_im = turned("a_re"), turned("a_im")
            steps = log_dt.rearrange("p (i g) -> p i g", g=2)
            for g in range(2):
                ve.tensor_copy(dt_[64 * g:64 * g + 64], steps[64 * g:64 * g + 64, :, g]).then_inc(dve_setup, 1)
                ve.wait_ge(dve_setup, S.next())
            ve.tensor_tensor(sc0, a_re, dt_, ALU.mult).then_inc(log_decay, 1)
            ve.tensor_tensor(theta, a_im, dt_, ALU.mult).then_inc(dve_setup, 1)
            ve.wait_ge(dve_setup, S.next())
            ve.tensor_scalar(turns_lo, theta, float(1.0 / (2.0 * np.pi)), None, ALU.mult).then_inc(dve_setup, 1)
            ve.wait_ge(dve_setup, S.next())
            ve.tensor_scalar(sc1, turns_lo, ROUND, ROUND, ALU.add, ALU.subtract).then_inc(dve_setup, 1)
            ve.wait_ge(dve_setup, S.next())
            ve.tensor_tensor(turns_lo, turns_lo, sc1, ALU.subtract).then_inc(dve_setup, 1)
            ve.wait_ge(dve_setup, S.next())
            ve.tensor_scalar(turns_hi, turns_lo, ROUND15, ROUND15, ALU.add, ALU.subtract).then_inc(dve_setup, 1)
            ve.wait_ge(dve_setup, S.next())
            ve.tensor_tensor(turns_lo, turns_lo, turns_hi, ALU.subtract).then_inc(dve_setup, 1)
            ve.wait_ge(dve_setup, S.next())
            ve.tensor_tensor(den, a_re, a_re, ALU.mult).then_inc(dve_setup, 1)
            ve.wait_ge(dve_setup, S.next())
            ve.tensor_tensor(sc1, a_im, a_im, ALU.mult).then_inc(dve_setup, 1)
            ve.wait_ge(dve_setup, S.next())
            ve.tensor_tensor(den, den, sc1, ALU.add).then_inc(dve_setup, 1)
            ve.wait_ge(dve_setup, S.next())
            ve.reciprocal(den, den).then_inc(dve_setup, 1)
            ve.wait_ge(dve_setup, S.next())
            angles(n, S, 0)

        def setup_second(n, S):
            angles(n, S, 1)
            for h in range(2):
                ve.wait_ge(half_ready, at(half_ready, n, h + 1))
                b = turn_b[:, h]
                ve.tensor_tensor(b, b, b, ALU.mult).then_inc(dve_setup, 1)
                ve.wait_ge(dve_setup, S.next())
                ve.tensor_scalar(cosT[:, 8 * h:8 * h + 8], b, -2.0, 1.0, ALU.mult, ALU.add).then_inc(dve_setup, 1)
                ve.wait_ge(dve_setup, S.next())
            a_re, a_im = turned("a_re"), turned("a_im")
            ve.wait_ge(decay_ready, at(decay_ready, n, 1))
            ve.wait_ge(sin_ready, at(sin_ready, n, 2))
            ve.tensor_tensor(a_bar_re, decay, cosT[:, :, 1], ALU.mult).then_inc(dve_setup, 1)
            ve.wait_ge(dve_setup, S.next())
            ve.tensor_tensor(a_bar_im, decay, sinT[:, :, 1], ALU.mult).then_inc(dve_setup, 1)
            ve.wait_ge(dve_setup, S.next())
            ve.tensor_scalar(sc0, a_bar_re, 1.0, None, ALU.subtract).then_inc(dve_setup, 1)
            ve.wait_ge(dve_setup, S.next())
            ve.tensor_tensor(f_re, sc0, a_re, ALU.mult).then_inc(dve_setup, 1)
            ve.wait_ge(dve_setup, S.next())
            ve.tensor_tensor(sc1, a_bar_im, a_im, ALU.mult).then_inc(dve_setup, 1)
            ve.wait_ge(dve_setup, S.next())
            ve.tensor_tensor(f_re, f_re, sc1, ALU.add).then_inc(dve_setup, 1)
            ve.wait_ge(dve_setup, S.next())
            ve.tensor_tensor(f_re, f_re, den, ALU.mult).then_inc(dve_setup, 1)
            ve.wait_ge(dve_setup, S.next())
            ve.tensor_tensor(f_im, a_bar_im, a_re, ALU.mult).then_inc(dve_setup, 1)
            ve.wait_ge(dve_setup, S.next())
            ve.tensor_tensor(sc1, sc0, a_im, ALU.mult).then_inc(dve_setup, 1)
            ve.wait_ge(dve_setup, S.next())
            ve.tensor_tensor(f_im, f_im, sc1, ALU.subtract).then_inc(dve_setup, 1)
            ve.wait_ge(dve_setup, S.next())
            ve.tensor_tensor(f_im, f_im, den, ALU.mult).then_inc(f_ready, 1)

        S = counted(dve_start, 0)
        ve.memset(glog, -BIG).then_inc(dve_start, 1)
        ve.wait_ge(dve_start, S.next())
        ve.wait_ge(x_in, 16)
        ve.wait_ge(const_in, 16)
        norm_squares(0)
        norm_scale(0)
        S = counted(dve_setup, 0)
        setup_first(0, S, 7)
        norm_turned(0, turned("norm1"))
        setup_second(0, S)
        S.close()

        with ve.Fori(0, DEPTH) as l:
            L = counted(dve_layer, l)
            ve.tensor_copy(gain2, turned("norm2")).then_inc(dve_layer, 1)
            ve.wait_ge(dve_layer, L.next())
            ve.wait_ge(u_mm, at(u_mm, l, 1))
            ve.tensor_copy(uT[:, 2:4].rearrange("p q s -> p (q s)"), ps[:, 5]).then_inc(uT_dve, 1)
            ve.wait_ge(ct_mm, at(ct_mm, l, 1))
            for v, (b, sign) in enumerate(((2, 1.0), (2, -1.0), (3, -1.0))):
                ve.tensor_scalar(c_lhs[:, v].rearrange("p q s -> p (q s)"), ps[:, b], sign, None,
                                 ALU.mult).then_inc(c_ready, 1)

            def scan(k):
                half, q = divmod(k, 4)
                tiles = slice(4 * q, 4 * q + 4)
                b = 4 + 2 * (k % 2)
                ve.wait_ge(bu_done, at(bu_done, l, k + 1))
                cs, sn = (x[:, tiles, 0:HALF].rearrange("p (b j) t -> p b j t", b=2) for x in (cosT, sinT))
                re, im = (ps[:, b:b + 2, r * SEQ:(r + 1) * SEQ].rearrange("p b (j t) -> p b j t", j=2) for r in range(2))
                out4 = [pre[:, v].rearrange("p (b j) t -> p b j t", b=2) for v in range(4)]
                if k > 0:
                    ve.wait_ge(scanned, at(scanned, l, k))
                for o, x, table in ((0, re, cs), (1, im, sn), (2, im, cs), (3, re, sn)):
                    ve.tensor_tensor(out4[o], x, table, ALU.mult).then_inc(dve_layer, 1)
                    L.add()
                ve.wait_ge(dve_layer, L.value() - 2)
                ve.tensor_tensor(pre[:, 0], pre[:, 0], pre[:, 1], ALU.add).then_inc(dve_layer, 1)
                ve.wait_ge(dve_layer, L.next() - 1)
                ve.tensor_tensor(pre[:, 2], pre[:, 2], pre[:, 3], ALU.subtract).then_inc(dve_layer, 1)
                ve.wait_ge(dve_layer, L.next())
                if k > 0:
                    ve.wait_ge(rotated, at(rotated, l, 4 * k))
                if k > 0:
                    ve.wait_ge(carried, at(carried, l, min(k, 4)))
                for j in range(4):
                    for r in range(2):
                        first = 0.0 if half == 0 else carry[:, r, 4 * q + j:4 * q + j + 1]
                        ins = ve.tensor_tensor_scan(wst[:, r, j], decay[:, 4 * q + j:4 * q + j + 1].to_broadcast([P, HALF]),
                                                    pre[:, 2 * r, j], first, ALU.mult, ALU.add)
                ins.then_inc(scanned, 1)

            def skip(k):
                half, q = divmod(k, 4)
                ve.wait_ge(y_done, at(y_done, l, k + 1))
                if k > 0:
                    ve.wait_ge(z_ready, at(z_ready, l, k))
                ve.scalar_tensor_tensor(y1, uT[:, q, half * HALF:(half + 1) * HALF], turned("skip")[:, q:q + 1],
                                        ps[:, 4 + 2 * (k % 2), 0:P], ALU.mult, ALU.add).then_inc(y_ready, 1)

            def head_rms(w):
                ve.wait_ge(qk_sq, at(qk_sq, l, 2 * w + 2))
                ve.tensor_reduce(head_ss[:, 2 * w:2 * w + 2], squares.rearrange("p t (h d) -> p t h d", h=HEADS), AX.X,
                                 ALU.add).then_inc(qk_ss, 1)
                ve.wait_ge(qk_std, at(qk_std, l, w + 1))
                ve.reciprocal(head_ss[:, 2 * w:2 * w + 2], head_rs[:, 2 * w:2 * w + 2]).then_inc(qk_inv, 1)

            def softmax_in(b):
                ve.wait_ge(scored, at(scored, l, b + 1))
                if b > 0:
                    ve.wait_ge(pv_done, at(pv_done, l, b))
                bank = (0, 2, 0)[b]
                flat_ps = ps[:, bank:bank + 2].rearrange("p b n -> p (b n)")
                if b == 0:
                    v, w = (z.rearrange("p (s k) -> p s k", s=8) for z in (probs, flat_ps))
                    ve.tensor_tensor(v, w, wide(const("causal"), 1, [8, P]), ALU.add).then_inc(dve_layer, 1)
                    ve.wait_ge(dve_layer, L.next())
                    ve.tensor_reduce(row_max, v, AX.X, ALU.max).then_inc(dve_layer, 1)
                    ve.wait_ge(dve_layer, L.next())
                    n = 8
                else:
                    v, w = (z.rearrange("p (s c k) -> p s c k", s=4, c=2) for z in (probs, flat_ps))
                    ve.tensor_copy(v[:, :, 0], w[:, :, 0]).then_inc(dve_layer, 1)
                    ve.wait_ge(dve_layer, L.next())
                    ve.tensor_tensor(v[:, :, 1], w[:, :, 1], wide(const("causal"), 1, [4, P]), ALU.add).then_inc(dve_layer, 1)
                    ve.wait_ge(dve_layer, L.next())
                    ve.tensor_reduce(row_max[:, 0:4], probs.rearrange("p (s k) -> p s k", s=4), AX.X, ALU.max).then_inc(dve_layer, 1)
                    ve.wait_ge(dve_layer, L.next())
                    n = 4
                ve.tensor_scalar(row_max[:, 0:n], row_max[:, 0:n], -ATT_SCALE, None, ALU.mult).then_inc(maxed, 1)

            def attention_out(b):
                ve.wait_ge(pv_done, at(pv_done, l, b + 1))
                n = (8, 4, 4)[b]
                ve.reciprocal(row_inv[:, 0:n], row_sum[:, 0:n]).then_inc(dve_layer, 1)
                ve.wait_ge(dve_layer, L.next())
                dst = attn[:, (0, 1, 1)[b], (0, 0, 256)[b]:(512, 256, 512)[b]].rearrange("p (h d) -> p h d", h=n)
                ve.tensor_tensor(dst, ps[:, (0, 2, 0)[b], 0:n * HD].rearrange("p (h d) -> p h d", h=n),
                                 wide(row_inv[:, 0:n], 2, [n, HD]), ALU.mult).then_inc(o_ready, 1)

            def rope_k(t):
                if t == 0:
                    ve.wait_ge(k_raw, at(k_raw, l, 2))
                    ve.wait_ge(rope_ready, at(rope_ready, l, 1))
                    ve.wait_ge(qk_inv, at(qk_inv, l, 2))
                r3 = raw[:, 2 + t].rearrange("p (h d) -> p h d", h=HEADS)
                r4 = raw[:, 2 + t].rearrange("p (h f d) -> p h f d", h=HEADS, f=2)
                t3 = rope_tmp_k[:, 0].rearrange("p (h d) -> p h d", h=HEADS)
                t4 = rope_tmp_k[:, 1].rearrange("p (h f d) -> p h f d", h=HEADS, f=2)
                ve.tensor_tensor(r3, r3, wide(head_ss[:, 2 + t], 2, [HEADS, HD]), ALU.mult).then_inc(dve_layer, 1)
                ve.wait_ge(dve_layer, L.next())
                ve.tensor_tensor(t3, r3, wide(rope[:, 1, 0, t], 1, [HEADS, HD]), ALU.mult).then_inc(dve_layer, 1)
                ve.wait_ge(dve_layer, L.next())
                for f in range(2):
                    ve.tensor_tensor(t4[:, :, f], r4[:, :, 1 - f], wide(rope[:, 1, 1, t, 32 * f:32 * f + 32], 1, [HEADS, 32]), ALU.mult).then_inc(dve_layer, 1)
                    ve.wait_ge(dve_layer, L.next())
                ve.tensor_tensor(raw[:, 2 + t], rope_tmp_k[:, 0], rope_tmp_k[:, 1], ALU.add).then_inc(k_roped, 1)

            scan(0)
            scan(1)
            skip(0)
            head_rms(0)
            scan(2)
            skip(1)
            scan(3)
            skip(2)
            scan(4)
            head_rms(1)
            skip(3)
            rope_k(0)
            scan(5)
            skip(4)
            rope_k(1)
            scan(6)
            skip(5)
            scan(7)
            skip(6)
            softmax_in(0)
            skip(7)
            attention_out(0)
            softmax_in(1)
            attention_out(1)
            softmax_in(2)
            attention_out(2)

            for u in range(4):
                t, half = divmod(u, 2)
                if u < 3:
                    ve.wait_ge(ya_done, at(ya_done, l, u + 1))
                else:
                    ve.wait_ge(w_used, at(w_used, l, 14))
                ve.wait_ge(ga_tanh, at(ga_tanh, l, u + 1))
                ve.scalar_tensor_tensor(mix[:, t, 512 * half:512 * half + 512], att_gate[:, u], 1.0,
                                        ps[:, 5 + 2 * (u % 2)], ALU.add, ALU.mult).then_inc(mix_a, 1)
            for u in range(4):
                t, half = divmod(u, 2)
                m = mix[:, t, 512 * half:512 * half + 512]
                g0, g1 = gates[:, 0, u % 2], gates[:, 1, u % 2]
                ve.wait_ge(gate_tanh, at(gate_tanh, l, 2 * (u + 1)))
                ve.scalar_tensor_tensor(g1, g1, 1.0, ps[:, 4 * (u % 2) + 1], ALU.add, ALU.mult).then_inc(dve_layer, 1)
                ve.wait_ge(dve_layer, L.next())
                ve.scalar_tensor_tensor(g0, g0, 1.0, g1, ALU.add, ALU.mult).then_inc(dve_layer, 1)
                ve.wait_ge(dve_layer, L.next())
                ve.scalar_tensor_tensor(m, g0, 0.25, m, ALU.mult, ALU.add).then_inc(mixed, 1)
                if u == 2:
                    ve.wait_ge(mixT_mm, at(mixT_mm, l, 2))
                    ve.tensor_copy(hT[:, 4:8, 0:P], ps[:, 7].rearrange("p (c s) -> p c s", c=4)).then_inc(mixT_dve, 1)

            def residual(t):
                for half in range(2):
                    c = slice(512 * half, 512 * half + 512)
                    ve.scalar_tensor_tensor(xs[:, t, c], ps[:, 4 * t + half], 0.5, xs[:, t, c], ALU.mult,
                                            ALU.add).then_inc(x_mid, 1)

            S = counted(dve_setup, l + 1)
            setup_first(l + 1, S, 2)
            ve.wait_ge(wo_done, at(wo_done, l, 1))
            residual(0)
            ve.wait_ge(mixT_mm, at(mixT_mm, l, 4))
            ve.tensor_copy(hT[:, 4:8, P:2 * P], ps[:, 7].rearrange("p (c s) -> p c s", c=4)).then_inc(mixT_dve, 1)
            setup_second(l + 1, S)
            S.close()
            ve.wait_ge(w_used, at(w_used, l, FRONT_GROUPS))
            residual(1)
            ve.wait_ge(x_mid, at(x_mid, l, 4))
            norm_squares(l * 2 + 1)
            norm_scale(l * 2 + 1)
            norm_turned(l * 2 + 1, gain2)

            ve.wait_ge(logits_mm, at(logits_mm, l, 1))
            lg = ps[:, 0, 0:72].rearrange("p (t n) -> p t n", t=NT)
            ve.tensor_tensor(glog[:, :, 0:4], lg[:, :, 0:4], wide(router_b[:, 0:4], 1, [NT, 4]), ALU.add).then_inc(dve_layer, 1)
            ve.wait_ge(dve_layer, L.next())
            ve.tensor_tensor(elog, lg[:, :, 4:36], wide(router_b[:, 4:36], 1, [NT, EXPERTS]), ALU.add).then_inc(dve_layer, 1)
            ve.wait_ge(dve_layer, L.next())
            ve.sem_inc(settled, 1)
            for t in range(NT):
                ve.max(tops[:, 0, t], glog[:, t]).then_inc(dve_layer, 1)
                L.add()
            ve.wait_ge(dve_layer, L.value())
            ve.sem_inc(settled, 1)
            for t in range(NT):
                ve.max_index(tops_at[:, 0, t], tops[:, 0, t], glog[:, t]).then_inc(dve_layer, 1)
                L.add()
            ve.wait_ge(dve_layer, L.value())
            ve.tensor_scalar(rt[:, 0], tops[:, 0, :, 0], -1.0, None, ALU.mult).then_inc(group_max, 1)
            ve.tensor_copy(ids[:, 0], tops_at[:, 0, :, 0]).then_inc(dve_layer, 1)
            ve.wait_ge(dve_layer, L.next())
            for t in range(NT):
                ve.tensor_scalar(emask[:, t], const("egroup"), ids[:, 0, t:t + 1], None, ALU.is_equal).then_inc(dve_layer, 1)
                ve.wait_ge(dve_layer, L.next())
            ve.tensor_scalar(assign, emask, 1.0, BIG, ALU.subtract, ALU.mult).then_inc(dve_layer, 1)
            ve.wait_ge(dve_layer, L.next())
            ve.tensor_tensor(elog, elog, emask, ALU.mult).then_inc(dve_layer, 1)
            ve.wait_ge(dve_layer, L.next())
            ve.tensor_tensor(elog, elog, assign, ALU.add).then_inc(dve_layer, 1)
            ve.wait_ge(dve_layer, L.next())
            ve.sem_inc(settled, 1)
            for t in range(NT):
                ve.max(tops[:, 1, t], elog[:, t]).then_inc(dve_layer, 1)
                L.add()
            ve.wait_ge(dve_layer, L.value())
            ve.sem_inc(settled, 1)
            for t in range(NT):
                ve.max_index(tops_at[:, 1, t], tops[:, 1, t], elog[:, t]).then_inc(dve_layer, 1)
                L.add()
            ve.wait_ge(dve_layer, L.value())
            ve.tensor_tensor(rt[:, 1], tops[:, 1, :, 1], tops[:, 1, :, 0], ALU.subtract).then_inc(top_diff, 1)
            for a in range(2):
                ve.tensor_copy(ids[:, 1 + a], tops_at[:, 1, :, a]).then_inc(dve_layer, 1)
                ve.wait_ge(dve_layer, L.next())
            for a in range(2):
                for t in range(NT):
                    ve.tensor_scalar(onehot[:, a, t], const("expert"), ids[:, 1 + a, t:t + 1], None, ALU.is_equal).then_inc(dve_layer, 1)
                    ve.wait_ge(dve_layer, L.next())
            ve.tensor_tensor(assign, onehot[:, 0], onehot[:, 1], ALU.add).then_inc(assigned, 1)
            ve.wait_ge(assigned, at(assigned, l, 1))
            ve.wait_ge(group_exp, at(group_exp, l, 2))
            ve.reciprocal(rt[:, 3], rt[:, 2]).then_inc(dve_layer, 1)
            ve.wait_ge(dve_layer, L.next())
            ve.wait_ge(top_exp, at(top_exp, l, 1))
            ve.tensor_scalar(rt[:, 5], rt[:, 4], 1.0, None, ALU.add).then_inc(dve_layer, 1)
            ve.wait_ge(dve_layer, L.next())
            ve.reciprocal(rt[:, 5], rt[:, 5]).then_inc(dve_layer, 1)
            ve.wait_ge(dve_layer, L.next())
            ve.scalar_tensor_tensor(rt[:, 6], rt[:, 3], 0.5, rt[:, 5], ALU.mult, ALU.mult).then_inc(dve_layer, 1)
            ve.wait_ge(dve_layer, L.next())
            ve.tensor_tensor(rt[:, 7], rt[:, 6], rt[:, 4], ALU.mult).then_inc(dve_layer, 1)
            ve.wait_ge(dve_layer, L.next())
            for a in range(2):
                for t in range(NT):
                    ve.tensor_scalar(onehot[:, a, t], onehot[:, a, t], rt[:, 6 + a, t:t + 1], None, ALU.mult).then_inc(dve_layer, 1)
                    ve.wait_ge(dve_layer, L.next())
            ve.tensor_tensor(weight_of[:, :, 0:EXPERTS], onehot[:, 0], onehot[:, 1], ALU.add).then_inc(dve_layer, 1)
            ve.wait_ge(dve_layer, L.next())
            ve.memset(slot_of[:, :, EXPERTS:BLOCKS], -1.0).then_inc(dve_layer, 1)
            ve.wait_ge(dve_layer, L.next())
            ve.memset(weight_of[:, :, EXPERTS:BLOCKS], 0.0).then_inc(dve_layer, 1)
            ve.wait_ge(dve_layer, L.next())
            ve.wait_ge(pos_mm, at(pos_mm, l, 1))
            ve.scalar_tensor_tensor(slot_of[:, :, 0:EXPERTS], ps[:, 1, 0:64].rearrange("p (t n) -> p t n", t=NT), 1.0,
                                    assign, ALU.add, ALU.mult).then_inc(dve_layer, 1)
            ve.wait_ge(dve_layer, L.next())
            ve.tensor_scalar(slot_of[:, :, 0:EXPERTS], slot_of[:, :, 0:EXPERTS], 1.0, None, ALU.subtract).then_inc(dve_layer, 1)
            ve.wait_ge(dve_layer, L.next())
            ve.tensor_copy(count, ps[:, 1, 64:96]).then_inc(dve_layer, 1)
            ve.wait_ge(dve_layer, L.next())
            ve.tensor_reduce(rt[:, 0, 0:1], count, AX.X, ALU.max).then_inc(dve_layer, 1)
            ve.wait_ge(dve_layer, L.next())
            ve.tensor_copy(ov_flag, rt[:, 0, 0:1]).then_inc(routed, 1)

            def build_pick(S, i, b):
                ve.tensor_tensor(match, const("slot").unsqueeze(1).unsqueeze(1).to_broadcast([P, NT, 2, SLOTS]),
                                 wide(slot_of[:, :, bass.ds(b * 2, 2)], 3, [NT, 2, SLOTS]), ALU.is_equal).then_inc(S["match"], 1)
                ve.wait_ge(S["match"], at(S["match"], l, i + 1))
                if not isinstance(i, int):
                    ve.wait_ge(S["gathered"], at(S["gathered"], l, i))
                ve.tensor_tensor(pick, match.rearrange("p t e s -> p t (e s)"), wide(rstd, 2, [NT, P]),
                                 ALU.mult).then_inc(S["pick"], 1)

            def leave_gather(S, i):
                ve.wait_ge(S["gathered"], at(S["gathered"], l, i + 1))
                ve.tensor_tensor(xT, ps[:, 2:4].rearrange("p b (k s) -> p (b k) s", k=4), wide(gain2, 2, [KC, P]),
                                 ALU.mult).then_inc(S["xT"], 1)

            def pair(S, i, b, down_done):
                ve.tensor_tensor(back.rearrange("p t (e s) -> p t e s", e=2), match,
                                 wide(weight_of[:, :, bass.ds(b * 2, 2)], 3, [NT, 2, SLOTS]), ALU.mult).then_inc(S["back"], 1)
                ve.wait_ge(S["back"], at(S["back"], l, i + 1))
                build_pick(S, i + 1, b + 1)
                ve.wait_ge(S["tanh"], at(S["tanh"], l, i + 1))
                ve.scalar_tensor_tensor(act_buf, act_buf, 1.0, ps[:, 0], ALU.add, ALU.mult).then_inc(S["silu"], 1)
                ve.wait_ge(S["silu"], at(S["silu"], l, i + 1))
                ve.tensor_tensor(act_buf, act_buf, ps[:, 1], ALU.mult).then_inc(S["h"], 1)
                leave_gather(S, i + 1)
                ve.wait_ge(S["backT_mm"], at(S["backT_mm"], l, i + 1))
                ve.tensor_copy(backT.rearrange("p t s -> p (t s)"), ps[:, 1, 0:NT * P]).then_inc(S["backT"], 1)
                down_done()
                ve.tensor_copy(ybuf[:, 1], ps[:, 3]).then_inc(S["y1"], 1)

            build_pick(main, 0, 0)
            leave_gather(main, 0)
            with ve.Fori(0, PAIRS) as p:
                pair(main, p, p, lambda: ve.wait_ge(w_used, at(w_used, l, FRONT_GROUPS + p * RING + 12)))

            most = ve.value_load(ov_flag[0:1, 0:1], min_val=0, max_val=SEQ)
            with ve.If(most > SLOTS):
                Q = counted(dve_list, l)

                def by_round(z):
                    return z.rearrange("p (r e) -> p r e", r=EXTRA)

                ve.tensor_tensor(by_round(ov_on), wide(count, 1, [EXTRA, EXPERTS]), by_round(const("ov_limit")), ALU.is_gt).then_inc(dve_list, 1)
                ve.wait_ge(dve_list, Q.next())
                ve.tensor_tensor_scan(ov_cum, const("ones")[:, 0:NJ], ov_on, 0.0, ALU.mult, ALU.add).then_inc(dve_list, 1)
                ve.wait_ge(dve_list, Q.next())
                ve.tensor_tensor(ov_sel, wide(ov_cum, 1, [OV_BLOCKS, NJ]), wide(const("ov_block"), 2, [OV_BLOCKS, NJ]), ALU.is_equal).then_inc(dve_list, 1)
                ve.wait_ge(dve_list, Q.next())
                ve.tensor_tensor(ov_sel, ov_sel, wide(ov_on, 1, [OV_BLOCKS, NJ]), ALU.mult).then_inc(dve_list, 1)
                ve.wait_ge(dve_list, Q.next())
                ve.tensor_tensor(ov_tmp, ov_sel, wide(const("ov_expert"), 1, [OV_BLOCKS, NJ]), ALU.mult).then_inc(dve_list, 1)
                ve.wait_ge(dve_list, Q.next())
                ve.tensor_reduce(row_inv, ov_tmp, AX.X, ALU.add).then_inc(dve_list, 1)
                ve.wait_ge(dve_list, Q.next())
                ve.tensor_copy(ov_ids, row_inv).then_inc(ov_listed, 1)
                for t in range(NT):
                    ve.tensor_tensor(by_round(ov_v), wide(slot_of[:, t, 0:EXPERTS], 1, [EXTRA, EXPERTS]),
                                     by_round(const("ov_shift")), ALU.add).then_inc(dve_list, 1)
                    ve.wait_ge(dve_list, Q.next())
                    ve.tensor_tensor(ov_tmp, ov_sel, wide(ov_v, 1, [OV_BLOCKS, NJ]), ALU.mult).then_inc(dve_list, 1)
                    ve.wait_ge(dve_list, Q.next())
                    ve.tensor_reduce(slot_of[:, t, EXPERTS:EXPERTS + OV_BLOCKS], ov_tmp, AX.X, ALU.add).then_inc(dve_list, 1)
                    ve.wait_ge(dve_list, Q.next())
                    for r in range(EXTRA):
                        e = slice(r * EXPERTS, (r + 1) * EXPERTS)
                        ve.tensor_tensor(ov_tmp[:, :, e], ov_sel[:, :, e], wide(weight_of[:, t, 0:EXPERTS], 1, [OV_BLOCKS, EXPERTS]), ALU.mult).then_inc(dve_list, 1)
                        ve.wait_ge(dve_list, Q.next())
                    ve.tensor_reduce(weight_of[:, t, EXPERTS:EXPERTS + OV_BLOCKS], ov_tmp, AX.X, ALU.add).then_inc(dve_list, 1)
                    ve.wait_ge(dve_list, Q.next())
                ve.tensor_scalar(slot_of[:, :, EXPERTS:EXPERTS + OV_BLOCKS], slot_of[:, :, EXPERTS:EXPERTS + OV_BLOCKS],
                                 1.0, None, ALU.subtract).then_inc(dve_list, 1)
                ve.wait_ge(dve_list, Q.next())
                Q.close()
                ve.wait_ge(main["gathered"], at(main["gathered"], l, PAIRS + 1))
                build_pick(over, 0, PAIRS)
                leave_gather(over, 0)
                with ve.Fori(0, OV_PAIRS) as i:
                    pair(over, i, i + PAIRS, lambda: ve.wait_ge(ov_used, at(ov_used, l, i * RING + 12)))
            with ve.Else():
                for s in [dve_list, ov_listed] + [over[n] for n in ("match", "pick", "xT", "back", "silu", "h", "backT", "y1")]:
                    ve.sem_inc(s, per[s.name])
            ve.nop()
            ve.wait_ge(main["scattered"], at(main["scattered"], l, PAIRS))
            ve.wait_ge(over["scattered"], at(over["scattered"], l, OV_PAIRS))
            for t in range(NT):
                for half in range(2):
                    c = slice(512 * half, 512 * half + 512)
                    ve.tensor_tensor(xs[:, t, c], ps[:, 4 + 2 * t + half], xs[:, t, c], ALU.add).then_inc(x_new, 1)
            L.close()
            ve.wait_ge(x_new, at(x_new, l, 4))
            norm_squares(l * 2 + 2)
            norm_scale(l * 2 + 2)
            norm_turned(l * 2 + 2, turned("norm1"))

    @block.gpsimd
    def _(pool):
        def setup(n):
            pool.wait_ge(setup_in, at(setup_in, n, per[setup_in.name]))
            S = counted(pool_setup, n)
            for r in range(2):
                pool.tensor_tensor(c_exp[:, r], wide(c_raw[:, r], 2, [QUADS, 2, NSTATE]),
                                   const("gside").unsqueeze(1).unsqueeze(3).to_broadcast([P, QUADS, 2, NSTATE]),
                                   ALU.mult).then_inc(expanded, 1)
            pool.wait_ge(f_ready, at(f_ready, n, 1))
            for v, (f, r) in enumerate(((f_re, 0), (f_im, 1), (f_re, 1), (f_im, 0))):
                pool.tensor_tensor(b_tmp[:, v], b_raw[:, r], wide(f, 2, [TILES, GCH]), ALU.mult).then_inc(pool_setup, 1)
                pool.wait_ge(pool_setup, S.next())
            pool.tensor_tensor(b_tmp[:, 0], b_tmp[:, 0], b_tmp[:, 1], ALU.subtract).then_inc(pool_setup, 1)
            pool.wait_ge(pool_setup, S.next())
            pool.tensor_tensor(b_tmp[:, 2], b_tmp[:, 2], b_tmp[:, 3], ALU.add).then_inc(pool_setup, 1)
            pool.wait_ge(pool_setup, S.next())
            for r in range(2):
                pool.tensor_tensor(b_exp[:, r], wide(b_tmp[:, 2 * r], 2, [TILES, 2, GCH]),
                                   const("side").unsqueeze(1).unsqueeze(3).to_broadcast([P, TILES, 2, GCH]),
                                   ALU.mult).then_inc(expanded, 1)
            S.close()

        pool.wait_ge(const_in, 16)
        setup(0)
        with pool.Fori(0, DEPTH) as l:
            L = counted(pool_layer, l)
            pool.wait_ge(layer_in, at(layer_in, l, per[layer_in.name]))
            ra, rb = (const(n).rearrange("p (t d) -> p t d", t=NT) for n in ("rope_a", "rope_b"))
            for w in range(2):
                pool.tensor_tensor(rope[:, w, 0], ra, wide(qk_gain[:, w], 1, [NT, HD]), ALU.mult).then_inc(pool_layer, 1)
                pool.wait_ge(pool_layer, L.next())
                for f in range(2):
                    ins = pool.tensor_tensor(rope[:, w, 1, :, 32 * f:32 * f + 32], rb[:, :, 32 * f:32 * f + 32],
                                             wide(qk_gain[:, w, 32 - 32 * f:64 - 32 * f], 1, [NT, 32]), ALU.mult)
                    if w and f:
                        ins.then_inc(rope_ready, 1)
                    else:
                        ins.then_inc(pool_layer, 1)
                        pool.wait_ge(pool_layer, L.next())
            pool.wait_ge(rope_ready, at(rope_ready, l, 1))

            def rotate(k):
                half, q = divmod(k, 4)
                tiles = slice(4 * q, 4 * q + 4)
                pool.wait_ge(scanned, at(scanned, l, k + 1))
                if k > 0:
                    pool.wait_ge(y_done, at(y_done, l, k))
                for v, (table, r) in enumerate(((cosT, 0), (sinT, 1), (sinT, 0), (cosT, 1))):
                    pool.tensor_tensor(post[:, v], wst[:, r], table[:, tiles, 0:HALF], ALU.mult).then_inc(rotated, 1)
                if half == 0:
                    last = [wst[:, r, :, HALF - 1] for r in range(2)]
                    cs, sn = cosT[:, tiles, HALF], sinT[:, tiles, HALF]
                    c = [carry[:, n, tiles] for n in range(4)]
                    pool.tensor_tensor(c[0], last[0], cs, ALU.mult).then_inc(pool_layer, 1)
                    pool.wait_ge(pool_layer, L.next())
                    pool.tensor_tensor(c[2], last[1], sn, ALU.mult).then_inc(pool_layer, 1)
                    pool.wait_ge(pool_layer, L.next())
                    pool.tensor_tensor(c[1], last[1], cs, ALU.mult).then_inc(pool_layer, 1)
                    pool.wait_ge(pool_layer, L.next())
                    pool.tensor_tensor(c[3], last[0], sn, ALU.mult).then_inc(pool_layer, 1)
                    pool.wait_ge(pool_layer, L.next())
                    pool.tensor_tensor(c[0], c[0], c[2], ALU.subtract).then_inc(pool_layer, 1)
                    pool.wait_ge(pool_layer, L.next())
                    pool.tensor_tensor(c[1], c[1], c[3], ALU.add).then_inc(carried, 1)

            def gelu(k):
                half, q = divmod(k, 4)
                pool.wait_ge(y_ready, at(y_ready, l, k + 1))
                pool.tensor_tensor(y2, y1, y1, ALU.mult).then_inc(pool_layer, 1)
                pool.wait_ge(pool_layer, L.next())
                pool.sem_inc(settled, 1)
                pool.tensor_scalar(y2, y2, 0.044715, 1.0, ALU.mult, ALU.add).then_inc(pool_layer, 1)
                pool.wait_ge(pool_layer, L.next())
                pool.tensor_tensor(y3, y2, y1, ALU.mult).then_inc(gelu_in, 1)
                pool.wait_ge(gelu_tanh, at(gelu_tanh, l, k + 1))
                pool.sem_inc(settled, 1)
                pool.tensor_scalar(y2, y2, 1.0, 1.0, ALU.mult, ALU.add).then_inc(pool_layer, 1)
                pool.wait_ge(pool_layer, L.next())
                pool.tensor_tensor(uT[:, q, half * HALF:(half + 1) * HALF], y2, y1, ALU.mult).then_inc(z_ready, 1)

            def rope_q(t):
                if t == 0:
                    pool.wait_ge(q_raw, at(q_raw, l, 2))
                    pool.wait_ge(qk_inv, at(qk_inv, l, 1))
                r3 = raw[:, t].rearrange("p (h d) -> p h d", h=HEADS)
                r4 = raw[:, t].rearrange("p (h f d) -> p h f d", h=HEADS, f=2)
                t3 = rope_tmp[:, 0].rearrange("p (h d) -> p h d", h=HEADS)
                t4 = rope_tmp[:, 1].rearrange("p (h f d) -> p h f d", h=HEADS, f=2)
                pool.tensor_tensor(r3, r3, wide(head_ss[:, t], 2, [HEADS, HD]), ALU.mult).then_inc(pool_layer, 1)
                pool.wait_ge(pool_layer, L.next())
                pool.tensor_tensor(t3, r3, wide(rope[:, 0, 0, t], 1, [HEADS, HD]), ALU.mult).then_inc(pool_layer, 1)
                pool.wait_ge(pool_layer, L.next())
                for f in range(2):
                    pool.tensor_tensor(t4[:, :, f], r4[:, :, 1 - f], wide(rope[:, 0, 1, t, 32 * f:32 * f + 32], 1, [HEADS, 32]), ALU.mult).then_inc(pool_layer, 1)
                    pool.wait_ge(pool_layer, L.next())
                pool.tensor_tensor(raw[:, t], rope_tmp[:, 0], rope_tmp[:, 1], ALU.add).then_inc(q_roped, 1)
                pool.wait_ge(q_roped, at(q_roped, l, t + 1))

            rotate(0)
            for k in range(1, 8):
                rotate(k)
                gelu(k - 1)
                if k in (2, 4):
                    rope_q(k // 2 - 1)
            gelu(7)
            L.close()
            pool.wait_ge(mixed, at(mixed, l, 4))
            setup(l + 1)

    ctx.close()


_INS = ["x", "norm1_g", "w_in", "ssm_a_re", "ssm_a_im", "ssm_log_dt", "ssm_b_re", "ssm_b_im", "ssm_c_re", "ssm_c_im",
        "ssm_d", "w_glu", "q_norm_g", "k_norm_g", "w_attn", "w_out", "norm2_g", "router_w_group", "router_b_group",
        "router_w_expert", "router_b_expert", "w_gate_up", "w_down"]


def kernel(**inputs):
    import numpy as _np
    import concourse.bacc as _bacc
    from concourse import mybir as _mybir
    from concourse.bass_utils import run_bass_kernel_spmd as _run

    nc = _bacc.Bacc("TRN2", target_bir_lowering=False, num_devices=1)
    arrays, args = {}, []
    for name in _INS:
        a = _np.ascontiguousarray(inputs[name])
        arrays[f"in_{name}_dram"] = a
        args.append(nc.dram_tensor(f"in_{name}_dram", a.shape, _mybir.dt.from_np(a.dtype), kind="ExternalInput").ap())
    c = constants()
    arrays["shape_constants"] = c
    args.append(nc.dram_tensor("shape_constants", c.shape, _mybir.dt.float32, kind="ExternalInput").ap())
    args.append(nc.dram_tensor("out_dram", (1, SEQ, D), _mybir.dt.float32, kind="ExternalOutput").ap())
    trunk(nc, *args)
    r = _run(nc, [arrays], core_ids=[0])
    return r.results[0]["out_dram"]
```

```python
import math
from contextlib import ExitStack

import numpy as np

import concourse.bass as bass
from concourse import mybir

F32 = mybir.dt.float32
I32 = mybir.dt.int32
U32 = mybir.dt.uint32
ALU = mybir.AluOpType
ACT = mybir.ActivationFunctionType
AX = mybir.AxisListType

P = 128
DEPTH = 2
D = 1024
SEQ = 256
NT = SEQ // P
KC = D // P
HEADS, HD = 8, 64
GROUPS, GCH, NSTATE = 32, 16, 64
TILES = GROUPS * NSTATE // P
QUADS = TILES // 4
HALF = SEQ // 2
TW = HALF + 1
EXPERTS, EGROUPS, EPG = 32, 4, 8
FF = 512
SLOTS = 64
PAIRS = EXPERTS // 2
OV_BLOCKS = 8
OV_PAIRS = OV_BLOCKS // 2
BLOCKS = EXPERTS + OV_BLOCKS + 2
EXTRA = SEQ // SLOTS - 1
RING = 12
FRONT_GROUPS = 26
EARLY = 3
LAYER_GROUPS = FRONT_GROUPS + RING * PAIRS
EPS = 1e-6
BIG = 3.0e38
ROUND = 1.5 * 2.0 ** 23
ROUND15 = 1.5 * 2.0 ** 8
TWO_PI = 6.2831850
LOG2_E = 1.4426950408889634
LN2_HIGH = 0.693359375
LN2_LOW = 0.6931471805599453 - LN2_HIGH
GELU_C = 0.7978845608028654
ATT_SCALE = HD ** -0.5

CONST = {}
_at = 0
for _name, _n in (("ident", P), ("before", P), ("ones", P), ("causal", P), ("zero", P), ("rope_a", NT * HD),
                  ("rope_b", NT * HD), ("slot", SLOTS), ("expert", EXPERTS), ("egroup", EXPERTS),
                  ("step", TW), ("ov_expert", EXTRA * EXPERTS), ("ov_shift", EXTRA * EXPERTS),
                  ("ov_limit", EXTRA * EXPERTS), ("ov_block", OV_BLOCKS), ("side", 2), ("gside", 2),
                  ("odd_tile", 2), ("eps", 1)):
    CONST[_name] = (_at, _at + _n)
    _at += _n
N_CONST = _at

VEC = {"norm1": (0, 8), "norm2": (8, 16), "skip": (16, 20), "a_re": (20, 36), "a_im": (36, 52)}
N_VEC = 52


def constants():
    c = np.zeros((P, N_CONST), np.float32)

    def put(name, value):
        a, b = CONST[name]
        c[:, a:b] = value

    row = np.arange(P)[:, None]
    col = np.arange(P)[None, :]
    put("ident", row == col)
    put("before", row < col)
    put("ones", 1.0)
    put("causal", np.where(col <= row, 0.0, -1e30))
    inv = (np.float32(10000.0) ** (-np.arange(0, HD, 2, dtype=np.float32) / np.float32(HD))).astype(np.float32)
    ang = np.arange(SEQ, dtype=np.float32)[:, None] * inv[None, :]
    cos, sin = np.cos(ang).astype(np.float32), np.sin(ang).astype(np.float32)
    a = np.concatenate([cos, cos], 1).reshape(NT, P, HD).transpose(1, 0, 2).reshape(P, -1)
    b = np.concatenate([-sin, sin], 1).reshape(NT, P, HD).transpose(1, 0, 2).reshape(P, -1)
    put("rope_a", a)
    put("rope_b", b)
    put("slot", np.arange(SLOTS))
    put("expert", np.arange(EXPERTS))
    put("egroup", np.arange(EXPERTS) // EPG)
    put("step", np.arange(TW))
    r = np.arange(EXTRA * EXPERTS) // EXPERTS
    put("ov_expert", np.arange(EXTRA * EXPERTS) % EXPERTS)
    put("ov_shift", 1.0 - SLOTS * (r + 1))
    put("ov_limit", SLOTS * (r + 1))
    put("ov_block", np.arange(OV_BLOCKS) + 1)
    put("side", (row // NSTATE) == np.arange(2)[None, :])
    put("gside", (row // GCH) % 2 == np.arange(2)[None, :])
    put("odd_tile", (row // (2 * GCH)) % 2 == np.arange(2)[None, :])
    put("eps", EPS)
    return c


class Counted:

    def __init__(self, start, per):
        self.start, self.per, self.n = start, per, 0

    def add(self):
        self.n += 1

    def value(self):
        return self.start + self.n

    def next(self):
        self.add()
        return self.value()

    def close(self):
        assert self.n == self.per, (self.n, self.per)


def trunk(nc, x, norm1_g, w_in, ssm_a_re, ssm_a_im, ssm_log_dt, ssm_b_re, ssm_b_im, ssm_c_re, ssm_c_im,
          ssm_d, w_glu, q_norm_g, k_norm_g, w_attn, w_out, norm2_g, router_w_group, router_b_group,
          router_w_expert, router_b_expert, w_gate_up, w_down, consts, out):
    ctx = ExitStack()

    def sb(name, cols, dt=F32):
        return ctx.enter_context(nc.sbuf_tensor(name, [P, cols], dt))[:]

    per, ahead = {}, {}

    def signal(name, times=1, start=0):
        sem = ctx.enter_context(nc.semaphore(name))
        per[sem.name], ahead[sem.name] = times, start
        return sem

    def at(sem, rnd, k):
        return rnd * per[sem.name] + k + ahead[sem.name]

    def counted(sem, rnd):
        return Counted(at(sem, rnd, 0), per[sem.name])

    ps = ctx.enter_context(nc.psum_tensor("ps", [P, 8, 512], F32))[:]

    ring = sb("ring", RING * 2 * D).rearrange("p (g c n) -> p g c n", g=RING, c=2)
    xs = sb("xs", NT * D).rearrange("p (t d) -> p t d", t=NT)
    hT_all = sb("hT", KC * SEQ)
    hT = hT_all.rearrange("p (k s) -> p k s", k=KC)
    cosT = sb("cosT", TILES * TW).rearrange("p (i t) -> p i t", i=TILES)
    sinT = sb("sinT", TILES * TW).rearrange("p (i t) -> p i t", i=TILES)
    b_lhs = sb("b_lhs", 2 * 2 * QUADS * P).rearrange("p (r o q s) -> p r o q s", r=2, o=2, q=QUADS)
    c_lhs = sb("c_lhs", 3 * QUADS * P).rearrange("p (v q s) -> p v q s", v=3, q=QUADS)
    cst = sb("cst", N_CONST)
    vec = sb("vec", N_VEC)
    rows = sb("rows", P)
    log_dt = sb("log_dt", GROUPS)
    diag = sb("diag", NT * P).rearrange("p (t s) -> p t s", t=NT)
    rope = sb("rope", 2 * 2 * NT * HD).rearrange("p (w f t d) -> p w f t d", w=2, f=2, t=NT)
    router_w = sb("router_w", KC * 36).rearrange("p (k n) -> p k n", k=KC)
    router_b = sb("router_b", 36)
    qk_gain = sb("qk_gain", 2 * HD).rearrange("p (w d) -> p w d", w=2)
    ov_flag = sb("ov_flag", 1, I32)
    ov_ids = sb("ov_ids", OV_BLOCKS, I32)
    tops = sb("tops", 4 * 8).rearrange("p (a t n) -> p a t n", a=2, t=NT)
    tops_at = sb("tops_at", 4 * 8, U32).rearrange("p (a t n) -> p a t n", a=2, t=NT)

    (decay, dt_, theta, turns_hi, turns_lo, den, f_re, f_im, a_bar_re, a_bar_im, sc0, sc1) = (
        sb(n, TILES) for n in ("decay", "dt", "theta", "turns_hi", "turns_lo", "den", "f_re", "f_im",
                               "a_bar_re", "a_bar_im", "sc0", "sc1"))
    carry = sb("carry", 4 * TILES).rearrange("p (r i) -> p r i", r=4)
    gain2 = sb("gain2", KC)
    ssq, std, rstd = (sb(n, NT) for n in ("ssq", "std", "rstd"))
    head_ss = sb("head_ss", 4 * HEADS).rearrange("p (n h) -> p n h", n=4)
    head_rs = sb("head_rs", 4 * HEADS).rearrange("p (n h) -> p n h", n=4)
    row_max, row_sum, row_inv = (sb(n, HEADS) for n in ("row_max", "row_sum", "row_inv"))
    glog = sb("glog", NT * 8).rearrange("p (t n) -> p t n", t=NT)
    elog = sb("elog", NT * EXPERTS).rearrange("p (t n) -> p t n", t=NT)
    emask = sb("emask", NT * EXPERTS).rearrange("p (t n) -> p t n", t=NT)
    assign = sb("assign", NT * EXPERTS).rearrange("p (t n) -> p t n", t=NT)
    onehot = sb("onehot", 2 * NT * EXPERTS).rearrange("p (a t n) -> p a t n", a=2, t=NT)
    ids = sb("ids", 3 * NT).rearrange("p (a t) -> p a t", a=3)
    rt = sb("rt", 8 * NT).rearrange("p (a t) -> p a t", a=8)
    count = sb("count", EXPERTS)
    slot_of = sb("slot_of", NT * BLOCKS).rearrange("p (t b) -> p t b", t=NT)
    weight_of = sb("weight_of", NT * BLOCKS).rearrange("p (t b) -> p t b", t=NT)

    def const(name):
        a, b = CONST[name]
        return cst[:, a:b]

    def turned(name):
        a, b = VEC[name]
        return vec[:, a:b]

    PHASE = 12672
    phase = sb("phase", PHASE)
    uT = phase[:, 0:1024].rearrange("p (q s) -> p q s", q=QUADS)
    raw = phase[:, 1024:3072].rearrange("p (n c) -> p n c", n=4)
    mix = phase[:, 1024:3072].rearrange("p (t d) -> p t d", t=NT)
    rope_tmp = phase[:, 3072:4096].rearrange("p (w n) -> p w n", w=2)
    rope_tmp_k = phase[:, 6144:7168].rearrange("p (w n) -> p w n", w=2)
    attn = rope_tmp
    squares = phase[:, 4096:5120].rearrange("p (t n) -> p t n", t=NT)
    vtok = phase[:, 4096:5120].rearrange("p (t n) -> p t n", t=NT)
    qT = phase[:, 5120:6144].rearrange("p (c s) -> p c s", c=4)
    oT = qT
    kT = phase[:, 6144:7168].rearrange("p (c s) -> p c s", c=4)
    probs = phase[:, 1024:2048]
    pre = phase[:, 7168:9216].rearrange("p (v i t) -> p v i t", v=4, i=4)
    wst = phase[:, 9216:10240].rearrange("p (v i t) -> p v i t", v=2, i=4)
    post = phase[:, 10240:12288].rearrange("p (v i t) -> p v i t", v=4, i=4)
    y1, y2, y3 = (phase[:, 12288 + 128 * n:12416 + 128 * n] for n in range(3))
    att_gate = phase[:, 7168:9216].rearrange("p (u n) -> p u n", u=4)
    gates = phase[:, 9216:11264].rearrange("p (w u n) -> p w u n", w=2, u=2)
    junk = phase[:, 0:2048].rearrange("p (t d) -> p t d", t=NT)
    rms_inv = phase[:, 2048:2304]
    turn_a = phase[:, 4096:6160].rearrange("p (h i t) -> p h i t", h=2, i=8)
    turn_b = phase[:, 6160:8224].rearrange("p (h i t) -> p h i t", h=2, i=8)
    b_tmp = phase[:, 8224:9248].rearrange("p (v i h) -> p v i h", v=4, i=TILES)
    b_exp = phase[:, 9248:10272].rearrange("p (r i g h) -> p r i g h", r=2, i=TILES, g=2)
    c_exp = phase[:, 10272:11296].rearrange("p (r q g s) -> p r q g s", r=2, q=QUADS, g=2)
    b_raw = phase[:, 11296:11808].rearrange("p (r i h) -> p r i h", r=2, i=TILES)
    c_raw = phase[:, 11808:12320].rearrange("p (r q s) -> p r q s", r=2, q=QUADS)
    early = [z.rearrange("p (c n) -> p c n", c=2) for z in (phase[:, 4096:6144], phase[:, 6144:8192], hT_all)]
    exp_tmp = phase[:, 12320:12448].rearrange("p (m n) -> p m n", m=4)
    one = phase[:, 12448:12496].rearrange("p (m n) -> p m n", m=3)
    xT = phase[:, 0:1024].rearrange("p (k s) -> p k s", k=KC)
    pick = phase[:, 1024:1280].rearrange("p (t s) -> p t s", t=NT)
    back = phase[:, 1280:1536].rearrange("p (t s) -> p t s", t=NT)
    match = phase[:, 1536:1792].rearrange("p (t e s) -> p t e s", t=NT, e=2)
    backT = phase[:, 1792:2048].rearrange("p (t s) -> p t s", t=NT)
    act_buf = phase[:, 2048:2560]
    ffT = phase[:, 2560:3072].rearrange("p (c s) -> p c s", c=4)
    ybuf = phase[:, 3072:4096].rearrange("p (h n) -> p h n", h=2)
    ov_sel = phase[:, 4096:4864].rearrange("p (b j) -> p b j", b=OV_BLOCKS)
    ov_tmp = phase[:, 4864:5632].rearrange("p (b j) -> p b j", b=OV_BLOCKS)
    NJ = EXTRA * EXPERTS
    ov_on, ov_cum, ov_v = (phase[:, 5632 + NJ * n:5632 + NJ * (n + 1)] for n in range(3))

    const_in, x_in = signal("const_in", 16), signal("x_in", 16)
    layer_in = signal("layer_in", 6 * 16)
    setup_in = signal("setup_in", 10 * 16)
    mixer_loads = [3 if g < 2 else 2 for g in range(RING)]
    landed = [signal(f"landed{g}", 16 * (mixer_loads[g] + PAIRS - (g < EARLY))) for g in range(RING)]
    early_in = [signal(f"early_in{g}", 16) for g in range(EARLY)]
    ov_landed = signal("ov_landed", 16 * RING * OV_PAIRS)
    w_used = signal("w_used", LAYER_GROUPS, RING)
    ov_used = signal("ov_used", RING * OV_PAIRS, 1)
    stored = signal("stored", 64)
    ssq_act, ssq_dve, std_ready, rstd_ready = (signal(n) for n in ("ssq_act", "ssq_dve", "std_ready", "rstd_ready"))
    x_turned, x_act, x_dve, router_ready = signal("x_turned", 4), signal("x_act", 2), signal("x_dve", 2), signal("router_ready")
    mid_sq, mid_std, mid_rstd = signal("mid_sq", 2), signal("mid_std"), signal("mid_rstd")
    diag_ready, hT_mm, spread_mm, spread, hT_ready = signal("diag_ready", 2), signal("hT_mm"), signal("spread_mm"), signal("spread"), signal("hT_ready", 8)
    u_mm, uT_act, uT_dve, k_mm = (signal(n) for n in ("u_mm", "uT_act", "uT_dve", "k_mm"))
    q_raw, k_raw, v_raw = (signal(n, 2) for n in ("q_raw", "k_raw", "v_raw"))
    rope_ready, qk_sq, qk_ss, qk_std = signal("rope_ready"), signal("qk_sq", 4), signal("qk_ss", 2), signal("qk_std", 2)
    qk_inv = signal("qk_inv", 2)
    q_roped, k_roped = signal("q_roped", 2), signal("k_roped", 2)
    qk_turned, qT_ready, kT_ready = signal("qk_turned", 2), signal("qT_ready", 2), signal("kT_ready", 2)
    scored, maxed, exped = signal("scored", 3), signal("maxed", 3), signal("exped", 16)
    p_turned, pT_ready, pv_done, o_ready = signal("p_turned", 3), signal("pT_ready", 6), signal("pv_done", 3), signal("o_ready", 3)
    o_turned, oT_ready = signal("o_turned"), signal("oT_ready", 2)
    bu_done, scanned, rotated, carried = signal("bu_done", 8), signal("scanned", 8), signal("rotated", 32), signal("carried", 4)
    y_done, y_ready, gelu_in, gelu_tanh, z_ready = (signal(n, 8) for n in ("y_done", "y_ready", "gelu_in", "gelu_tanh", "z_ready"))
    ga_done, ya_done, ga_tanh, mix_a = signal("ga_done", 3), signal("ya_done", 3), signal("ga_tanh", 4), signal("mix_a", 4)
    gs_done, glu_done, gate_tanh, mixed = signal("gs_done", 3), signal("glu_done", 3), signal("gate_tanh", 8), signal("mixed", 4)
    mixT_mm, mixT_act, mixT_dve = signal("mixT_mm", 4), signal("mixT_act", 2), signal("mixT_dve", 2)
    wo_done, x_mid, x_new = signal("wo_done", 1), signal("x_mid", 4), signal("x_new", 4)
    vec_mm, vec_ready = signal("vec_mm"), signal("vec_ready")
    turn_ready, one_ready, turns_ready, tables_ready = signal("turn_ready"), signal("one_ready", 2), signal("turns_ready", 2), signal("tables_ready")
    sin_ready, half_sine, half_ready = signal("sin_ready", 2), signal("half_sine", 2), signal("half_ready", 2)
    f_ready, expanded = signal("f_ready"), signal("expanded", 4)
    bt_mm, ct_mm, b_ready, c_ready = signal("bt_mm"), signal("ct_mm"), signal("b_ready", 4), signal("c_ready", 3)
    logits_mm, group_max, group_exp, top_diff, top_exp = (signal(n, k) for n, k in (
        ("logits_mm", 1), ("group_max", 1), ("group_exp", 2), ("top_diff", 1), ("top_exp", 1)))
    assigned, pos_mm, routed, ov_listed = signal("assigned"), signal("pos_mm"), signal("routed"), signal("ov_listed")
    dve_start, dve_layer, dve_setup, dve_list = signal("dve_start", 2), signal("dve_layer", 116), signal("dve_setup", 66), signal("dve_list", 21)
    settled = signal("settled")
    pool_layer, pool_setup = signal("pool_layer", 57), signal("pool_setup", 6)

    def pair_signals(prefix, pairs, used):
        s = {"pairs": pairs, "used": used}
        for n in ("match", "pick", "gathered", "xT"):
            s[n] = signal(prefix + n, pairs + 1)
        for n in ("back", "tanh", "silu", "h", "ffT_mm", "backT_mm", "ffT", "backT", "y0_mm", "y0", "y1", "scattered"):
            s[n] = signal(prefix + n, pairs)
        return s

    main, over = pair_signals("m_", PAIRS, w_used), pair_signals("ov_", OV_PAIRS, ov_used)

    def wide(ap, axis, shape):
        return ap.unsqueeze(axis).to_broadcast([P] + list(shape))

    win_d = w_in.rearrange("l (k p) n -> l p k n", p=P)
    wattn_d = w_attn.rearrange("l (k p) n -> l p k n", p=P)
    wglu_d = w_glu.rearrange("l (k p) (c n) -> l p k c n", p=P, c=2)
    wout_d = w_out.rearrange("l (k p) n -> l p k n", p=P)
    wgu_d = w_gate_up.rearrange("l e (k p) n -> (l e) p k n", p=P)
    wdn_d = w_down.rearrange("l e (k p) n -> (l e) p k n", p=P)

    U0, V0, GS, GA = 0, D, 2 * D, 3 * D
    front = []
    for j in range(4):
        front.append((j, lambda l, j=j: win_d[bass.ds(l, 1), :, 2 * j:2 * j + 2, U0:U0 + D]))
    for j in range(4):
        front.append((4 + j, lambda l, j=j: win_d[bass.ds(l, 1), :, 2 * j:2 * j + 2, V0:V0 + D]))
    for j in range(4):
        front.append((8 + j, lambda l, j=j: win_d[bass.ds(l, 1), :, 2 * j:2 * j + 2, GA:GA + D]))
    for j in range(2):
        front.append((j, lambda l, j=j: wattn_d[bass.ds(l, 1), :, 2 * j:2 * j + 2, :]))
    for j in range(4):
        front.append((2 + j, lambda l, j=j: win_d[bass.ds(l, 1), :, 2 * j:2 * j + 2, GS:GS + D]))
    for j in range(4):
        front.append((6 + j, lambda l, j=j: wglu_d[bass.ds(l, 1), :, j, :, :]))
    for j in range(4):
        front.append(((10 + j) % RING, lambda l, j=j: wout_d[bass.ds(l, 1), :, 2 * j:2 * j + 2, :]))
    assert len(front) == FRONT_GROUPS

    def pair_group(g):
        return (g % 2, False, g // 2) if g < 8 else (g % 2, True, (g - 8) // 2)

    def flat(ap, pattern="o p c n -> (o p) c n"):
        return ap.rearrange(pattern)

    def load_expert_group(sp, g, index, place, landing):
        _, down, j = pair_group(g)
        src = (wdn_d if down else wgu_d)[bass.ds(index, 1), :, 2 * j:2 * j + 2, :]
        sp.dma_start(place, flat(src)).then_inc(landing, 16)

    block = ctx.enter_context(nc.Block())

    @block.sync
    def _(sp):
        sp.dma_start(xs, x.rearrange("o (t p) d -> p (o t) d", p=P)).then_inc(x_in, 16)
        sp.dma_start(cst, consts).then_inc(const_in, 16)
        with sp.Fori(0, DEPTH) as l:
            for n, (g, src) in enumerate(front):
                sp.wait_ge(w_used, at(w_used, l, n + 1 - RING))
                sp.dma_start(ring[:, g], flat(src(l))).then_inc(landed[g], 16)
            for g in range(EARLY, RING):
                sp.wait_ge(w_used, at(w_used, l, RING + g + 1))
                sp.sem_inc(settled, 1)
                load_expert_group(sp, g, l * EXPERTS + g % 2, ring[:, g], landed[g])
            for g in range(EARLY):
                if g == 0:
                    sp.wait_ge(tables_ready, at(tables_ready, l + 1, 1))
                if g == 2:
                    sp.wait_ge(logits_mm, at(logits_mm, l, 1))
                sp.sem_inc(settled, 1)
                load_expert_group(sp, g, l * EXPERTS + g % 2, early[g], early_in[g])
            for g in range(RING):
                if g < 2:
                    sp.wait_ge(w_used, at(w_used, l, 2 * RING + g + 1))
                elif g >= EARLY:
                    sp.wait_ge(w_used, at(w_used, l, FRONT_GROUPS + g + 1))
                sp.sem_inc(settled, 1)
                load_expert_group(sp, g, l * EXPERTS + 2 + g % 2, ring[:, g], landed[g])
            with sp.Fori(2, PAIRS) as p:
                for g in range(RING):
                    sp.wait_ge(w_used, at(w_used, l, FRONT_GROUPS + (p - 1) * RING + g + 1))
                    sp.sem_inc(settled, 1)
                    load_expert_group(sp, g, l * EXPERTS + p * 2 + g % 2, ring[:, g], landed[g])
            sp.wait_ge(routed, at(routed, l, 1))
            sp.sem_inc(settled, 1)
            most = sp.value_load(ov_flag[0:1, 0:1], min_val=0, max_val=SEQ)
            with sp.If(most > SLOTS):
                sp.wait_ge(ov_listed, at(ov_listed, l, 1))
                sp.sem_inc(settled, 1)
                sp.wait_ge(w_used, at(w_used, l, LAYER_GROUPS))
                sp.sem_inc(settled, 1)
                with sp.Fori(0, OV_PAIRS) as i:
                    sp.wait_ge(ov_used, at(ov_used, l, i * RING))
                    for e in range(2):
                        expert = sp.value_load(ov_ids[0:1, bass.ds(i * 2 + e, 1)], min_val=0, max_val=EXPERTS - 1)
                        for g in range(e, RING, 2):
                            load_expert_group(sp, g, l * EXPERTS + expert, ring[:, g], ov_landed)
                sp.wait_ge(ov_used, at(ov_used, l, RING * OV_PAIRS))
                sp.sem_inc(settled, 1)
            with sp.Else():
                sp.sem_inc(ov_landed, per[ov_landed.name])
            sp.nop()
        for t in range(NT):
            sp.wait_ge(x_new, at(x_new, DEPTH - 1, 2 * (t + 1)))
            sp.dma_start(out.rearrange("o (t p) d -> p (o t) d", p=P)[:, t], xs[:, t]).then_inc(stored, 16)
        sp.wait_ge(stored, 16 * NT)

    @block.tensor
    def _(pe):
        def norm(n):
            for t in range(NT):
                if not isinstance(n, int):
                    pe.wait_ge(x_new, at(x_new, n - 1, 2 * (t + 1)))
                for k in range(KC):
                    mm = pe.transpose(ps[:, k // 2, (k % 2) * SEQ + t * P:(k % 2) * SEQ + (t + 1) * P],
                                      xs[:, t, k * P:(k + 1) * P], const("ident"))
            mm.then_inc(hT_mm, 1)
            pe.wait_ge(diag_ready, at(diag_ready, n, 2))
            for t in range(NT):
                mm = pe.matmul(ps[:, 4, t * P:(t + 1) * P], const("ones"), diag[:, t], start=True, stop=True)
            mm.then_inc(spread_mm, 1)

        def setup_vectors(n, bank):
            pe.wait_ge(setup_in, at(setup_in, n, per[setup_in.name]))
            pe.sem_inc(settled, 1)
            pe.transpose(ps[:, bank, 0:N_VEC], rows[0:N_VEC, :], const("ident")[0:N_VEC, 0:N_VEC]).then_inc(vec_mm, 1)

        def setup_matrices(l):
            pe.wait_ge(expanded, at(expanded, l, 4))
            for r in range(2):
                for q in range(QUADS):
                    mm = pe.transpose(ps[:, r, q * P:(q + 1) * P],
                                      b_exp[:, r, 4 * q:4 * q + 4].rearrange("p i g h -> p (i g h)"), const("ident"))
            mm.then_inc(bt_mm, 1)
            for r in range(2):
                for q in range(QUADS):
                    mm = pe.transpose(ps[:, 2 + r, q * P:(q + 1) * P],
                                      c_exp[:, r, q].rearrange("p g s -> p (g s)"), const("ident"))
            mm.then_inc(ct_mm, 1)

        pe.wait_ge(const_in, 16)
        pe.wait_ge(x_in, 16)
        pe.sem_inc(w_used, ahead[w_used.name])
        pe.sem_inc(ov_used, ahead[ov_used.name])
        norm(0)
        setup_vectors(0, 7)
        pe.wait_ge(vec_ready, at(vec_ready, 0, 1))

        with pe.Fori(0, DEPTH) as l:
            def weights(g, turn):
                pe.wait_ge(landed[g], at(landed[g], l, 16 * (turn + 1)))

            def release(mm):
                mm.then_inc(w_used, 1)

            def project_u():
                for k in range(KC):
                    pe.wait_ge(hT_ready, at(hT_ready, l, k + 1))
                    if k % 2 == 0:
                        weights(k // 2, 0)
                    for c in range(4):
                        mm = pe.matmul(ps[:, 4 + c // 2, (c % 2) * SEQ:(c % 2 + 1) * SEQ],
                                       ring[:, k // 2, k % 2, c * P:(c + 1) * P], hT[:, k],
                                       start=(k == 0 and c % 2 == 0), stop=(k == KC - 1), skip_group_check=True)
                mm.then_inc(u_mm, 1)

            def project_qkv(which, ks):
                bank, group, col = {"q": (0, 0, 512), "k": (2, 4, 0), "v": (0, 4, 512)}[which]
                for k in ks:
                    if k == 0 and which == "q":
                        pe.wait_ge(b_ready, at(b_ready, l, 4))
                        pe.wait_ge(c_ready, at(c_ready, l, 3))
                    if k == 0 and which == "v":
                        pe.wait_ge(q_raw, at(q_raw, l, 2))
                        pe.wait_ge(qk_sq, at(qk_sq, l, 2))
                    if which == "k" and k % 2 == 0:
                        weights(4 + k // 2, 0)
                    for t in range(NT):
                        mm = pe.matmul(ps[:, bank + t], hT[:, k, t * P:(t + 1) * P],
                                       ring[:, group + k // 2, k % 2, col:col + 512], start=(k == 0), stop=(k == KC - 1))
                    if k % 2 and which != "k":
                        release(mm)
                    if which == "k" and k == KC - 1:
                        mm.then_inc(k_mm, 1)

            def scan_input(k):
                half, q = divmod(k, 4)
                if k == 0:
                    pe.wait_ge(uT_act, at(uT_act, l, 1))
                    pe.wait_ge(uT_dve, at(uT_dve, l, 1))
                if k == 0:
                    pe.wait_ge(b_ready, at(b_ready, l, 4))
                if k >= 2:
                    pe.wait_ge(y_ready, at(y_ready, l, k - 1))
                for part in range(2):
                    for j in (0, 2, 1, 3):
                        r = slice(64 * (j // 2), 64 * (j // 2) + 64)
                        mm = pe.matmul(ps[:, 4 + 2 * (k % 2) + j // 2, (2 * part + j % 2) * P:(2 * part + j % 2 + 1) * P],
                                       b_lhs[r, part, j % 2, q], uT[r, q, half * HALF:(half + 1) * HALF],
                                       start=True, stop=True)
                mm.then_inc(bu_done, 1)

            def scan_output(k):
                q = k % 4
                pe.wait_ge(rotated, at(rotated, l, 4 * (k + 1)))
                for v in range(4):
                    for j in range(4):
                        mm = pe.matmul(ps[32 * j:32 * j + 32, 4 + 2 * (k % 2), 0:P],
                                       c_lhs[:, (0, 1, 2, 2)[v], q, 32 * j:32 * j + 32], post[:, v, j],
                                       start=(v == 0), stop=(v == 3), skip_group_check=True)
                mm.then_inc(y_done, 1)

            def turn_heads(w):
                if w == 0:
                    pe.wait_ge(k_raw, at(k_raw, l, 2))
                    pe.wait_ge(qk_sq, at(qk_sq, l, 4))
                    pe.wait_ge(q_roped, at(q_roped, l, 2))
                else:
                    pe.wait_ge(v_raw, at(v_raw, l, 2))
                    pe.wait_ge(k_roped, at(k_roped, l, 2))
                for t in range(NT):
                    for c in range(4):
                        mm = pe.transpose(ps[:, 2 - 2 * w + c // 2, (c % 2) * SEQ + t * P:(c % 2) * SEQ + (t + 1) * P],
                                          raw[:, 2 * w + t, c * P:(c + 1) * P], const("ident"))
                mm.then_inc(qk_turned, 1)

            BATCH = [(0, range(0, 8)), (1, range(0, 4)), (1, range(4, 8))]

            def bank(b):
                return (0, 2, 0)[b]

            def scores(b):
                tile, heads = BATCH[b]
                n = P * (tile + 1)
                if b == 0:
                    pe.wait_ge(qT_ready, at(qT_ready, l, 2))
                    pe.wait_ge(kT_ready, at(kT_ready, l, 2))
                if b == 2:
                    pe.wait_ge(o_ready, at(o_ready, l, 1))
                for i, h in enumerate(heads):
                    r = slice(64 * (h % 2), 64 * (h % 2) + 64)
                    mm = pe.matmul(ps[:, bank(b) + h % 2, (i // 2) * n:(i // 2 + 1) * n],
                                   qT[r, h // 2, tile * P:(tile + 1) * P], kT[r, h // 2, 0:n], start=True, stop=True)
                mm.then_inc(scored, 1)

            def turn_probs(b):
                pe.wait_ge(exped, at(exped, l, (8, 12, 16)[b]))
                for j in range(8):
                    mm = pe.transpose(ps[:, bank(b) + j // 4, (j % 4) * P:(j % 4 + 1) * P], probs[:, j * P:(j + 1) * P],
                                      const("ident"))
                mm.then_inc(p_turned, 1)

            def values(b):
                tile, heads = BATCH[b]
                pe.wait_ge(pT_ready, at(pT_ready, l, 2 * (b + 1)))
                for i, h in enumerate(heads):
                    s = (h % 2) * (len(heads) // 2) + i // 2
                    for c in range(tile + 1):
                        j = s * (tile + 1) + c
                        mm = pe.matmul(ps[:, bank(b), i * HD:(i + 1) * HD], probs[:, j * P:(j + 1) * P],
                                       vtok[:, c, h * HD:(h + 1) * HD], start=(c == 0), stop=(c == tile))
                mm.then_inc(pv_done, 1)

            def turn_attention():
                pe.wait_ge(o_ready, at(o_ready, l, 3))
                for t in range(NT):
                    for c in range(4):
                        mm = pe.transpose(ps[:, 2 + c // 2, (c % 2) * SEQ + t * P:(c % 2) * SEQ + (t + 1) * P],
                                          attn[:, t, c * P:(c + 1) * P], const("ident"))
                mm.then_inc(o_turned, 1)

            def attention_gate(u):
                t, half = divmod(u, 2)
                if u == 0:
                    for j in range(4):
                        weights(8 + j, 0)
                if u < 2:
                    pe.wait_ge(y_ready, at(y_ready, l, 7 + u))
                else:
                    pe.wait_ge(ga_tanh, at(ga_tanh, l, u - 1))
                for k in range(KC):
                    mm = pe.matmul(ps[:, 4 + 2 * (u % 2)], hT[:, k, t * P:(t + 1) * P],
                                   ring[:, 8 + k // 2, k % 2, 512 * half:512 * half + 512], start=(k == 0), stop=(k == KC - 1))
                    if u == 3 and k % 2:
                        release(mm)
                if u < 3:
                    mm.then_inc(ga_done, 1)

            def attention_project(u):
                t, half = divmod(u, 2)
                if u == 0:
                    pe.wait_ge(oT_ready, at(oT_ready, l, 2))
                    weights(0, 1)
                    weights(1, 1)
                if u >= 2:
                    pe.wait_ge(mix_a, at(mix_a, l, u - 1))
                for c in range(4):
                    mm = pe.matmul(ps[:, 5 + 2 * (u % 2)], oT[:, c, t * P:(t + 1) * P],
                                   ring[:, c // 2, c % 2, 512 * half:512 * half + 512], start=(c == 0), stop=(c == 3))
                    if u == 3 and c % 2:
                        release(mm)
                if u < 3:
                    mm.then_inc(ya_done, 1)

            def ssm_gate(u):
                t, half = divmod(u, 2)
                if u == 0:
                    for j in range(4):
                        weights(2 + j, 1)
                if u == 1:
                    pe.wait_ge(mix_a, at(mix_a, l, 4))
                if u >= 2:
                    pe.wait_ge(mixed, at(mixed, l, u - 1))
                for k in range(KC):
                    mm = pe.matmul(ps[:, 4 * (u % 2)], hT[:, k, t * P:(t + 1) * P],
                                   ring[:, 2 + k // 2, k % 2, 512 * half:512 * half + 512], start=(k == 0), stop=(k == KC - 1))
                    if u == 3 and k % 2:
                        release(mm)
                if u < 3:
                    mm.then_inc(gs_done, 1)

            def ssm_project(u):
                t, half = divmod(u, 2)
                pe.wait_ge(z_ready, at(z_ready, l, 4 * (t + 1)))
                for k in range(4):
                    if u == 0:
                        weights(6 + k, 1)
                    for w in range(2):
                        mm = pe.matmul(ps[:, 4 * (u % 2) + 1 + w], uT[:, k, t * P:(t + 1) * P],
                                       ring[:, 6 + k, w, 512 * half:512 * half + 512], start=(k == 0), stop=(k == 3))
                    if u == 3:
                        release(mm)
                if u < 3:
                    mm.then_inc(glu_done, 1)

            def turn_mix(t):
                if t == 0:
                    pe.wait_ge(vec_ready, at(vec_ready, l + 1, 1))
                pe.wait_ge(mixed, at(mixed, l, 2 * (t + 1)))
                if t:
                    pe.wait_ge(mixT_act, at(mixT_act, l, t))
                    pe.wait_ge(mixT_dve, at(mixT_dve, l, t))
                for c in range(KC):
                    mm = pe.transpose(ps[:, (3, 7)[c // 4], (c % 4) * P:(c % 4 + 1) * P], mix[:, t, c * P:(c + 1) * P],
                                      const("ident"))
                    if c % 4 == 3:
                        mm.then_inc(mixT_mm, 1)

            def project_out(t, ks=range(KC)):
                if 0 in ks:
                    pe.wait_ge(mixT_act, at(mixT_act, l, t + 1))
                    pe.wait_ge(mixT_dve, at(mixT_dve, l, t + 1))
                    pe.wait_ge(mixed, at(mixed, l, 3 + t))
                for k in ks:
                    g = (10 + k // 2) % RING
                    if t == 0 and k % 2 == 0:
                        weights(g, 1 if k < 4 else 2)
                    for half in range(2):
                        mm = pe.matmul(ps[:, 4 * t + half], hT[:, k, t * P:(t + 1) * P],
                                       ring[:, g, k % 2, 512 * half:512 * half + 512], start=(k == 0), stop=(k == KC - 1))
                    if t == 1 and k % 2:
                        release(mm)
                if t == 0:
                    mm.then_inc(wo_done, 1)

            def turn_x(t):
                pe.wait_ge(x_mid, at(x_mid, l, 2 * (t + 1)))
                for c in range(KC):
                    mm = pe.transpose(ps[:, 2 + 4 * t + c // 4, (c % 4) * P:(c % 4 + 1) * P], xs[:, t, c * P:(c + 1) * P],
                                      const("ident"))
                    if c % 4 == 3:
                        mm.then_inc(x_turned, 1)

            def route(t):
                if t == 0:
                    pe.wait_ge(router_ready, at(router_ready, l, 1))
                pe.wait_ge(x_act, at(x_act, l, t + 1))
                pe.wait_ge(x_dve, at(x_dve, l, t + 1))
                for k in range(KC):
                    mm = pe.matmul(ps[:, 0, t * 36:(t + 1) * 36], hT[:, k, t * P:(t + 1) * P], router_w[:, k],
                                   start=(k == 0), stop=(k == KC - 1))
                if t == NT - 1:
                    mm.then_inc(logits_mm, 1)

            project_u()
            setup_matrices(l)
            project_qkv("q", range(0, 2))
            scan_input(0)
            project_qkv("q", range(2, 3))
            scan_input(1)
            project_qkv("q", range(3, 7))
            scan_output(0)
            project_qkv("q", range(7, 8))
            scan_input(2)
            project_qkv("k", range(0, 2))
            scan_output(1)
            project_qkv("k", range(2, 3))
            scan_input(3)
            project_qkv("k", range(3, 5))
            scan_output(2)
            project_qkv("k", range(5, 6))
            scan_input(4)
            project_qkv("k", range(6, 8))
            project_qkv("v", range(0, 2))
            scan_output(3)
            project_qkv("v", range(2, 3))
            scan_input(5)
            project_qkv("v", range(3, 5))
            scan_output(4)
            project_qkv("v", range(5, 6))
            scan_input(6)
            project_qkv("v", range(6, 8))
            scan_output(5)
            turn_heads(0)
            scan_input(7)
            turn_heads(1)
            scan_output(6)
            scores(0)
            attention_gate(0)
            turn_probs(0)
            scores(1)
            scan_output(7)
            values(0)
            attention_gate(1)
            turn_probs(1)
            scores(2)
            values(1)
            attention_gate(2)
            turn_probs(2)
            values(2)
            attention_gate(3)
            turn_attention()
            ssm_gate(0)
            for u in range(4):
                attention_project(u)
            ssm_project(0)
            setup_vectors(l + 1, 3)
            for u in range(1, 3):
                ssm_gate(u)
                ssm_project(u)
            turn_mix(0)
            ssm_gate(3)
            ssm_project(3)
            project_out(0)
            turn_mix(1)
            project_out(1, range(0, 5))
            turn_x(0)
            project_out(1, range(5, KC))
            route(0)
            turn_x(1)
            route(1)

            for n in range(4):
                pe.matmul(ps[:, 4 + n], const("zero"), cst[:, 0:512], start=True, stop=False, skip_group_check=True)
            pe.wait_ge(assigned, at(assigned, l, 1))
            pe.matmul(ps[:, 1, 0:32], const("before"), assign[:, 0], start=True, stop=True)
            pe.matmul(ps[:, 1, 32:64], const("ones"), assign[:, 0], start=True, stop=False)
            pe.matmul(ps[:, 1, 32:64], const("before"), assign[:, 1], start=False, stop=True)
            pe.matmul(ps[:, 1, 64:96], const("ones"), assign[:, 0], start=True, stop=False)
            pe.matmul(ps[:, 1, 64:96], const("ones"), assign[:, 1], start=False, stop=True).then_inc(pos_mm, 1)

            def gather(S, i):
                pe.wait_ge(S["pick"], at(S["pick"], l, i + 1))
                for k in range(KC):
                    for t in range(NT):
                        mm = pe.matmul(ps[:, 2 + k // 4, (k % 4) * P:(k % 4 + 1) * P], xs[:, t, k * P:(k + 1) * P],
                                       pick[:, t], start=(t == 0), stop=(t == NT - 1))
                mm.then_inc(S["gathered"], 1)

            def pair(S, i, wait_weights, place=lambda g: ring[:, g]):
                pe.wait_ge(S["xT"], at(S["xT"], l, i + 1))
                for k in range(KC):
                    for e in range(2):
                        g = 2 * (k // 2) + e
                        if k % 2 == 0:
                            wait_weights(g)
                        rows_e = slice(SLOTS * e, SLOTS * (e + 1))
                        for half in range(2):
                            mm = pe.matmul(ps[rows_e, half], xT[:, k, rows_e], place(g)[:, k % 2, 512 * half:512 * half + 512],
                                           start=(k == 0), stop=(k == KC - 1), skip_group_check=True)
                        if k % 2:
                            mm.then_inc(S["used"], 1)
                gather(S, i + 1)
                pe.wait_ge(S["h"], at(S["h"], l, i + 1))
                for c in range(4):
                    mm = pe.transpose(ps[:, 0, c * P:(c + 1) * P], act_buf[:, c * P:(c + 1) * P], const("ident"))
                mm.then_inc(S["ffT_mm"], 1)
                pe.wait_ge(S["back"], at(S["back"], l, i + 1))
                for t in range(NT):
                    mm = pe.transpose(ps[:, 1, t * P:(t + 1) * P], back[:, t], const("ident"))
                mm.then_inc(S["backT_mm"], 1)
                pe.wait_ge(S["ffT"], at(S["ffT"], l, i + 1))
                pe.wait_ge(S["xT"], at(S["xT"], l, i + 2))
                for half in range(2):
                    for c in range(4):
                        for e in range(2):
                            g = 8 + 2 * (c // 2) + e
                            if half == 0 and c % 2 == 0:
                                wait_weights(g)
                            rows_e = slice(SLOTS * e, SLOTS * (e + 1))
                            mm = pe.matmul(ps[rows_e, 2 + half], ffT[:, c, rows_e],
                                           place(g)[:, c % 2, 512 * half:512 * half + 512],
                                           start=(c == 0), stop=(c == 3), skip_group_check=True)
                            if half == 1 and c % 2:
                                mm.then_inc(S["used"], 1)
                    if half == 0:
                        mm.then_inc(S["y0_mm"], 1)
                pe.wait_ge(S["backT"], at(S["backT"], l, i + 1))
                for half in range(2):
                    pe.wait_ge(S[("y0", "y1")[half]], at(S[("y0", "y1")[half]], l, i + 1))
                    for t in range(NT):
                        mm = pe.matmul(ps[:, 4 + 2 * t + half], backT[:, t], ybuf[:, half],
                                       start=False, stop=False, skip_group_check=True)
                mm.then_inc(S["scattered"], 1)

            gather(main, 0)
            def pair_landed(g, p):
                if g < EARLY:
                    pe.wait_ge(landed[g], at(landed[g], l, 16 * mixer_loads[g] + p * 16))
                else:
                    pe.wait_ge(landed[g], at(landed[g], l, 16 * mixer_loads[g] + (p + 1) * 16))

            def first_landed(g):
                if g < EARLY:
                    pe.wait_ge(early_in[g], at(early_in[g], l, 16))
                else:
                    pair_landed(g, 0)

            pair(main, 0, first_landed, lambda g: early[g] if g < EARLY else ring[:, g])
            with pe.Fori(1, PAIRS) as p:
                pair(main, p, lambda g: pair_landed(g, p))
            most = pe.value_load(ov_flag[0:1, 0:1], min_val=0, max_val=SEQ)
            with pe.If(most > SLOTS):
                gather(over, 0)
                with pe.Fori(0, OV_PAIRS) as i:
                    pe.wait_ge(ov_landed, at(ov_landed, l, (i + 1) * 16 * RING))
                    pair(over, i, lambda g: None)
            with pe.Else():
                for n in ("gathered", "ffT_mm", "backT_mm", "y0_mm", "scattered"):
                    pe.sem_inc(over[n], per[over[n].name])
                pe.sem_inc(ov_used, per[ov_used.name])
            pe.nop()
            with pe.If(l < DEPTH - 1):
                norm(l + 1)
            pe.nop()

    @block.scalar
    def _(act):
        def load_setup(l):
            def put(dst, src):
                act.dma_start(dst, src).then_inc(setup_in, 16)

            one = bass.ds(l, 1)
            put(rows[0:8, :], norm1_g[one].rearrange("o (r c) -> (o r) c", c=P))
            put(rows[8:16, :], norm2_g[one].rearrange("o (r c) -> (o r) c", c=P))
            put(rows[16:20, :], ssm_d[one].rearrange("o (r c) -> (o r) c", c=P))
            put(rows[20:36, :], ssm_a_re[one].rearrange("o (i g) s -> (o i) (g s)", g=2))
            put(rows[36:52, :], ssm_a_im[one].rearrange("o (i g) s -> (o i) (g s)", g=2))
            put(log_dt, ssm_log_dt[one].to_broadcast([P, GROUPS]))
            for r, b in enumerate((ssm_b_re, ssm_b_im)):
                put(b_raw[:, r], b[one].rearrange("o (i g) s h -> (o g s) i h", g=2))
            for r, c in enumerate((ssm_c_re, ssm_c_im)):
                put(c_raw[:, r], c[one].rearrange("o (q g) h s -> (o g h) q s", q=QUADS))

        def load_layer(l):
            def put(dst, src):
                act.dma_start(dst, src).then_inc(layer_in, 16)

            one = bass.ds(l, 1)
            put(qk_gain[:, 0], q_norm_g[one].to_broadcast([P, HD]))
            put(qk_gain[:, 1], k_norm_g[one].to_broadcast([P, HD]))
            put(router_w[:, :, 0:4], router_w_group[one].rearrange("o (k p) n -> (o p) k n", p=P))
            put(router_w[:, :, 4:36], router_w_expert[one].rearrange("o (k p) n -> (o p) k n", p=P))
            put(router_b[:, 0:4], router_b_group[one].to_broadcast([P, EGROUPS]))
            put(router_b[:, 4:36], router_b_expert[one].to_broadcast([P, EXPERTS]))

        def norm_squares(n):
            act.activation(junk[:, 0], xs[:, 0], ACT.Square, accum_out=ssq[:, 0:1]).then_inc(ssq_act, 1)
            act.wait_ge(ssq_act, at(ssq_act, n, 1))
            act.wait_ge(ssq_dve, at(ssq_dve, n, 1))
            act.wait_ge(const_in, 16)
            act.activation(std, ssq, ACT.Sqrt, bias=const("eps"), scale=1.0 / D).then_inc(std_ready, 1)

        def setup_one(n):
            act.wait_ge(turn_ready, at(turn_ready, n, 1))
            act.activation(one[:, 1], one[:, 0], ACT.Sin, scale=TWO_PI).then_inc(one_ready, 1)
            act.activation(one[:, 2], one[:, 0], ACT.Sin, scale=TWO_PI / 2).then_inc(one_ready, 1)

        def setup_sines(n, h):
            act.wait_ge(turns_ready, at(turns_ready, n, h + 1))
            act.activation(turn_b[:, h], turn_a[:, h], ACT.Sin, scale=TWO_PI / 2).then_inc(half_sine, 1)
            act.wait_ge(half_sine, at(half_sine, n, h + 1))
            act.activation(turn_b[:, h], turn_b[:, h], ACT.Square).then_inc(half_ready, 1)
            act.activation(sinT[:, 8 * h:8 * h + 8], turn_a[:, h], ACT.Sin, scale=TWO_PI).then_inc(sin_ready, 1)

        load_setup(0)
        act.wait_ge(x_in, 16)
        norm_squares(0)
        setup_one(0)
        for h in range(2):
            setup_sines(0, h)

        with act.Fori(0, DEPTH) as l:
            load_layer(l)
            act.wait_ge(u_mm, at(u_mm, l, 1))
            act.copy(uT[:, 0:2].rearrange("p q s -> p (q s)"), ps[:, 4]).then_inc(uT_act, 1)
            act.wait_ge(bt_mm, at(bt_mm, l, 1))
            for r in range(2):
                for o in range(2):
                    act.activation(b_lhs[:, r, o].rearrange("p q s -> p (q s)"), ps[:, r], ACT.Copy,
                                   scale=const("odd_tile")[:, o:o + 1]).then_inc(b_ready, 1)

            def heads_out(w):
                if w == 0:
                    act.wait_ge(w_used, at(w_used, l, 4))
                else:
                    act.wait_ge(k_mm, at(k_mm, l, 1))
                for t in range(NT):
                    act.copy(raw[:, 2 * w + t], ps[:, 2 * w + t]).then_inc((q_raw, k_raw)[w], 1)
                if w == 1:
                    act.wait_ge(qk_ss, at(qk_ss, l, 1))
                for t in range(NT):
                    act.activation(squares[:, t], ps[:, 2 * w + t], ACT.Square).then_inc(qk_sq, 1)

            def heads_std(w):
                act.wait_ge(qk_ss, at(qk_ss, l, w + 1))
                act.activation(head_rs[:, 2 * w:2 * w + 2], head_ss[:, 2 * w:2 * w + 2], ACT.Sqrt, bias=const("eps"),
                               scale=1.0 / HD).then_inc(qk_std, 1)

            def gelu(k):
                act.wait_ge(gelu_in, at(gelu_in, l, k + 1))
                act.activation(y2, y3, ACT.Tanh, scale=GELU_C).then_inc(gelu_tanh, 1)

            def exps(b):
                n = (8, 4, 4)[b]
                w = 1024 // n
                act.wait_ge(maxed, at(maxed, l, b + 1))
                for s in range(n):
                    i = 2 * (s % (n // 2)) + s // (n // 2)
                    act.activation(probs[:, s * w:(s + 1) * w], probs[:, s * w:(s + 1) * w], ACT.Exp,
                                   bias=row_max[:, s:s + 1], scale=ATT_SCALE,
                                   accum_out=row_sum[:, i:i + 1]).then_inc(exped, 1)

            def probs_turned(b):
                act.wait_ge(p_turned, at(p_turned, l, b + 1))
                for n in range(2):
                    act.copy(probs[:, n * 512:(n + 1) * 512], ps[:, (0, 2, 0)[b] + n]).then_inc(pT_ready, 1)

            def att_gate_out(u):
                if u < 3:
                    act.wait_ge(ga_done, at(ga_done, l, u + 1))
                else:
                    act.wait_ge(w_used, at(w_used, l, 12))
                if u == 0:
                    act.wait_ge(scanned, at(scanned, l, 8))
                act.activation(att_gate[:, u], ps[:, 4 + 2 * (u % 2)], ACT.Tanh, scale=0.5).then_inc(ga_tanh, 1)

            heads_out(0)
            heads_std(0)
            gelu(0)
            gelu(1)
            heads_out(1)
            gelu(2)
            heads_std(1)
            gelu(3)
            act.wait_ge(w_used, at(w_used, l, 8))
            for t in range(NT):
                act.copy(vtok[:, t], ps[:, t]).then_inc(v_raw, 1)
            gelu(4)
            act.wait_ge(qk_turned, at(qk_turned, l, 1))
            for n in range(2):
                act.copy(qT[:, 2 * n:2 * n + 2].rearrange("p c s -> p (c s)"), ps[:, 2 + n]).then_inc(qT_ready, 1)
            gelu(5)
            act.wait_ge(qk_turned, at(qk_turned, l, 2))
            for n in range(2):
                act.copy(kT[:, 2 * n:2 * n + 2].rearrange("p c s -> p (c s)"), ps[:, n]).then_inc(kT_ready, 1)
            exps(0)
            probs_turned(0)
            gelu(6)
            att_gate_out(0)
            exps(1)
            probs_turned(1)
            gelu(7)
            att_gate_out(1)
            exps(2)
            probs_turned(2)
            att_gate_out(2)
            att_gate_out(3)
            act.wait_ge(o_turned, at(o_turned, l, 1))
            for n in range(2):
                act.copy(oT[:, 2 * n:2 * n + 2].rearrange("p c s -> p (c s)"), ps[:, 2 + n]).then_inc(oT_ready, 1)
            act.wait_ge(z_ready, at(z_ready, l, 8))
            load_setup(1 - l)
            for u in range(4):
                b = 4 * (u % 2)
                if u < 3:
                    act.wait_ge(gs_done, at(gs_done, l, u + 1))
                else:
                    act.wait_ge(w_used, at(w_used, l, 18))
                if u >= 2:
                    act.wait_ge(mixed, at(mixed, l, u - 1))
                act.activation(gates[:, 0, u % 2], ps[:, b], ACT.Tanh, scale=0.5).then_inc(gate_tanh, 1)
                if u < 3:
                    act.wait_ge(glu_done, at(glu_done, l, u + 1))
                else:
                    act.wait_ge(w_used, at(w_used, l, 22))
                act.activation(gates[:, 1, u % 2], ps[:, b + 2], ACT.Tanh, scale=0.25).then_inc(gate_tanh, 1)
                if u == 0:
                    setup_one(l + 1)
                if u == 1:
                    setup_sines(l + 1, 0)
                if u == 2:
                    act.wait_ge(mixT_mm, at(mixT_mm, l, 1))
                    act.copy(hT[:, 0:4, 0:P], ps[:, 3].rearrange("p (c s) -> p c s", c=4)).then_inc(mixT_act, 1)
                    setup_sines(l + 1, 1)
            act.wait_ge(mixT_mm, at(mixT_mm, l, 3))
            act.copy(hT[:, 0:4, P:2 * P], ps[:, 3].rearrange("p (c s) -> p c s", c=4)).then_inc(mixT_act, 1)
            act.wait_ge(x_mid, at(x_mid, l, 2))
            act.activation(junk[:, 0], xs[:, 0], ACT.Square, accum_out=ssq[:, 0:1]).then_inc(mid_sq, 1)
            act.wait_ge(x_turned, at(x_turned, l, 1))
            act.copy(hT[:, 0:4, 0:P], ps[:, 2].rearrange("p (c s) -> p c s", c=4)).then_inc(x_act, 1)
            act.wait_ge(x_turned, at(x_turned, l, 3))
            act.copy(hT[:, 0:4, P:2 * P], ps[:, 6].rearrange("p (c s) -> p c s", c=4)).then_inc(x_act, 1)
            act.activation(junk[:, 1], xs[:, 1], ACT.Square, accum_out=ssq[:, 1:2]).then_inc(mid_sq, 1)
            act.wait_ge(mid_sq, at(mid_sq, l, 2))
            act.activation(std, ssq, ACT.Sqrt, bias=const("eps"), scale=1.0 / D).then_inc(mid_std, 1)
            act.wait_ge(group_max, at(group_max, l, 1))
            for t in range(NT):
                act.activation(glog[:, t, 0:EGROUPS], glog[:, t, 0:EGROUPS], ACT.Exp, bias=rt[:, 0, t:t + 1],
                               accum_out=rt[:, 2, t:t + 1]).then_inc(group_exp, 1)
            act.wait_ge(top_diff, at(top_diff, l, 1))
            act.activation(rt[:, 4], rt[:, 1], ACT.Exp).then_inc(top_exp, 1)

            def pair(S, i, gate_up_done):
                gate_up_done()
                act.activation(act_buf, ps[:, 0], ACT.Tanh, scale=0.5).then_inc(S["tanh"], 1)
                act.wait_ge(S["ffT_mm"], at(S["ffT_mm"], l, i + 1))
                act.copy(ffT.rearrange("p c s -> p (c s)"), ps[:, 0]).then_inc(S["ffT"], 1)
                act.wait_ge(S["y0_mm"], at(S["y0_mm"], l, i + 1))
                act.copy(ybuf[:, 0], ps[:, 2]).then_inc(S["y0"], 1)

            with act.Fori(0, PAIRS) as p:
                pair(main, p, lambda: act.wait_ge(w_used, at(w_used, l, FRONT_GROUPS + p * RING + 8)))
            act.wait_ge(routed, at(routed, l, 1))
            act.sem_inc(settled, 1)
            most = act.value_load(ov_flag[0:1, 0:1], min_val=0, max_val=SEQ)
            with act.If(most > SLOTS):
                with act.Fori(0, OV_PAIRS) as i:
                    pair(over, i, lambda: act.wait_ge(ov_used, at(ov_used, l, i * RING + 8)))
            with act.Else():
                for n in ("tanh", "ffT", "y0"):
                    act.sem_inc(over[n], per[over[n].name])
            act.nop()
            with act.If(l < DEPTH - 1):
                act.wait_ge(x_new, at(x_new, l, 4))
                norm_squares(l + 1)
            act.nop()

    @block.vector
    def _(ve):
        def norm_squares(n):
            ve.tensor_tensor_reduce(out=junk[:, 1], in0=xs[:, 1], in1=xs[:, 1], scale=1.0, scalar=0.0, op0=ALU.mult,
                                    op1=ALU.add, accum_out=ssq[:, 1:2]).then_inc(ssq_dve, 1)

        def norm_scale(n):
            ve.wait_ge(std_ready, at(std_ready, n, 1))
            ve.reciprocal(rstd, std).then_inc(rstd_ready, 1)
            ve.wait_ge(rstd_ready, at(rstd_ready, n, 1))
            for t in range(NT):
                ve.tensor_scalar(diag[:, t], const("ident"), rstd[:, t:t + 1], None, ALU.mult).then_inc(diag_ready, 1)

        def norm_turned(n, gain):
            ve.wait_ge(spread_mm, at(spread_mm, n, 1))
            ve.tensor_copy(rms_inv, ps[:, 4, 0:SEQ]).then_inc(spread, 1)
            ve.wait_ge(spread, at(spread, n, 1))
            ve.wait_ge(hT_mm, at(hT_mm, n, 1))
            for k in range(KC):
                ve.scalar_tensor_tensor(hT[:, k], ps[:, k // 2, (k % 2) * SEQ:(k % 2 + 1) * SEQ], gain[:, k:k + 1], rms_inv,
                                        ALU.mult, ALU.mult).then_inc(hT_ready, 1)

        def angles(S, h):
            a, b = turn_a[:, h], turn_b[:, h]
            tiles = slice(8 * h, 8 * h + 8)
            step = wide(const("step"), 1, [8, TW])
            ve.tensor_tensor(a, step, wide(turns_hi[:, tiles], 2, [8, TW]), ALU.mult).then_inc(dve_setup, 1)
            ve.wait_ge(dve_setup, S.next())
            ve.tensor_scalar(b, a, ROUND, ROUND, ALU.add, ALU.subtract).then_inc(dve_setup, 1)
            ve.wait_ge(dve_setup, S.next())
            ve.tensor_tensor(a, a, b, ALU.subtract).then_inc(dve_setup, 1)
            ve.wait_ge(dve_setup, S.next())
            ve.tensor_tensor(b, step, wide(turns_lo[:, tiles], 2, [8, TW]), ALU.mult).then_inc(dve_setup, 1)
            ve.wait_ge(dve_setup, S.next())
            ve.tensor_tensor(a, a, b, ALU.add).then_inc(dve_setup, 1)
            ve.wait_ge(dve_setup, S.next())
            ve.tensor_scalar(b, a, ROUND, ROUND, ALU.add, ALU.subtract).then_inc(dve_setup, 1)
            ve.wait_ge(dve_setup, S.next())
            ve.tensor_tensor(a, a, b, ALU.subtract).then_inc(turns_ready, 1)

        def exp(S, out, x, n):
            k, r, p, power = (exp_tmp[:, m, 0:n] for m in range(4))
            ve.tensor_scalar(r, x, -87.0, 88.0, ALU.max, ALU.min).then_inc(dve_setup, 1)
            ve.wait_ge(dve_setup, S.next())
            ve.tensor_scalar(k, r, LOG2_E, ROUND, ALU.mult, ALU.add).then_inc(dve_setup, 1)
            ve.wait_ge(dve_setup, S.next())
            ve.tensor_scalar(k, k, ROUND, None, ALU.subtract).then_inc(dve_setup, 1)
            ve.wait_ge(dve_setup, S.next())
            for part in (LN2_HIGH, LN2_LOW):
                ve.scalar_tensor_tensor(r, k, -part, r, ALU.mult, ALU.add).then_inc(dve_setup, 1)
                ve.wait_ge(dve_setup, S.next())
            ve.tensor_scalar(power.bitcast(I32), k, 127.0, 2.0 ** 23, ALU.add, ALU.mult).then_inc(dve_setup, 1)
            S.add()
            ve.tensor_scalar(p, r, 1.0 / math.factorial(7), None, ALU.mult).then_inc(dve_setup, 1)
            ve.wait_ge(dve_setup, S.next())
            for m in range(6, 0, -1):
                ve.scalar_tensor_tensor(p, p, 1.0 / math.factorial(m), r, ALU.add, ALU.mult).then_inc(dve_setup, 1)
                ve.wait_ge(dve_setup, S.next())
            return ve.scalar_tensor_tensor(out, p, 1.0, power, ALU.add, ALU.mult)

        def take_vectors(n, bank):
            ve.wait_ge(vec_mm, at(vec_mm, n, 1))
            ve.tensor_copy(vec, ps[:, bank, 0:N_VEC]).then_inc(vec_ready, 1)
            ve.wait_ge(vec_ready, at(vec_ready, n, 1))

        def setup_first(n, S):
            ve.wait_ge(setup_in, at(setup_in, n, per[setup_in.name]))
            exp(S, log_dt, log_dt, GROUPS).then_inc(dve_setup, 1)
            ve.wait_ge(dve_setup, S.next())
            a_re, a_im = turned("a_re"), turned("a_im")
            steps = log_dt.rearrange("p (i g) -> p i g", g=2)
            for g in range(2):
                ve.tensor_copy(dt_[64 * g:64 * g + 64], steps[64 * g:64 * g + 64, :, g]).then_inc(dve_setup, 1)
                ve.wait_ge(dve_setup, S.next())
            ve.tensor_tensor(sc0, a_re, dt_, ALU.mult).then_inc(dve_setup, 1)
            ve.wait_ge(dve_setup, S.next())
            ve.tensor_tensor(theta, a_im, dt_, ALU.mult).then_inc(dve_setup, 1)
            ve.wait_ge(dve_setup, S.next())
            ve.tensor_scalar(turns_lo, theta, float(1.0 / (2.0 * np.pi)), None, ALU.mult).then_inc(dve_setup, 1)
            ve.wait_ge(dve_setup, S.next())
            ve.tensor_scalar(sc1, turns_lo, ROUND, ROUND, ALU.add, ALU.subtract).then_inc(dve_setup, 1)
            ve.wait_ge(dve_setup, S.next())
            ve.tensor_tensor(turns_lo, turns_lo, sc1, ALU.subtract).then_inc(dve_setup, 1)
            ve.wait_ge(dve_setup, S.next())
            ve.tensor_scalar(turns_hi, turns_lo, ROUND15, ROUND15, ALU.add, ALU.subtract).then_inc(dve_setup, 1)
            ve.wait_ge(dve_setup, S.next())
            ve.tensor_tensor(turns_lo, turns_lo, turns_hi, ALU.subtract).then_inc(dve_setup, 1)
            ve.wait_ge(dve_setup, S.next())
            ve.tensor_tensor(one[:, 0], turns_hi, turns_lo, ALU.add).then_inc(turn_ready, 1)
            ve.tensor_tensor(den, a_re, a_re, ALU.mult).then_inc(dve_setup, 1)
            ve.wait_ge(dve_setup, S.next())
            ve.tensor_tensor(sc1, a_im, a_im, ALU.mult).then_inc(dve_setup, 1)
            ve.wait_ge(dve_setup, S.next())
            ve.tensor_tensor(den, den, sc1, ALU.add).then_inc(dve_setup, 1)
            ve.wait_ge(dve_setup, S.next())
            ve.reciprocal(den, den).then_inc(dve_setup, 1)
            ve.wait_ge(dve_setup, S.next())
            exp(S, decay, sc0, TILES).then_inc(dve_setup, 1)
            ve.wait_ge(dve_setup, S.next())
            ve.wait_ge(one_ready, at(one_ready, n, 2))
            ve.tensor_tensor(one[:, 2], one[:, 2], one[:, 2], ALU.mult).then_inc(dve_setup, 1)
            ve.wait_ge(dve_setup, S.next())
            ve.tensor_scalar(one[:, 2], one[:, 2], -2.0, 1.0, ALU.mult, ALU.add).then_inc(dve_setup, 1)
            ve.wait_ge(dve_setup, S.next())
            ve.tensor_tensor(a_bar_re, decay, one[:, 2], ALU.mult).then_inc(dve_setup, 1)
            ve.wait_ge(dve_setup, S.next())
            ve.tensor_tensor(a_bar_im, decay, one[:, 1], ALU.mult).then_inc(dve_setup, 1)
            ve.wait_ge(dve_setup, S.next())
            ve.tensor_scalar(sc0, a_bar_re, 1.0, None, ALU.subtract).then_inc(dve_setup, 1)
            ve.wait_ge(dve_setup, S.next())
            ve.tensor_tensor(f_re, sc0, a_re, ALU.mult).then_inc(dve_setup, 1)
            ve.wait_ge(dve_setup, S.next())
            ve.tensor_tensor(sc1, a_bar_im, a_im, ALU.mult).then_inc(dve_setup, 1)
            ve.wait_ge(dve_setup, S.next())
            ve.tensor_tensor(f_re, f_re, sc1, ALU.add).then_inc(dve_setup, 1)
            ve.wait_ge(dve_setup, S.next())
            ve.tensor_tensor(f_re, f_re, den, ALU.mult).then_inc(dve_setup, 1)
            ve.wait_ge(dve_setup, S.next())
            ve.tensor_tensor(f_im, a_bar_im, a_re, ALU.mult).then_inc(dve_setup, 1)
            ve.wait_ge(dve_setup, S.next())
            ve.tensor_tensor(sc1, sc0, a_im, ALU.mult).then_inc(dve_setup, 1)
            ve.wait_ge(dve_setup, S.next())
            ve.tensor_tensor(f_im, f_im, sc1, ALU.subtract).then_inc(dve_setup, 1)
            ve.wait_ge(dve_setup, S.next())
            ve.tensor_tensor(f_im, f_im, den, ALU.mult).then_inc(f_ready, 1)

        def setup_second(n, S):
            for h in range(2):
                ve.wait_ge(half_ready, at(half_ready, n, h + 1))
                b = turn_b[:, h]
                ins = ve.tensor_scalar(cosT[:, 8 * h:8 * h + 8], b, -2.0, 1.0, ALU.mult, ALU.add)
                if h == 0:
                    ins.then_inc(dve_setup, 1)
                    ve.wait_ge(dve_setup, S.next())
                else:
                    ins.then_inc(tables_ready, 1)
                    ve.wait_ge(sin_ready, at(sin_ready, n, 2))
                    ve.wait_ge(tables_ready, at(tables_ready, n, 1))

        S = counted(dve_start, 0)
        ve.memset(glog, -BIG).then_inc(dve_start, 1)
        ve.wait_ge(dve_start, S.next())
        ve.wait_ge(x_in, 16)
        norm_squares(0)
        ve.wait_ge(const_in, 16)
        norm_scale(0)
        take_vectors(0, 7)
        norm_turned(0, turned("norm1"))
        S = counted(dve_setup, 0)
        setup_first(0, S)
        angles(S, 0)
        angles(S, 1)
        setup_second(0, S)
        S.close()

        with ve.Fori(0, DEPTH) as l:
            L = counted(dve_layer, l)
            ve.tensor_copy(gain2, turned("norm2")).then_inc(dve_layer, 1)
            ve.wait_ge(dve_layer, L.next())
            ve.memset(slot_of[:, :, EXPERTS:BLOCKS], -1.0).then_inc(dve_layer, 1)
            ve.wait_ge(dve_layer, L.next())
            ve.memset(weight_of[:, :, EXPERTS:BLOCKS], 0.0).then_inc(dve_layer, 1)
            ve.wait_ge(dve_layer, L.next())
            ve.wait_ge(u_mm, at(u_mm, l, 1))
            ve.tensor_copy(uT[:, 2:4].rearrange("p q s -> p (q s)"), ps[:, 5]).then_inc(uT_dve, 1)
            ve.wait_ge(ct_mm, at(ct_mm, l, 1))
            for v, (b, sign) in enumerate(((2, 1.0), (2, -1.0), (3, -1.0))):
                ve.tensor_scalar(c_lhs[:, v].rearrange("p q s -> p (q s)"), ps[:, b], sign, None,
                                 ALU.mult).then_inc(c_ready, 1)

            def scan(k):
                half, q = divmod(k, 4)
                tiles = slice(4 * q, 4 * q + 4)
                b = 4 + 2 * (k % 2)
                ve.wait_ge(bu_done, at(bu_done, l, k + 1))
                cs, sn = (x[:, tiles, 0:HALF].rearrange("p (b j) t -> p b j t", b=2) for x in (cosT, sinT))
                re, im = (ps[:, b:b + 2, r * SEQ:(r + 1) * SEQ].rearrange("p b (j t) -> p b j t", j=2) for r in range(2))
                out4 = [pre[:, v].rearrange("p (b j) t -> p b j t", b=2) for v in range(4)]
                if k > 0:
                    ve.wait_ge(scanned, at(scanned, l, k))
                for o, x, table in ((0, re, cs), (1, im, sn), (2, im, cs), (3, re, sn)):
                    ve.tensor_tensor(out4[o], x, table, ALU.mult).then_inc(dve_layer, 1)
                    L.add()
                ve.wait_ge(dve_layer, L.value() - 2)
                ve.tensor_tensor(pre[:, 0], pre[:, 0], pre[:, 1], ALU.add).then_inc(dve_layer, 1)
                ve.wait_ge(dve_layer, L.next() - 1)
                ve.tensor_tensor(pre[:, 2], pre[:, 2], pre[:, 3], ALU.subtract).then_inc(dve_layer, 1)
                ve.wait_ge(dve_layer, L.next())
                if k > 0:
                    ve.wait_ge(rotated, at(rotated, l, 4 * k))
                if k > 0:
                    ve.wait_ge(carried, at(carried, l, min(k, 4)))
                for j in range(4):
                    for r in range(2):
                        first = 0.0 if half == 0 else carry[:, r, 4 * q + j:4 * q + j + 1]
                        ins = ve.tensor_tensor_scan(wst[:, r, j], decay[:, 4 * q + j:4 * q + j + 1].to_broadcast([P, HALF]),
                                                    pre[:, 2 * r, j], first, ALU.mult, ALU.add)
                ins.then_inc(scanned, 1)

            def skip(k):
                half, q = divmod(k, 4)
                ve.wait_ge(y_done, at(y_done, l, k + 1))
                if k > 0:
                    ve.wait_ge(z_ready, at(z_ready, l, k))
                ve.scalar_tensor_tensor(y1, uT[:, q, half * HALF:(half + 1) * HALF], turned("skip")[:, q:q + 1],
                                        ps[:, 4 + 2 * (k % 2), 0:P], ALU.mult, ALU.add).then_inc(y_ready, 1)

            def head_rms(w):
                ve.wait_ge(qk_sq, at(qk_sq, l, 2 * w + 2))
                ve.tensor_reduce(head_ss[:, 2 * w:2 * w + 2], squares.rearrange("p t (h d) -> p t h d", h=HEADS), AX.X,
                                 ALU.add).then_inc(qk_ss, 1)
                ve.wait_ge(qk_std, at(qk_std, l, w + 1))
                ve.reciprocal(head_ss[:, 2 * w:2 * w + 2], head_rs[:, 2 * w:2 * w + 2]).then_inc(qk_inv, 1)

            def softmax_in(b):
                ve.wait_ge(scored, at(scored, l, b + 1))
                if b > 0:
                    ve.wait_ge(pv_done, at(pv_done, l, b))
                bank = (0, 2, 0)[b]
                flat_ps = ps[:, bank:bank + 2].rearrange("p b n -> p (b n)")
                if b == 0:
                    v, w = (z.rearrange("p (s k) -> p s k", s=8) for z in (probs, flat_ps))
                    ve.tensor_tensor(v, w, wide(const("causal"), 1, [8, P]), ALU.add).then_inc(dve_layer, 1)
                    ve.wait_ge(dve_layer, L.next())
                    ve.tensor_reduce(row_max, v, AX.X, ALU.max).then_inc(dve_layer, 1)
                    ve.wait_ge(dve_layer, L.next())
                    n = 8
                else:
                    v, w = (z.rearrange("p (s c k) -> p s c k", s=4, c=2) for z in (probs, flat_ps))
                    ve.tensor_copy(v[:, :, 0], w[:, :, 0]).then_inc(dve_layer, 1)
                    ve.wait_ge(dve_layer, L.next())
                    ve.tensor_tensor(v[:, :, 1], w[:, :, 1], wide(const("causal"), 1, [4, P]), ALU.add).then_inc(dve_layer, 1)
                    ve.wait_ge(dve_layer, L.next())
                    ve.tensor_reduce(row_max[:, 0:4], probs.rearrange("p (s k) -> p s k", s=4), AX.X, ALU.max).then_inc(dve_layer, 1)
                    ve.wait_ge(dve_layer, L.next())
                    n = 4
                ve.tensor_scalar(row_max[:, 0:n], row_max[:, 0:n], -ATT_SCALE, None, ALU.mult).then_inc(maxed, 1)

            def attention_out(b):
                ve.wait_ge(pv_done, at(pv_done, l, b + 1))
                n = (8, 4, 4)[b]
                ve.reciprocal(row_inv[:, 0:n], row_sum[:, 0:n]).then_inc(dve_layer, 1)
                ve.wait_ge(dve_layer, L.next())
                dst = attn[:, (0, 1, 1)[b], (0, 0, 256)[b]:(512, 256, 512)[b]].rearrange("p (h d) -> p h d", h=n)
                ve.tensor_tensor(dst, ps[:, (0, 2, 0)[b], 0:n * HD].rearrange("p (h d) -> p h d", h=n),
                                 wide(row_inv[:, 0:n], 2, [n, HD]), ALU.mult).then_inc(o_ready, 1)

            def rope_k(t):
                if t == 0:
                    ve.wait_ge(k_raw, at(k_raw, l, 2))
                    ve.wait_ge(rope_ready, at(rope_ready, l, 1))
                    ve.wait_ge(qk_inv, at(qk_inv, l, 2))
                r3 = raw[:, 2 + t].rearrange("p (h d) -> p h d", h=HEADS)
                r4 = raw[:, 2 + t].rearrange("p (h f d) -> p h f d", h=HEADS, f=2)
                t3 = rope_tmp_k[:, 0].rearrange("p (h d) -> p h d", h=HEADS)
                t4 = rope_tmp_k[:, 1].rearrange("p (h f d) -> p h f d", h=HEADS, f=2)
                ve.tensor_tensor(r3, r3, wide(head_ss[:, 2 + t], 2, [HEADS, HD]), ALU.mult).then_inc(dve_layer, 1)
                ve.wait_ge(dve_layer, L.next())
                ve.tensor_tensor(t3, r3, wide(rope[:, 1, 0, t], 1, [HEADS, HD]), ALU.mult).then_inc(dve_layer, 1)
                ve.wait_ge(dve_layer, L.next())
                for f in range(2):
                    ve.tensor_tensor(t4[:, :, f], r4[:, :, 1 - f], wide(rope[:, 1, 1, t, 32 * f:32 * f + 32], 1, [HEADS, 32]), ALU.mult).then_inc(dve_layer, 1)
                    ve.wait_ge(dve_layer, L.next())
                ve.tensor_tensor(raw[:, 2 + t], rope_tmp_k[:, 0], rope_tmp_k[:, 1], ALU.add).then_inc(k_roped, 1)

            scan(0)
            scan(1)
            skip(0)
            head_rms(0)
            scan(2)
            skip(1)
            scan(3)
            skip(2)
            scan(4)
            head_rms(1)
            skip(3)
            rope_k(0)
            scan(5)
            skip(4)
            rope_k(1)
            scan(6)
            skip(5)
            scan(7)
            skip(6)
            softmax_in(0)
            skip(7)
            attention_out(0)
            softmax_in(1)
            attention_out(1)
            softmax_in(2)
            attention_out(2)

            for u in range(4):
                t, half = divmod(u, 2)
                if u < 3:
                    ve.wait_ge(ya_done, at(ya_done, l, u + 1))
                else:
                    ve.wait_ge(w_used, at(w_used, l, 14))
                ve.wait_ge(ga_tanh, at(ga_tanh, l, u + 1))
                ve.scalar_tensor_tensor(mix[:, t, 512 * half:512 * half + 512], att_gate[:, u], 1.0,
                                        ps[:, 5 + 2 * (u % 2)], ALU.add, ALU.mult).then_inc(mix_a, 1)
            S = counted(dve_setup, l + 1)
            for u in range(4):
                t, half = divmod(u, 2)
                m = mix[:, t, 512 * half:512 * half + 512]
                g0, g1 = gates[:, 0, u % 2], gates[:, 1, u % 2]
                ve.wait_ge(gate_tanh, at(gate_tanh, l, 2 * (u + 1)))
                ve.scalar_tensor_tensor(g1, g1, 1.0, ps[:, 4 * (u % 2) + 1], ALU.add, ALU.mult).then_inc(dve_layer, 1)
                ve.wait_ge(dve_layer, L.next())
                ve.scalar_tensor_tensor(g0, g0, 1.0, g1, ALU.add, ALU.mult).then_inc(dve_layer, 1)
                ve.wait_ge(dve_layer, L.next())
                ve.scalar_tensor_tensor(m, g0, 0.25, m, ALU.mult, ALU.add).then_inc(mixed, 1)
                if u == 2:
                    ve.wait_ge(mixT_mm, at(mixT_mm, l, 2))
                    ve.tensor_copy(hT[:, 4:8, 0:P], ps[:, 7].rearrange("p (c s) -> p c s", c=4)).then_inc(mixT_dve, 1)
                if u == 0:
                    take_vectors(l + 1, 3)
                    setup_first(l + 1, S)
                if u == 1:
                    angles(S, 0)
                if u == 2:
                    angles(S, 1)
                if u == 3:
                    setup_second(l + 1, S)
                    S.close()

            def residual(t):
                for half in range(2):
                    c = slice(512 * half, 512 * half + 512)
                    ve.scalar_tensor_tensor(xs[:, t, c], ps[:, 4 * t + half], 0.5, xs[:, t, c], ALU.mult,
                                            ALU.add).then_inc(x_mid, 1)

            def turned_x(t):
                ve.wait_ge(x_turned, at(x_turned, l, 2 * (t + 1)))
                ve.tensor_copy(hT[:, 4:8, t * P:(t + 1) * P], ps[:, 3 + 4 * t].rearrange("p (c s) -> p c s", c=4)).then_inc(x_dve, 1)

            ve.wait_ge(wo_done, at(wo_done, l, 1))
            residual(0)
            ve.wait_ge(mixT_mm, at(mixT_mm, l, 4))
            ve.tensor_copy(hT[:, 4:8, P:2 * P], ps[:, 7].rearrange("p (c s) -> p c s", c=4)).then_inc(mixT_dve, 1)
            turned_x(0)
            ve.wait_ge(w_used, at(w_used, l, FRONT_GROUPS))
            residual(1)
            turned_x(1)
            ve.wait_ge(mid_std, at(mid_std, l, 1))
            ve.reciprocal(rstd, std).then_inc(mid_rstd, 1)
            ve.wait_ge(mid_rstd, at(mid_rstd, l, 1))

            ve.wait_ge(logits_mm, at(logits_mm, l, 1))
            lg = ps[:, 0, 0:72].rearrange("p (t n) -> p t n", t=NT)
            for t in range(NT):
                ve.scalar_tensor_tensor(glog[:, t, 0:EGROUPS], lg[:, t, 0:4], rstd[:, t:t + 1], router_b[:, 0:4], ALU.mult,
                                        ALU.add).then_inc(dve_layer, 1)
                L.add()
            for t in range(NT):
                ve.scalar_tensor_tensor(elog[:, t], lg[:, t, 4:36], rstd[:, t:t + 1], router_b[:, 4:36], ALU.mult,
                                        ALU.add).then_inc(dve_layer, 1)
                L.add()
            ve.wait_ge(dve_layer, L.value())
            ve.sem_inc(settled, 1)
            for t in range(NT):
                ve.max(tops[:, 0, t], glog[:, t]).then_inc(dve_layer, 1)
                L.add()
            ve.wait_ge(dve_layer, L.value())
            ve.sem_inc(settled, 1)
            for t in range(NT):
                ve.max_index(tops_at[:, 0, t], tops[:, 0, t], glog[:, t]).then_inc(dve_layer, 1)
                L.add()
            ve.wait_ge(dve_layer, L.value())
            ve.tensor_scalar(rt[:, 0], tops[:, 0, :, 0], -1.0, None, ALU.mult).then_inc(group_max, 1)
            ve.tensor_copy(ids[:, 0], tops_at[:, 0, :, 0]).then_inc(dve_layer, 1)
            ve.wait_ge(dve_layer, L.next())
            for t in range(NT):
                ve.tensor_scalar(emask[:, t], const("egroup"), ids[:, 0, t:t + 1], None, ALU.is_equal).then_inc(dve_layer, 1)
                L.add()
            ve.wait_ge(dve_layer, L.value())
            ve.tensor_scalar(assign, emask, 1.0, BIG, ALU.subtract, ALU.mult).then_inc(dve_layer, 1)
            ve.wait_ge(dve_layer, L.next())
            ve.tensor_tensor(elog, elog, emask, ALU.mult).then_inc(dve_layer, 1)
            ve.wait_ge(dve_layer, L.next())
            ve.tensor_tensor(elog, elog, assign, ALU.add).then_inc(dve_layer, 1)
            ve.wait_ge(dve_layer, L.next())
            ve.sem_inc(settled, 1)
            for t in range(NT):
                ve.max(tops[:, 1, t], elog[:, t]).then_inc(dve_layer, 1)
                L.add()
            ve.wait_ge(dve_layer, L.value())
            ve.sem_inc(settled, 1)
            for t in range(NT):
                ve.max_index(tops_at[:, 1, t], tops[:, 1, t], elog[:, t]).then_inc(dve_layer, 1)
                L.add()
            ve.wait_ge(dve_layer, L.value())
            ve.tensor_tensor(rt[:, 1], tops[:, 1, :, 1], tops[:, 1, :, 0], ALU.subtract).then_inc(top_diff, 1)
            for a in range(2):
                ve.tensor_copy(ids[:, 1 + a], tops_at[:, 1, :, a]).then_inc(dve_layer, 1)
                L.add()
            ve.wait_ge(dve_layer, L.value())
            for a in range(2):
                for t in range(NT):
                    ve.tensor_scalar(onehot[:, a, t], const("expert"), ids[:, 1 + a, t:t + 1], None, ALU.is_equal).then_inc(dve_layer, 1)
                    L.add()
            ve.wait_ge(dve_layer, L.value())
            ve.tensor_tensor(assign, onehot[:, 0], onehot[:, 1], ALU.add).then_inc(assigned, 1)
            ve.wait_ge(assigned, at(assigned, l, 1))
            def build_pick(S, i, b):
                ve.tensor_tensor(match, const("slot").unsqueeze(1).unsqueeze(1).to_broadcast([P, NT, 2, SLOTS]),
                                 wide(slot_of[:, :, bass.ds(b * 2, 2)], 3, [NT, 2, SLOTS]), ALU.is_equal).then_inc(S["match"], 1)
                ve.wait_ge(S["match"], at(S["match"], l, i + 1))
                if not isinstance(i, int):
                    ve.wait_ge(S["gathered"], at(S["gathered"], l, i))
                ve.tensor_tensor(pick, match.rearrange("p t e s -> p t (e s)"), wide(rstd, 2, [NT, P]),
                                 ALU.mult).then_inc(S["pick"], 1)

            def leave_gather(S, i):
                ve.wait_ge(S["gathered"], at(S["gathered"], l, i + 1))
                ve.tensor_tensor(xT, ps[:, 2:4].rearrange("p b (k s) -> p (b k) s", k=4), wide(gain2, 2, [KC, P]),
                                 ALU.mult).then_inc(S["xT"], 1)

            def pair(S, i, b, down_done):
                ve.tensor_tensor(back.rearrange("p t (e s) -> p t e s", e=2), match,
                                 wide(weight_of[:, :, bass.ds(b * 2, 2)], 3, [NT, 2, SLOTS]), ALU.mult).then_inc(S["back"], 1)
                ve.wait_ge(S["back"], at(S["back"], l, i + 1))
                build_pick(S, i + 1, b + 1)
                ve.wait_ge(S["tanh"], at(S["tanh"], l, i + 1))
                ve.scalar_tensor_tensor(act_buf, act_buf, 1.0, ps[:, 0], ALU.add, ALU.mult).then_inc(S["silu"], 1)
                ve.wait_ge(S["silu"], at(S["silu"], l, i + 1))
                ve.tensor_tensor(act_buf, act_buf, ps[:, 1], ALU.mult).then_inc(S["h"], 1)
                leave_gather(S, i + 1)
                ve.wait_ge(S["backT_mm"], at(S["backT_mm"], l, i + 1))
                ve.tensor_copy(backT.rearrange("p t s -> p (t s)"), ps[:, 1, 0:NT * P]).then_inc(S["backT"], 1)
                down_done()
                ve.tensor_copy(ybuf[:, 1], ps[:, 3]).then_inc(S["y1"], 1)

            ve.wait_ge(pos_mm, at(pos_mm, l, 1))
            ve.scalar_tensor_tensor(slot_of[:, :, 0:EXPERTS], ps[:, 1, 0:64].rearrange("p (t n) -> p t n", t=NT), 1.0,
                                    assign, ALU.add, ALU.mult).then_inc(dve_layer, 1)
            ve.wait_ge(dve_layer, L.next())
            ve.tensor_scalar(slot_of[:, :, 0:EXPERTS], slot_of[:, :, 0:EXPERTS], 1.0, None, ALU.subtract).then_inc(dve_layer, 1)
            ve.wait_ge(dve_layer, L.next())
            build_pick(main, 0, 0)
            ve.wait_ge(group_exp, at(group_exp, l, 2))
            ve.reciprocal(rt[:, 3], rt[:, 2]).then_inc(dve_layer, 1)
            ve.wait_ge(dve_layer, L.next())
            ve.wait_ge(top_exp, at(top_exp, l, 1))
            ve.tensor_scalar(rt[:, 5], rt[:, 4], 1.0, None, ALU.add).then_inc(dve_layer, 1)
            ve.wait_ge(dve_layer, L.next())
            ve.reciprocal(rt[:, 5], rt[:, 5]).then_inc(dve_layer, 1)
            ve.wait_ge(dve_layer, L.next())
            ve.scalar_tensor_tensor(rt[:, 6], rt[:, 3], 0.5, rt[:, 5], ALU.mult, ALU.mult).then_inc(dve_layer, 1)
            ve.wait_ge(dve_layer, L.next())
            ve.tensor_tensor(rt[:, 7], rt[:, 6], rt[:, 4], ALU.mult).then_inc(dve_layer, 1)
            ve.wait_ge(dve_layer, L.next())
            for a in range(2):
                for t in range(NT):
                    ve.tensor_scalar(onehot[:, a, t], onehot[:, a, t], rt[:, 6 + a, t:t + 1], None, ALU.mult).then_inc(dve_layer, 1)
                    ve.wait_ge(dve_layer, L.next())
            ve.tensor_tensor(weight_of[:, :, 0:EXPERTS], onehot[:, 0], onehot[:, 1], ALU.add).then_inc(dve_layer, 1)
            ve.wait_ge(dve_layer, L.next())
            ve.tensor_copy(count, ps[:, 1, 64:96]).then_inc(dve_layer, 1)
            ve.wait_ge(dve_layer, L.next())
            ve.tensor_reduce(rt[:, 0, 0:1], count, AX.X, ALU.max).then_inc(dve_layer, 1)
            ve.wait_ge(dve_layer, L.next())
            ve.tensor_copy(ov_flag, rt[:, 0, 0:1]).then_inc(routed, 1)

            leave_gather(main, 0)
            with ve.Fori(0, PAIRS) as p:
                pair(main, p, p, lambda: ve.wait_ge(w_used, at(w_used, l, FRONT_GROUPS + p * RING + 12)))

            most = ve.value_load(ov_flag[0:1, 0:1], min_val=0, max_val=SEQ)
            with ve.If(most > SLOTS):
                Q = counted(dve_list, l)

                def by_round(z):
                    return z.rearrange("p (r e) -> p r e", r=EXTRA)

                ve.tensor_tensor(by_round(ov_on), wide(count, 1, [EXTRA, EXPERTS]), by_round(const("ov_limit")), ALU.is_gt).then_inc(dve_list, 1)
                ve.wait_ge(dve_list, Q.next())
                ve.tensor_tensor_scan(ov_cum, const("ones")[:, 0:NJ], ov_on, 0.0, ALU.mult, ALU.add).then_inc(dve_list, 1)
                ve.wait_ge(dve_list, Q.next())
                ve.tensor_tensor(ov_sel, wide(ov_cum, 1, [OV_BLOCKS, NJ]), wide(const("ov_block"), 2, [OV_BLOCKS, NJ]), ALU.is_equal).then_inc(dve_list, 1)
                ve.wait_ge(dve_list, Q.next())
                ve.tensor_tensor(ov_sel, ov_sel, wide(ov_on, 1, [OV_BLOCKS, NJ]), ALU.mult).then_inc(dve_list, 1)
                ve.wait_ge(dve_list, Q.next())
                ve.tensor_tensor(ov_tmp, ov_sel, wide(const("ov_expert"), 1, [OV_BLOCKS, NJ]), ALU.mult).then_inc(dve_list, 1)
                ve.wait_ge(dve_list, Q.next())
                ve.tensor_reduce(row_inv, ov_tmp, AX.X, ALU.add).then_inc(dve_list, 1)
                ve.wait_ge(dve_list, Q.next())
                ve.tensor_copy(ov_ids, row_inv).then_inc(ov_listed, 1)
                for t in range(NT):
                    ve.tensor_tensor(by_round(ov_v), wide(slot_of[:, t, 0:EXPERTS], 1, [EXTRA, EXPERTS]),
                                     by_round(const("ov_shift")), ALU.add).then_inc(dve_list, 1)
                    ve.wait_ge(dve_list, Q.next())
                    ve.tensor_tensor(ov_tmp, ov_sel, wide(ov_v, 1, [OV_BLOCKS, NJ]), ALU.mult).then_inc(dve_list, 1)
                    ve.wait_ge(dve_list, Q.next())
                    ve.tensor_reduce(slot_of[:, t, EXPERTS:EXPERTS + OV_BLOCKS], ov_tmp, AX.X, ALU.add).then_inc(dve_list, 1)
                    ve.wait_ge(dve_list, Q.next())
                    for r in range(EXTRA):
                        e = slice(r * EXPERTS, (r + 1) * EXPERTS)
                        ve.tensor_tensor(ov_tmp[:, :, e], ov_sel[:, :, e], wide(weight_of[:, t, 0:EXPERTS], 1, [OV_BLOCKS, EXPERTS]), ALU.mult).then_inc(dve_list, 1)
                        ve.wait_ge(dve_list, Q.next())
                    ve.tensor_reduce(weight_of[:, t, EXPERTS:EXPERTS + OV_BLOCKS], ov_tmp, AX.X, ALU.add).then_inc(dve_list, 1)
                    ve.wait_ge(dve_list, Q.next())
                ve.tensor_scalar(slot_of[:, :, EXPERTS:EXPERTS + OV_BLOCKS], slot_of[:, :, EXPERTS:EXPERTS + OV_BLOCKS],
                                 1.0, None, ALU.subtract).then_inc(dve_list, 1)
                ve.wait_ge(dve_list, Q.next())
                Q.close()
                ve.wait_ge(main["gathered"], at(main["gathered"], l, PAIRS + 1))
                build_pick(over, 0, PAIRS)
                leave_gather(over, 0)
                with ve.Fori(0, OV_PAIRS) as i:
                    pair(over, i, i + PAIRS, lambda: ve.wait_ge(ov_used, at(ov_used, l, i * RING + 12)))
            with ve.Else():
                for s in [dve_list, ov_listed] + [over[n] for n in ("match", "pick", "xT", "back", "silu", "h", "backT", "y1")]:
                    ve.sem_inc(s, per[s.name])
            ve.nop()
            ve.wait_ge(main["scattered"], at(main["scattered"], l, PAIRS))
            ve.wait_ge(over["scattered"], at(over["scattered"], l, OV_PAIRS))
            for t in range(NT):
                for half in range(2):
                    c = slice(512 * half, 512 * half + 512)
                    ve.tensor_tensor(xs[:, t, c], ps[:, 4 + 2 * t + half], xs[:, t, c], ALU.add).then_inc(x_new, 1)
            L.close()
            with ve.If(l < DEPTH - 1):
                ve.wait_ge(x_new, at(x_new, l, 4))
                norm_squares(l + 1)
                norm_scale(l + 1)
                norm_turned(l + 1, turned("norm1"))
            ve.nop()

    @block.gpsimd
    def _(pool):
        def setup(n):
            pool.wait_ge(setup_in, at(setup_in, n, per[setup_in.name]))
            S = counted(pool_setup, n)
            for r in range(2):
                pool.tensor_tensor(c_exp[:, r], wide(c_raw[:, r], 2, [QUADS, 2, NSTATE]),
                                   const("gside").unsqueeze(1).unsqueeze(3).to_broadcast([P, QUADS, 2, NSTATE]),
                                   ALU.mult).then_inc(expanded, 1)
            pool.wait_ge(f_ready, at(f_ready, n, 1))
            for v, (f, r) in enumerate(((f_re, 0), (f_im, 1), (f_re, 1), (f_im, 0))):
                pool.tensor_tensor(b_tmp[:, v], b_raw[:, r], wide(f, 2, [TILES, GCH]), ALU.mult).then_inc(pool_setup, 1)
                pool.wait_ge(pool_setup, S.next())
            pool.tensor_tensor(b_tmp[:, 0], b_tmp[:, 0], b_tmp[:, 1], ALU.subtract).then_inc(pool_setup, 1)
            pool.wait_ge(pool_setup, S.next())
            pool.tensor_tensor(b_tmp[:, 2], b_tmp[:, 2], b_tmp[:, 3], ALU.add).then_inc(pool_setup, 1)
            pool.wait_ge(pool_setup, S.next())
            for r in range(2):
                pool.tensor_tensor(b_exp[:, r], wide(b_tmp[:, 2 * r], 2, [TILES, 2, GCH]),
                                   const("side").unsqueeze(1).unsqueeze(3).to_broadcast([P, TILES, 2, GCH]),
                                   ALU.mult).then_inc(expanded, 1)
            S.close()

        pool.wait_ge(const_in, 16)
        setup(0)
        with pool.Fori(0, DEPTH) as l:
            L = counted(pool_layer, l)
            pool.wait_ge(layer_in, at(layer_in, l, per[layer_in.name]))
            ra, rb = (const(n).rearrange("p (t d) -> p t d", t=NT) for n in ("rope_a", "rope_b"))
            pool.wait_ge(vec_ready, at(vec_ready, l, 1))
            pool.tensor_tensor(router_w, router_w, wide(turned("norm2"), 2, [KC, 36]), ALU.mult).then_inc(router_ready, 1)
            pool.wait_ge(router_ready, at(router_ready, l, 1))
            for w in range(2):
                pool.tensor_tensor(rope[:, w, 0], ra, wide(qk_gain[:, w], 1, [NT, HD]), ALU.mult).then_inc(pool_layer, 1)
                pool.wait_ge(pool_layer, L.next())
                for f in range(2):
                    ins = pool.tensor_tensor(rope[:, w, 1, :, 32 * f:32 * f + 32], rb[:, :, 32 * f:32 * f + 32],
                                             wide(qk_gain[:, w, 32 - 32 * f:64 - 32 * f], 1, [NT, 32]), ALU.mult)
                    if w and f:
                        ins.then_inc(rope_ready, 1)
                    else:
                        ins.then_inc(pool_layer, 1)
                        pool.wait_ge(pool_layer, L.next())
            pool.wait_ge(rope_ready, at(rope_ready, l, 1))

            def rotate(k):
                half, q = divmod(k, 4)
                tiles = slice(4 * q, 4 * q + 4)
                pool.wait_ge(scanned, at(scanned, l, k + 1))
                if k > 0:
                    pool.wait_ge(y_done, at(y_done, l, k))
                for v, (table, r) in enumerate(((cosT, 0), (sinT, 1), (sinT, 0), (cosT, 1))):
                    pool.tensor_tensor(post[:, v], wst[:, r], table[:, tiles, 0:HALF], ALU.mult).then_inc(rotated, 1)
                if half == 0:
                    last = [wst[:, r, :, HALF - 1] for r in range(2)]
                    cs, sn = cosT[:, tiles, HALF], sinT[:, tiles, HALF]
                    c = [carry[:, n, tiles] for n in range(4)]
                    pool.tensor_tensor(c[0], last[0], cs, ALU.mult).then_inc(pool_layer, 1)
                    pool.wait_ge(pool_layer, L.next())
                    pool.tensor_tensor(c[2], last[1], sn, ALU.mult).then_inc(pool_layer, 1)
                    pool.wait_ge(pool_layer, L.next())
                    pool.tensor_tensor(c[1], last[1], cs, ALU.mult).then_inc(pool_layer, 1)
                    pool.wait_ge(pool_layer, L.next())
                    pool.tensor_tensor(c[3], last[0], sn, ALU.mult).then_inc(pool_layer, 1)
                    pool.wait_ge(pool_layer, L.next())
                    pool.tensor_tensor(c[0], c[0], c[2], ALU.subtract).then_inc(pool_layer, 1)
                    pool.wait_ge(pool_layer, L.next())
                    pool.tensor_tensor(c[1], c[1], c[3], ALU.add).then_inc(carried, 1)

            def gelu(k):
                half, q = divmod(k, 4)
                pool.wait_ge(y_ready, at(y_ready, l, k + 1))
                pool.tensor_tensor(y2, y1, y1, ALU.mult).then_inc(pool_layer, 1)
                pool.wait_ge(pool_layer, L.next())
                pool.sem_inc(settled, 1)
                pool.tensor_scalar(y2, y2, 0.044715, 1.0, ALU.mult, ALU.add).then_inc(pool_layer, 1)
                pool.wait_ge(pool_layer, L.next())
                pool.tensor_tensor(y3, y2, y1, ALU.mult).then_inc(gelu_in, 1)
                pool.wait_ge(gelu_tanh, at(gelu_tanh, l, k + 1))
                pool.sem_inc(settled, 1)
                pool.tensor_scalar(y2, y2, 1.0, 1.0, ALU.mult, ALU.add).then_inc(pool_layer, 1)
                pool.wait_ge(pool_layer, L.next())
                pool.tensor_tensor(uT[:, q, half * HALF:(half + 1) * HALF], y2, y1, ALU.mult).then_inc(z_ready, 1)

            def rope_q(t):
                if t == 0:
                    pool.wait_ge(q_raw, at(q_raw, l, 2))
                    pool.wait_ge(qk_inv, at(qk_inv, l, 1))
                r3 = raw[:, t].rearrange("p (h d) -> p h d", h=HEADS)
                r4 = raw[:, t].rearrange("p (h f d) -> p h f d", h=HEADS, f=2)
                t3 = rope_tmp[:, 0].rearrange("p (h d) -> p h d", h=HEADS)
                t4 = rope_tmp[:, 1].rearrange("p (h f d) -> p h f d", h=HEADS, f=2)
                pool.tensor_tensor(r3, r3, wide(head_ss[:, t], 2, [HEADS, HD]), ALU.mult).then_inc(pool_layer, 1)
                pool.wait_ge(pool_layer, L.next())
                pool.tensor_tensor(t3, r3, wide(rope[:, 0, 0, t], 1, [HEADS, HD]), ALU.mult).then_inc(pool_layer, 1)
                pool.wait_ge(pool_layer, L.next())
                for f in range(2):
                    pool.tensor_tensor(t4[:, :, f], r4[:, :, 1 - f], wide(rope[:, 0, 1, t, 32 * f:32 * f + 32], 1, [HEADS, 32]), ALU.mult).then_inc(pool_layer, 1)
                    pool.wait_ge(pool_layer, L.next())
                pool.tensor_tensor(raw[:, t], rope_tmp[:, 0], rope_tmp[:, 1], ALU.add).then_inc(q_roped, 1)
                pool.wait_ge(q_roped, at(q_roped, l, t + 1))

            rotate(0)
            for k in range(1, 8):
                rotate(k)
                gelu(k - 1)
                if k in (2, 4):
                    rope_q(k // 2 - 1)
            gelu(7)
            L.close()
            pool.wait_ge(mixed, at(mixed, l, 4))
            setup(l + 1)

    ctx.close()


_INS = ["x", "norm1_g", "w_in", "ssm_a_re", "ssm_a_im", "ssm_log_dt", "ssm_b_re", "ssm_b_im", "ssm_c_re", "ssm_c_im",
        "ssm_d", "w_glu", "q_norm_g", "k_norm_g", "w_attn", "w_out", "norm2_g", "router_w_group", "router_b_group",
        "router_w_expert", "router_b_expert", "w_gate_up", "w_down"]


def kernel(**inputs):
    import numpy as _np
    import concourse.bacc as _bacc
    from concourse import mybir as _mybir
    from concourse.bass_utils import run_bass_kernel_spmd as _run

    nc = _bacc.Bacc("TRN2", target_bir_lowering=False, num_devices=1)
    arrays, args = {}, []
    for name in _INS:
        a = _np.ascontiguousarray(inputs[name])
        arrays[f"in_{name}_dram"] = a
        args.append(nc.dram_tensor(f"in_{name}_dram", a.shape, _mybir.dt.from_np(a.dtype), kind="ExternalInput").ap())
    c = constants()
    arrays["shape_constants"] = c
    args.append(nc.dram_tensor("shape_constants", c.shape, _mybir.dt.float32, kind="ExternalInput").ap())
    args.append(nc.dram_tensor("out_dram", (1, SEQ, D), _mybir.dt.float32, kind="ExternalOutput").ap())
    trunk(nc, *args)
    r = _run(nc, [arrays], core_ids=[0])
    return r.results[0]["out_dram"]
```
